# Optimizing a Trainium2 kernel written in Bass

```python
import jax, jax.numpy as jnp
from jax import lax
import numpy as np
import math

D_MODEL = 1024
BATCH = 1
SEQ = 512
DEPTH = 1

N_ATTN_HEADS = 8
HEAD_DIM = 64
ATTN_WIDTH = N_ATTN_HEADS * HEAD_DIM
DILATED_PATTERNS = ((128, 1), (512, 4), (2048, 16))
SPAN = 128
MAX_DILATION = 16
PAD_MULT = MAX_DILATION * SPAN
LRU_WIDTH = D_MODEL // 2
N_LRU_BLOCKS = 8
LRU_BLOCK = LRU_WIDTH // N_LRU_BLOCKS
CONV_WIDTH = 4
LRU_C = 8.0
MIX_WIDTH = ATTN_WIDTH + LRU_WIDTH
IN_WIDTH = 3 * ATTN_WIDTH + 2 * LRU_WIDTH
D_FF = 4 * D_MODEL
NORM_EPS = 1e-6


def rms_norm(x, g):
    xf = x.astype(jnp.float32)
    y = xf * lax.rsqrt(jnp.mean(xf * xf, axis=-1, keepdims=True) + NORM_EPS)
    return (y * g.astype(jnp.float32)).astype(x.dtype)

def dilated_branch(q, k, v, window, dilation):
    b, sp, h, dh = q.shape
    span = window // dilation
    nb = sp // (dilation * span)

    def split(t):
        return t.reshape(b, nb, span, dilation, h, dh).transpose(0, 3, 4, 1, 2, 5)

    def with_prev(t):
        prev = jnp.pad(t, ((0, 0), (0, 0), (0, 0), (1, 0), (0, 0), (0, 0)))[:, :, :, :-1]
        return jnp.concatenate([prev, t], axis=4)

    qb = split(q)
    kb = with_prev(split(k))
    vb = with_prev(split(v))
    s = jnp.einsum('bchnqd,bchnkd->bchnqk', qb, kb,
                   preferred_element_type=jnp.float32) * (HEAD_DIM ** -0.5)
    qi = jnp.arange(span)[:, None]
    kj = jnp.arange(2 * span)[None, :]
    dist = span + qi - kj
    blk = jnp.arange(nb)[:, None, None]
    valid = (dist >= 0) & (dist <= span) & ((blk > 0) | (kj >= span))
    s = jnp.where(valid, s, -jnp.inf)
    mx = jnp.max(s, axis=-1, keepdims=True)
    p = jnp.exp(s - mx)
    den = jnp.sum(p, axis=-1)
    o = jnp.einsum('bchnqk,bchnkd->bchnqd', p, vb.astype(jnp.float32)) / den[..., None]
    lse = mx[..., 0] + jnp.log(den)
    o = o.transpose(0, 3, 4, 1, 2, 5).reshape(b, sp, h, dh)
    lse = lse.transpose(0, 3, 4, 1, 2).reshape(b, sp, h)
    return o, lse

def dilated_attention(q, k, v):
    b, s, h, dh = q.shape
    sp = -(-s // PAD_MULT) * PAD_MULT
    pad = ((0, 0), (0, sp - s), (0, 0), (0, 0))
    qp, kp, vp = jnp.pad(q, pad), jnp.pad(k, pad), jnp.pad(v, pad)
    outs, lses = [], []
    for window, dilation in DILATED_PATTERNS:
        o, l = dilated_branch(qp, kp, vp, window, dilation)
        outs.append(o)
        lses.append(l)
    wts = jax.nn.softmax(jnp.stack(lses, axis=0), axis=0)
    o = jnp.einsum('pbsh,pbshd->bshd', wts, jnp.stack(outs, axis=0))
    return o[:, :s].astype(q.dtype)

def causal_depthwise_conv(x, w, bias):
    c = x.shape[-1]
    y = lax.conv_general_dilated(x, w[:, None, :].astype(x.dtype), window_strides=(1,),
                                 padding=[(CONV_WIDTH - 1, 0)],
                                 dimension_numbers=('NWC', 'WIO', 'NWC'),
                                 feature_group_count=c)
    return y + bias.astype(x.dtype)

def rg_lru(x, w_r, b_r, w_i, b_i, lam):
    b, s, c = x.shape
    xf = x.astype(jnp.float32)
    xb = xf.reshape(b, s, N_LRU_BLOCKS, LRU_BLOCK)
    r = jax.nn.sigmoid(jnp.einsum('bsnc,ncd->bsnd', xb, w_r.astype(jnp.float32)).reshape(b, s, c)
                       + b_r.astype(jnp.float32))
    i = jax.nn.sigmoid(jnp.einsum('bsnc,ncd->bsnd', xb, w_i.astype(jnp.float32)).reshape(b, s, c)
                       + b_i.astype(jnp.float32))
    log_a = -LRU_C * r * jax.nn.softplus(-lam.astype(jnp.float32))
    a = jnp.exp(log_a)
    u = jnp.sqrt(-jnp.expm1(2.0 * log_a)) * (i * xf)

    def combine(left, right):
        a_l, h_l = left
        a_r, h_r = right
        return a_l * a_r, a_r * h_l + h_r

    _, h = lax.associative_scan(combine, (a, u), axis=1)
    return h.astype(x.dtype)

def hybrid_mixer(h, w_in, conv_w, conv_b, w_r, b_r, w_i, b_i, lam, w_out):
    b, s, _ = h.shape
    z = h @ w_in
    q, k, v, xr, gr = jnp.split(
        z, [ATTN_WIDTH, 2 * ATTN_WIDTH, 3 * ATTN_WIDTH, 3 * ATTN_WIDTH + LRU_WIDTH], axis=-1)
    shp = (b, s, N_ATTN_HEADS, HEAD_DIM)
    attn = dilated_attention(q.reshape(shp), k.reshape(shp), v.reshape(shp)).reshape(b, s, ATTN_WIDTH)
    xr = causal_depthwise_conv(xr, conv_w, conv_b)
    rec = rg_lru(xr, w_r, b_r, w_i, b_i, lam) * jax.nn.gelu(gr)
    return jnp.concatenate([attn.astype(h.dtype), rec.astype(h.dtype)], axis=-1) @ w_out

def squared_relu_mlp(h, w1, w2):
    a = jax.nn.relu(h @ w1)
    return (a * a) @ w2

def first_inputs(seed: int = 0) -> dict:
    key = jax.random.key(seed)
    ks = jax.random.split(key, 20)
    f32 = jnp.float32

    def gain(k):
        return 1.0 + 0.05 * jax.random.normal(k, (DEPTH, D_MODEL), f32)

    u = jax.random.uniform(ks[10], (DEPTH, LRU_WIDTH), f32, 0.9, 0.999)
    a0 = u ** (1.0 / LRU_C)
    lru_lambda = jnp.log(a0) - jnp.log1p(-a0)
    return {
        "x": jax.random.normal(ks[0], (BATCH, SEQ, D_MODEL), f32),
        "mix_norm_pre": gain(ks[1]),
        "mix_norm_post": gain(ks[2]),
        "mlp_norm_pre": gain(ks[3]),
        "mlp_norm_post": gain(ks[4]),
        "w_in": jax.random.normal(ks[5], (DEPTH, D_MODEL, IN_WIDTH), f32) * D_MODEL ** -0.5,
        "conv_w": jax.random.normal(ks[6], (DEPTH, CONV_WIDTH, LRU_WIDTH), f32) * CONV_WIDTH ** -0.5,
        "conv_b": 0.01 * jax.random.normal(ks[7], (DEPTH, LRU_WIDTH), f32),
        "w_rgate": jax.random.normal(ks[8], (DEPTH, N_LRU_BLOCKS, LRU_BLOCK, LRU_BLOCK), f32) * LRU_BLOCK ** -0.5,
        "b_rgate": 0.01 * jax.random.normal(ks[9], (DEPTH, LRU_WIDTH), f32),
        "w_igate": jax.random.normal(ks[11], (DEPTH, N_LRU_BLOCKS, LRU_BLOCK, LRU_BLOCK), f32) * LRU_BLOCK ** -0.5,
        "b_igate": 0.01 * jax.random.normal(ks[12], (DEPTH, LRU_WIDTH), f32),
        "lru_lambda": lru_lambda,
        "w_out": jax.random.normal(ks[13], (DEPTH, MIX_WIDTH, D_MODEL), f32) * MIX_WIDTH ** -0.5,
        "w_ff_in": jax.random.normal(ks[14], (DEPTH, D_MODEL, D_FF), f32) * D_MODEL ** -0.5,
        "w_ff_out": jax.random.normal(ks[15], (DEPTH, D_FF, D_MODEL), f32) * D_FF ** -0.5,
    }

def first_block(x, mix_norm_pre, mix_norm_post, mlp_norm_pre, mlp_norm_post, w_in, conv_w, conv_b,
              w_rgate, b_rgate, w_igate, b_igate, lru_lambda, w_out, w_ff_in, w_ff_out):
    for l in range(DEPTH):
        h = rms_norm(x, mix_norm_pre[l])
        m = hybrid_mixer(h, w_in[l], conv_w[l], conv_b[l], w_rgate[l], b_rgate[l],
                         w_igate[l], b_igate[l], lru_lambda[l], w_out[l])
        x = x + rms_norm(m, mix_norm_post[l])
        h = rms_norm(x, mlp_norm_pre[l])
        x = x + rms_norm(squared_relu_mlp(h, w_ff_in[l], w_ff_out[l]), mlp_norm_post[l])
    return x


D_MIX = D_MODEL
GLA_WIDTH = D_MIX // 2
S5_WIDTH = D_MIX - GLA_WIDTH
GLA_HEADS = 4
GLA_DV = GLA_WIDTH // GLA_HEADS
GLA_DK = GLA_DV // 2
GLA_LOWRANK = 16
GLA_TAU = 16.0
GLA_CHUNK = 64
S5_CH = 16
S5_GROUPS = S5_WIDTH // S5_CH
S5_STATE = 64
DT_MIN = 1e-3
DT_MAX = 1e-1
N_EXPERTS = 32
TOP_K = 4
D_FF_2 = D_MODEL
SWIGLU_ALPHA = 1.702
SWIGLU_LIMIT = 7.0
MOE_BLOCK = 128
EPS = 1e-6
Q_COLS = GLA_HEADS * GLA_DK
K_COLS = GLA_HEADS * GLA_DK
V_COLS = GLA_WIDTH
G_COLS = GLA_WIDTH
A_COLS = GLA_LOWRANK
U_COLS = S5_WIDTH
N_IN = Q_COLS + K_COLS + V_COLS + G_COLS + A_COLS + U_COLS
SPLITS = [Q_COLS, Q_COLS + K_COLS, Q_COLS + K_COLS + V_COLS, Q_COLS + K_COLS + V_COLS + G_COLS,
          Q_COLS + K_COLS + V_COLS + G_COLS + A_COLS]


def rmsnorm(x, g):
    xf = x.astype(jnp.float32)
    r = lax.rsqrt(jnp.mean(xf * xf, axis=-1, keepdims=True) + EPS)
    return (xf * r * g.astype(jnp.float32)).astype(x.dtype)

def gla_chunked(q, k, v, log_a):
    f32 = jnp.float32
    B_, H_, T_, DK_ = q.shape
    DV_ = v.shape[-1]
    C = GLA_CHUNK
    nc = T_ // C
    q = q.astype(f32).reshape(B_, H_, nc, C, DK_) * (DK_ ** -0.5)
    k = k.astype(f32).reshape(B_, H_, nc, C, DK_)
    v = v.astype(f32).reshape(B_, H_, nc, C, DV_)
    b = jnp.cumsum(log_a.astype(f32).reshape(B_, H_, nc, C, DK_), axis=3)
    b_last = b[:, :, :, -1:, :]
    q_dec = q * jnp.exp(b)
    k_inv = k * jnp.exp(-b)
    k_to_end = k * jnp.exp(b_last - b)
    causal = jnp.tril(jnp.ones((C, C), dtype=bool))
    scores = jnp.where(causal, jnp.einsum('bhnik,bhnjk->bhnij', q_dec, k_inv), 0.0)
    o_intra = jnp.einsum('bhnij,bhnjv->bhniv', scores, v)
    delta = jnp.einsum('bhnjk,bhnjv->bhnkv', k_to_end, v)
    decay = jnp.exp(b_last[:, :, :, 0, :])

    def step(S, inp):
        d, dS = inp
        return d[..., None] * S + dS, S

    S0 = jnp.zeros((B_, H_, DK_, DV_), f32)
    _, S_prev = lax.scan(step, S0, (jnp.moveaxis(decay, 2, 0), jnp.moveaxis(delta, 2, 0)))
    S_prev = jnp.moveaxis(S_prev, 0, 2)
    o_inter = jnp.einsum('bhnik,bhnkv->bhniv', q_dec, S_prev)
    return (o_intra + o_inter).reshape(B_, H_, T_, DV_)

def s5_layer(u, lam_re, lam_im, log_dt, b_re, b_im, c_re, c_im, d, glu_w, glu_b):
    f32 = jnp.float32
    B_, T_, _ = u.shape
    uf = u.astype(f32).reshape(B_, T_, S5_GROUPS, S5_CH)
    lr = lam_re.astype(f32)
    li = lam_im.astype(f32)
    dt = jnp.exp(log_dt.astype(f32))[:, None]
    mag = jnp.exp(lr * dt)
    ab_re = mag * jnp.cos(li * dt)
    ab_im = mag * jnp.sin(li * dt)
    den = lr * lr + li * li
    f_re = ((ab_re - 1.0) * lr + ab_im * li) / den
    f_im = (ab_im * lr - (ab_re - 1.0) * li) / den
    br = b_re.astype(f32)
    bi = b_im.astype(f32)
    bb_re = f_re[..., None] * br - f_im[..., None] * bi
    bb_im = f_re[..., None] * bi + f_im[..., None] * br
    bu_re = jnp.einsum('btgh,gph->btgp', uf, bb_re)
    bu_im = jnp.einsum('btgh,gph->btgp', uf, bb_im)
    a_re = jnp.broadcast_to(ab_re, (1, T_, S5_GROUPS, S5_STATE))
    a_im = jnp.broadcast_to(ab_im, (1, T_, S5_GROUPS, S5_STATE))

    def combine(e1, e2):
        a1r, a1i, b1r, b1i = e1
        a2r, a2i, b2r, b2i = e2
        return (a2r * a1r - a2i * a1i,
                a2r * a1i + a2i * a1r,
                a2r * b1r - a2i * b1i + b2r,
                a2r * b1i + a2i * b1r + b2i)

    _, _, xr, xi = lax.associative_scan(combine, (a_re, a_im, bu_re, bu_im), axis=1)
    y = (jnp.einsum('btgp,ghp->btgh', xr, c_re.astype(f32))
         - jnp.einsum('btgp,ghp->btgh', xi, c_im.astype(f32))
         + d.astype(f32) * uf)
    y = jax.nn.gelu(y.reshape(B_, T_, S5_WIDTH))
    return y * jax.nn.sigmoid(y @ glu_w.astype(f32) + glu_b.astype(f32))

def moe_ffn(h, router_w, router_b, w_gu, b_gu, w_down, b_down):
    f32 = jnp.float32
    B_, T_, D_ = h.shape
    N = B_ * T_
    NK = N * TOP_K
    xt = h.reshape(N, D_)
    logits = (xt @ router_w + router_b).astype(f32)
    top_val, top_idx = lax.top_k(logits, TOP_K)
    gate = jax.nn.softmax(top_val, axis=-1)
    flat_e = top_idx.reshape(NK).astype(jnp.int32)
    flat_tok = jnp.arange(NK, dtype=jnp.int32) // TOP_K
    flat_w = gate.reshape(NK)
    order = jnp.argsort(flat_e)
    se, stok, sw = flat_e[order], flat_tok[order], flat_w[order]
    counts = jnp.zeros((N_EXPERTS,), jnp.int32).at[flat_e].add(1)
    starts = jnp.cumsum(counts) - counts
    padded = (counts + MOE_BLOCK - 1) // MOE_BLOCK * MOE_BLOCK
    pends = jnp.cumsum(padded)
    pstarts = pends - padded
    dest = pstarts[se] + jnp.arange(NK, dtype=jnp.int32) - starts[se]
    n_blocks = -(-NK // MOE_BLOCK) + N_EXPERTS
    cap = n_blocks * MOE_BLOCK
    tok_buf = jnp.full((cap,), N, jnp.int32).at[dest].set(stok)
    w_buf = jnp.zeros((cap,), f32).at[dest].set(sw)
    block_e = jnp.minimum(
        jnp.searchsorted(pends, jnp.arange(n_blocks, dtype=jnp.int32) * MOE_BLOCK, side='right'),
        N_EXPERTS - 1).astype(jnp.int32)
    x_pad = jnp.concatenate([xt, jnp.zeros((1, D_), xt.dtype)], axis=0)
    xb = x_pad[tok_buf].reshape(n_blocks, MOE_BLOCK, D_)

    def expert_block(args):
        xblk, e = args
        gu = xblk @ w_gu[e] + b_gu[e]
        g, up = gu[:, :D_FF_2], gu[:, D_FF_2:]
        g = jnp.minimum(g, SWIGLU_LIMIT)
        up = jnp.clip(up, -SWIGLU_LIMIT, SWIGLU_LIMIT)
        act = (up + 1.0) * (g * jax.nn.sigmoid(SWIGLU_ALPHA * g))
        return act @ w_down[e] + b_down[e]

    yb = lax.map(expert_block, (xb, block_e)).reshape(cap, D_)
    out = jnp.zeros((N + 1, D_), f32).at[tok_buf].add(yb.astype(f32) * w_buf[:, None])[:N]
    return out.reshape(B_, T_, D_).astype(h.dtype)

def second_inputs(seed: int = 0) -> dict:
    key = jax.random.key(seed)
    ks = jax.random.split(key, 32)
    f32 = jnp.float32
    L, D = DEPTH, D_MODEL

    def nrm(k, shape, scale):
        return jax.random.normal(k, shape, f32) * scale

    n_idx = jnp.arange(S5_STATE, dtype=f32)
    return {
        "x": nrm(ks[0], (BATCH, SEQ, D), 1.0),
        "c": nrm(ks[1], (BATCH, D), 1.0),
        "ada_w": nrm(ks[2], (L, D, 6 * D), 0.02),
        "ada_b": nrm(ks[3], (L, 6 * D), 0.02),
        "mix_pre_g": 1.0 + nrm(ks[4], (L, D), 0.05),
        "mix_post_g": 1.0 + nrm(ks[5], (L, D), 0.05),
        "ffn_pre_g": 1.0 + nrm(ks[6], (L, D), 0.05),
        "ffn_post_g": 1.0 + nrm(ks[7], (L, D), 0.05),
        "w_in": nrm(ks[8], (L, D, N_IN), D ** -0.5),
        "w_alpha": nrm(ks[9], (L, GLA_LOWRANK, GLA_HEADS * GLA_DK), GLA_LOWRANK ** -0.5),
        "b_alpha": nrm(ks[10], (L, GLA_HEADS * GLA_DK), 0.1),
        "gla_norm_g": 1.0 + nrm(ks[11], (L, GLA_DV), 0.05),
        "s5_lambda_re": -0.5 + nrm(ks[12], (L, S5_GROUPS, S5_STATE), 0.01),
        "s5_lambda_im": math.pi * n_idx + nrm(ks[13], (L, S5_GROUPS, S5_STATE), 0.01),
        "s5_log_dt": jax.random.uniform(ks[14], (L, S5_GROUPS), f32, math.log(DT_MIN), math.log(DT_MAX)),
        "s5_b_re": nrm(ks[15], (L, S5_GROUPS, S5_STATE, S5_CH), (2 * S5_CH) ** -0.5),
        "s5_b_im": nrm(ks[16], (L, S5_GROUPS, S5_STATE, S5_CH), (2 * S5_CH) ** -0.5),
        "s5_c_re": nrm(ks[17], (L, S5_GROUPS, S5_CH, S5_STATE), S5_STATE ** -0.5),
        "s5_c_im": nrm(ks[18], (L, S5_GROUPS, S5_CH, S5_STATE), S5_STATE ** -0.5),
        "s5_d": nrm(ks[19], (L, S5_GROUPS, S5_CH), 1.0),
        "s5_glu_w": nrm(ks[20], (L, S5_WIDTH, S5_WIDTH), S5_WIDTH ** -0.5),
        "s5_glu_b": nrm(ks[21], (L, S5_WIDTH), 0.01),
        "w_out": nrm(ks[22], (L, D_MIX, D), D_MIX ** -0.5),
        "router_w": nrm(ks[23], (L, D, N_EXPERTS), D ** -0.5),
        "router_b": nrm(ks[24], (L, N_EXPERTS), 0.01),
        "exp_w_gu": nrm(ks[25], (L, N_EXPERTS, D, 2 * D_FF_2), D ** -0.5),
        "exp_b_gu": nrm(ks[26], (L, N_EXPERTS, 2 * D_FF_2), 0.01),
        "exp_w_down": nrm(ks[27], (L, N_EXPERTS, D_FF_2, D), D_FF_2 ** -0.5),
        "exp_b_down": nrm(ks[28], (L, N_EXPERTS, D), 0.01),
    }

def second_block(x, c, ada_w, ada_b, mix_pre_g, mix_post_g, ffn_pre_g, ffn_post_g, w_in, w_alpha, b_alpha,
              gla_norm_g, s5_lambda_re, s5_lambda_im, s5_log_dt, s5_b_re, s5_b_im, s5_c_re, s5_c_im, s5_d,
              s5_glu_w, s5_glu_b, w_out, router_w, router_b, exp_w_gu, exp_b_gu, exp_w_down, exp_b_down):
    B_, T_, D_ = x.shape
    h = x
    for l in range(DEPTH):
        mod = jax.nn.silu(c) @ ada_w[l] + ada_b[l]
        sh1, sc1, g1, sh2, sc2, g2 = jnp.split(mod, 6, axis=-1)

        hn = rmsnorm(h, mix_pre_g[l]) * (1.0 + sc1[:, None, :]) + sh1[:, None, :]
        proj = hn @ w_in[l]
        q, k, v, og, a_lr, u = jnp.split(proj, SPLITS, axis=-1)

        def heads(t, dh):
            return t.reshape(B_, T_, GLA_HEADS, dh).transpose(0, 2, 1, 3)

        log_a = jax.nn.log_sigmoid((a_lr @ w_alpha[l] + b_alpha[l]).astype(jnp.float32)) / GLA_TAU
        o = gla_chunked(heads(q, GLA_DK), heads(k, GLA_DK), heads(v, GLA_DV), heads(log_a, GLA_DK))
        o = rmsnorm(o, gla_norm_g[l]).transpose(0, 2, 1, 3)
        gla_out = (o * jax.nn.silu(og.astype(jnp.float32)).reshape(B_, T_, GLA_HEADS, GLA_DV))
        gla_out = gla_out.reshape(B_, T_, GLA_WIDTH).astype(hn.dtype)

        s5_out = s5_layer(u, s5_lambda_re[l], s5_lambda_im[l], s5_log_dt[l], s5_b_re[l], s5_b_im[l],
                          s5_c_re[l], s5_c_im[l], s5_d[l], s5_glu_w[l], s5_glu_b[l]).astype(hn.dtype)

        mix = jnp.concatenate([gla_out, s5_out], axis=-1) @ w_out[l]
        h = h + g1[:, None, :] * rmsnorm(mix, mix_post_g[l])

        hn2 = rmsnorm(h, ffn_pre_g[l]) * (1.0 + sc2[:, None, :]) + sh2[:, None, :]
        ff = moe_ffn(hn2, router_w[l], router_b[l], exp_w_gu[l], exp_b_gu[l], exp_w_down[l], exp_b_down[l])
        h = h + g2[:, None, :] * rmsnorm(ff, ffn_post_g[l])
    return h


def setup_inputs(seed=0):
    out = dict(first_inputs(seed))
    for name, value in second_inputs(seed + 1).items():
        if name != "x":
            out[name + "_2"] = value
    return out


def reference(
    x, mix_norm_pre, mix_norm_post, mlp_norm_pre, mlp_norm_post, w_in, conv_w, conv_b, w_rgate,
    b_rgate, w_igate, b_igate, lru_lambda, w_out, w_ff_in, w_ff_out, c_2, ada_w_2, ada_b_2,
    mix_pre_g_2, mix_post_g_2, ffn_pre_g_2, ffn_post_g_2, w_in_2, w_alpha_2, b_alpha_2,
    gla_norm_g_2, s5_lambda_re_2, s5_lambda_im_2, s5_log_dt_2, s5_b_re_2, s5_b_im_2, s5_c_re_2,
    s5_c_im_2, s5_d_2, s5_glu_w_2, s5_glu_b_2, w_out_2, router_w_2, router_b_2, exp_w_gu_2,
    exp_b_gu_2, exp_w_down_2, exp_b_down_2,
):
    x = first_block(
        x, mix_norm_pre, mix_norm_post, mlp_norm_pre, mlp_norm_post, w_in, conv_w, conv_b,
        w_rgate, b_rgate, w_igate, b_igate, lru_lambda, w_out, w_ff_in, w_ff_out,
    )
    return second_block(
        x, c_2, ada_w_2, ada_b_2, mix_pre_g_2, mix_post_g_2, ffn_pre_g_2, ffn_post_g_2, w_in_2,
        w_alpha_2, b_alpha_2, gla_norm_g_2, s5_lambda_re_2, s5_lambda_im_2, s5_log_dt_2,
        s5_b_re_2, s5_b_im_2, s5_c_re_2, s5_c_im_2, s5_d_2, s5_glu_w_2, s5_glu_b_2, w_out_2,
        router_w_2, router_b_2, exp_w_gu_2, exp_b_gu_2, exp_w_down_2, exp_b_down_2,
    )


_drawn_inputs = setup_inputs


def setup_inputs(seed=0):
    import zlib

    import numpy as np

    out = dict(_drawn_inputs(seed))
    spreads = {}
    factors = {'b_rgate': 8.0,
     'b_igate': 4.831,
     'ffn_post_g_2': 5.256,
     'gla_norm_g_2': 3.123,
     's5_lambda_re_2': 8.0,
     's5_log_dt_2': 3.152,
     's5_b_re_2': 2.979,
     's5_b_im_2': 3.029,
     's5_c_re_2': 3.108,
     's5_c_im_2': 3.003,
     's5_glu_b_2': 8.0,
     'router_b_2': 3.352,
     'exp_b_gu_2': 8.0,
     'exp_b_down_2': 8.0}
    for name, (base, spread) in spreads.items():
        noise = np.random.default_rng([zlib.crc32(name.encode()), seed]).standard_normal(out[name].shape)
        drawn = base * np.exp(spread * noise) if base else spread * noise
        out[name] = __import__('jax').numpy.asarray(drawn.astype(out[name].dtype))
    for name, factor in factors.items():
        out[name] = (out[name] * factor).astype(out[name].dtype)
    return out
```

```python
import math
from contextlib import ExitStack

import numpy as np

import concourse.bass as bass
from concourse import mybir

F32 = mybir.dt.float32
I32 = mybir.dt.int32
U32 = mybir.dt.uint32
ALU = mybir.AluOpType
ACT = mybir.ActivationFunctionType
AX = mybir.AxisListType

P = 128
T = 512
NT = T // P
D = 1024
KD = D // P
EPS = 1e-6
HALF = 512
FF = 4 * D
NF = FF // P
HEADS, DH = 8, 64
NEG = -1.0e30
LRU_C = 8.0
CONV = 4
NL = 4
GH, GDK, GDV, CH = 4, 64, 128, 64
NCH = T // CH
TAU = 16.0
SG, SC, SS = 32, 16, 64
NQ = SG // 2
SL = 8
SNC = T // SL
NPOW = SL + 1
TWO_PI = 2.0 * math.pi
PI_A = 6.28125
PI_B = 0.0019350051879882812
PI_C = TWO_PI - PI_A - PI_B
ROUND = 12582912.0
PI_MAX = 3.1415925
NE, TOPK = 32, 4
SWI_ALPHA, SWI_LIMIT = 1.702, 7.0
MAX_EXTRA = (T * TOPK - 1) // P
MAX_BLOCKS = NE + MAX_EXTRA
SLOTS = (MAX_BLOCKS + 1) * P
DRING = 4
RING = 6
BLK = KD * HALF
SCR = 22336

VECS = [("mix_norm_pre", 8), ("mlp_norm_pre", 8), ("mix_pre_g_2", 8), ("ffn_pre_g_2", 8),
        ("mix_post_g_2", 8), ("ffn_post_g_2", 8), ("conv_w", 16), ("conv_b", 4), ("b_rgate", 4),
        ("b_igate", 4), ("lru_lambda", 4), ("b_alpha_2", 2), ("s5_glu_b_2", 4), ("c_2", 8),
        ("ada_b_2", 48)]
NVEC = sum(n for _, n in VECS)
COL = {}
for _i, (_name, _n) in enumerate(VECS):
    COL[_name] = (sum(n for _, n in VECS[:_i]), _n)

N_SMALL = 16
N_S5 = 2 + 1 + SL

ST_SS, ST_R, ST_PS, ST_DEN, ST_MX = 0, 4, 8, 16, 32
ST_LAM, ST_MOD, ST_PG, ST_GR, ST_DEC = 64, 96, 112, 128, 160
ST_N = 192


def bank_plan():
    turns, plan, count = [0] * 8, {}, [0]

    def give(key, bank=None):
        if bank is None:
            bank, count[0] = count[0] % 8, count[0] + 1
        plan[key] = (bank, turns[bank])
        turns[bank] += 1

    def norm(s):
        return [("norm", s, i, h) for i in range(NT) for h in range(2)]

    keys = norm(1) + ["ada"] + [("s5b", n) for n in range(8)]
    keys += [("s5k", par, q4) for par in range(2) for q4 in range(4)]
    keys += [(w, m) for w in ("xr", "gr", "q", "k", "v") for m in range(4)]
    keys += [("gate", g, m) for m in range(NL) for g in range(2)]
    for key in keys:
        give(key)
    for i in range(NT):
        give(("o", i), 7)
        for h in range(HEADS):
            give(("s", i, h), h % 4)
            give(("pt", i, h), 4 + h % 2)
        give(("at", i), 6)
    count[0] = 0
    keys = [("wo", 1, i, n) for n in range(2) for i in range(NT)] + norm(2)
    keys += [("f1", m) for m in range(NF)] + [("f2", i, n) for i in range(NT) for n in range(2)]
    keys += norm(3) + [("pg", s, n) for s in range(2) for n in range(2)]
    keys += [("gq", m) for m in range(4)] + [("u", m) for m in range(4)] + ["a16"]
    keys += [("za", m) for m in range(2)] + [("gv", i) for i in range(NT)] + [("og", i) for i in range(NT)]
    keys += [("D", ri, q8) for ri in range(2) for q8 in range(2)]
    keys += [("ke", i) for i in range(NT)] + [("gs", h) for h in range(GH)]
    keys += [("gd", pair, cp) for pair in range(2) for cp in range(2)]
    keys += [("go", i, par) for i in range(NT) for par in range(2)] + [("gt", i) for i in range(NT)]
    keys += [("Y", par, q8) for par in range(2) for q8 in range(2)] + [("glu", m) for m in range(4)]
    keys += [("wo", 2, i, n) for n in range(2) for i in range(NT)] + norm(4) + ["lg", "rk"]
    for key in keys:
        give(key)
    return plan


def weight_plan():
    return ([("ada", c) for c in range(12)] + [("w_in", c) for c in (3, 4, 0, 1, 2)]
            + [("w_out", c) for c in range(2)] + [("ff_in", c) for c in range(8)]
            + [("ff_out", c) for c in range(8)]
            + [("w_in_2", c) for c in (0, 3, 1, 2)] + [("s5", c) for c in range(3)]
            + [("s5_glu", 0)] + [("w_out_2", c) for c in range(2)])


def program(nc, a, out):
    plan = bank_plan()
    blocks = weight_plan()
    block_no = {key: n for n, key in enumerate(blocks)}

    with ExitStack() as ctx:
        def sb(name, shape, dt=F32):
            return ctx.enter_context(nc.sbuf_tensor(name, shape, dt))

        def scratch(name, shape, dt=F32):
            return nc.dram_tensor(name, shape, dt, kind="Internal").ap()

        sems = {}

        def S(name):
            if name not in sems:
                sems[name] = ctx.enter_context(nc.semaphore(name))
            return sems[name]

        s5_dram = [scratch(f"s5_{n}", (P, BLK)) for n in ("inject", "toeplitz", "readout")]
        turn_dram = scratch("s5_turn", (P, 3 * NQ * SNC))
        u_dram = scratch("u_dram", (T, T))
        y_dram = scratch("y_dram", (T, T))
        xs_dram = scratch("xs_dram", (T, D))
        slot_token = scratch("slot_token", (SLOTS, 1), I32)
        y_slots = scratch("y_slots", (SLOTS, D))

        ring = sb("ring", [P, DRING * BLK])
        x_res = sb("x_res", [P, NT, D])
        actT = sb("actT", [P, KD, T])
        scr = sb("scr", [P, SCR])
        ident = sb("ident", [P, P])
        ones = sb("ones", [P, P])
        att_bias = sb("att_bias", [P, NT, P])
        gla_mask = sb("gla_mask", [P, NT, P], I32)
        chunk_go = sb("chunk_go", [P, T])
        before = sb("before", [P, P])
        cols = sb("cols", [P, NVEC])
        silu_c = sb("silu_c", [P, KD])
        post_g = sb("post_g", [P, 2, D])
        st = sb("st", [P, ST_N])
        eps = sb("eps", [P, 1])
        w_a16 = sb("w_a16", [P, KD, 16])
        w_alpha = sb("w_alpha", [16, GH * GDK])
        w_gate = sb("w_gate", [P, 2, NL, P])
        gla_g = sb("gla_g", [P, GDV])
        router_w = sb("router_w", [P, KD, NE])
        router_b = sb("router_b", [P, NE])
        tok_id = sb("tok_id", [P, NT], I32)

        def view(at, *shape, of=scr):
            ap = of[:, at:at + math.prod(shape)]
            if len(shape) == 1:
                return ap
            names = "abcd"[:len(shape)]
            return ap.rearrange(f"p ({' '.join(names)}) -> p {' '.join(names)}",
                                **dict(zip(names, shape)))

        def col(name, k=0, n=1):
            return cols[:, COL[name][0] + k:COL[name][0] + k + n]

        def over(ap, axis, n):
            ap = ap.unsqueeze(axis)
            shape = list(ap.shape)
            shape[axis] = n
            return ap.broadcast_to(shape)

        def slot(s):
            return ring[:, s * BLK:(s + 1) * BLK] if s < DRING else scr[:, (s - DRING) * BLK:(s - DRING + 1) * BLK]

        xn, junk, post_tmp = view(0, 2, D), view(2048, D), view(3072, 2, HALF)
        mask_f, dist = view(11264, NT, P), view(11776, NT, P).bitcast(I32)
        dist_i, cnt, cnt_t = view(12288, NT, P).bitcast(I32), view(12800, NT, P), view(13568, NT, P)
        par = view(3072, 3, NQ)
        b_r, b_i, c_r, c_i = (view(3120 + 256 * n, NQ, SC) for n in range(4))
        bb_r, bb_i, bb_t = (view(4144 + 256 * n, NQ, SC) for n in range(3))
        pw_l, pw_th, pw_k, pw_t, pw_r, pw_i = (view(4912 + 272 * n, NPOW, NQ) for n in range(6))
        s5_s = view(6544 - 0, 7, NQ)
        ca_r, ca_n, ca_t = view(6656, NQ, NPOW, SC), view(8960, NQ, NPOW, SC), view(11264, NQ, NPOW, SC)
        bx_r, bx_i = view(13568, NQ, SL, SC), view(15616, NQ, SL, SC)
        inject = view(17664, NQ, 2, P)
        taps = view(13568, 2, NQ, P)
        turn = view(17664, 3, NQ, SNC)
        ang, ang_k, ang_r = (view(13568 + 1024 * n, NQ, SNC) for n in range(3))
        zero = view(21760, HALF)
        step_i, step_f = view(14080, SNC).bitcast(I32), view(22272, SNC)
        s5_d = sb("s5_d", [SC, 2, NQ])
        att_s, att_pt, att_row = view(0, 4, T), view(2048, 2, NT, P), view(3072, T)
        qT, kT, v = view(4096, 4, T), view(6144, 4, T), view(8192, NT, T)
        xr, gr, xc = view(10240, NL, T), view(12288, NL, T), view(14336, NL, T)
        lru_a, lru_u = view(16384, NL, T), view(18432, NL, T)
        hidT = view(4096, NF, T)
        diag = view(20480, KD, P)
        gq, gk, g_t, g_b, g_e = (view(4096 + 1024 * n, 2, T) for n in range(5))
        g_end, g_endr, g_row = g_b, view(8192, NT, GH * GDK), view(6144, 2, T)
        gv, og = view(9216, NT, T), view(11264, NT, T)
        g_st = view(13312, 2, NCH - 1, GDV)
        a16 = view(15360, T)
        g_sT = actT[:, 0:4, :]
        uT = view(17920, 4, T)
        s5_u = view(15872, SG, SNC)
        s5_x = [view(17920 + 1024 * ri, NQ, SNC) for ri in range(2)]
        s5_v = [actT[:, 4 + 2 * ri:6 + 2 * ri, :].rearrange("p a (b c) -> p (a b) c", c=SNC) for ri in range(2)]
        s5_turn = view(0, 3, NQ, SNC)
        s5_tmp = view(19968, NQ, SNC)
        s5_y = view(17920, SG, SNC)
        yT = view(15872, 4, T)
        sig = view(19968, 2, T)
        xs = view(8192, NT, D)
        junk4 = view(18432, D)
        rt = 19456
        lg, mask = view(rt, NT, NE), view(rt + 128, NT, NE)
        pick, prod = view(rt + 256, NT, TOPK, NE), view(rt + 768, NT, TOPK, NE)
        rank, pos = view(rt + 1280, NT, NE), view(rt + 1408, NT, NE)
        cnt_e, ov, ov_in, base_hi, base_d = (view(rt + 1536 + 32 * n, NE) for n in range(5))
        le_f = view(rt + 1728, MAX_EXTRA + 1, NE)
        top_v, top_i, top_f = view(rt + 2240, NT, 8), view(rt + 2272, NT, 8).bitcast(U32), view(rt + 2304, NT, 8)
        gsum, posf, blk_f = view(rt + 2336, NT), view(rt + 2344, NT * TOPK), view(rt + 2360, NE)
        gate = sb("gate", [P, NT, TOPK])
        posi = sb("posi", [P, NT * TOPK], I32)
        blk_e = sb("blk_e", [1, 64], I32)
        bgu, bdn = view(8192, 2 * D), view(10240, D)
        bgu_row, bdn_row = view(11264, 2 * D), view(13312, D)
        y_row = view(14336, D)
        sw_t, sw_g, sw_s, sw_u, sw_p = (view(15360 + HALF * n, HALF) for n in range(5))
        slot_idx = sb("slot_idx", [P, 1], I32)
        xg = actT[:, 0:2, :].rearrange("p a b -> p (a b)")
        xgT = actT[:, 2:4, :].rearrange("p a (k s) -> p (a k) s", s=P)
        h_row = actT[:, 4:6, :].rearrange("p a b -> p (a b)")
        hT = actT[:, 6:8, :].rearrange("p a (k s) -> p (a k) s", s=P)
        y_pick = [view(n * D, D, of=ring) for n in range(NT * TOPK)]
        ff = scr[:, 8192:8192 + NT * D].rearrange("p (i d) -> p i d", i=NT)

        ps = ctx.enter_context(nc.psum_tensor("ps", [P, 8, HALF], F32))
        bank_full = [S(f"bank_full{b}") for b in range(8)]
        bank_copied = [S(f"bank_copied{b}") for b in range(8)]

        def full(eng, key):
            b, turn_no = plan[key]
            eng.wait_ge(bank_full[b], turn_no + 1)
            return ps[:, b, :]

        def copied(eng, key):
            b, turn_no = plan[key]
            eng.wait_ge(bank_copied[b], turn_no + 1)

        def out_of(key, ins):
            ins.then_inc(bank_copied[plan[key][0]], 1)

        def lam(n):
            return st[:, ST_LAM + NL * n:ST_LAM + NL * (n + 1)]

        def stepper(eng, name):
            n = [0]

            def step(ins):
                n[0] += 1
                ins.then_inc(S(name), 1)
                eng.wait_ge(S(name), n[0])
            return step

        block = ctx.enter_context(nc.Block())

        @block.sync
        def _(sp):
            for i in range(NT):
                sp.dma_start(x_res[:, i, :], a["x"][0, i * P:(i + 1) * P, :]).then_inc(S(f"x_in{i}"), 16)
            sp.wait_ge(S("small_in"), 16 * N_SMALL)

            def source(name, c):
                if name == "ff_out":
                    return a["w_ff_out"][0, c * HALF:(c + 1) * HALF, :].rearrange("(k p) n -> p k n", p=P)
                w = {"ada": "ada_w_2", "ff_in": "w_ff_in", "s5_glu": "s5_glu_w_2"}.get(name, name)
                at = c * HALF + (16 if (name, c) == ("w_in_2", 3) else 0)
                return a[w][0, :, at:at + HALF].rearrange("(k p) n -> p k n", p=P)

            last_job = {"w_in": lambda c: ("qkv"[c] if c < 3 else "xr gr".split()[c - 3], 3),
                        "w_out": lambda c: ("wo", 1, NT - 1, c), "ff_in": lambda c: ("f1", 4 * c + 3),
                        "w_in_2": lambda c: (("gq", "gv", "og", "u")[c], 3),
                        "s5": lambda c: ("Y", 1, 1) if c else ("D", 1, 1), "s5_glu": lambda c: ("glu", 3),
                        "w_out_2": lambda c: ("wo", 2, NT - 1, c)}

            def block_free(n):
                name, c = blocks[n]
                if name == "ada" and c < 11:
                    sp.wait_ge(S("ada_used"), c + 1)
                elif name == "ada":
                    full(sp, "ada")
                elif name == "ff_out" and c < 7:
                    sp.wait_ge(S("ff_out_used"), c + 1)
                elif name == "ff_out":
                    full(sp, ("f2", NT - 1, 1))
                else:
                    full(sp, last_job[name](c))

            for n, (name, c) in enumerate(blocks):
                s = n % DRING
                if n >= DRING:
                    block_free(n - DRING)
                dst = slot(s)
                if name == "s5":
                    if c == 0:
                        sp.wait_ge(S("s5_const"), 16 * N_S5)
                    sp.dma_start(dst, s5_dram[c]).then_inc(S(f"block_in{s}"), 16)
                else:
                    src = source(name, c)
                    sp.dma_start(dst[:, 0:src.shape[1] * src.shape[2]].rearrange("p (k n) -> p k n", k=src.shape[1]),
                                 src).then_inc(S(f"block_in{s}"), 16)

            def expert_blocks(e, b, js):
                for j in js:
                    if not (isinstance(b, int) and b == 0):
                        if j < 4:
                            sp.wait_ge(S("gu_full"), 4 * b + j - 3)
                        else:
                            sp.wait_ge(S("dn_full"), 2 * b + j - 5)
                    w = a["exp_w_gu_2"] if j < 4 else a["exp_w_down_2"]
                    at = (j % 2) * D + (j // 2) * HALF if j < 4 else (j - 4) * HALF
                    src = w[0, bass.ds(e, 1), :, at:at + HALF].rearrange("o (k p) n -> p (o k) n", p=P)
                    sp.dma_start(slot(j).rearrange("p (k n) -> p k n", k=KD), src).then_inc(S(f"part_in{j}"), 16)

            for n in range(len(blocks) - DRING, len(blocks)):
                block_free(n)
            sp.wait_ge(S("x_mix2"), NT)
            expert_blocks(0, 0, range(RING))
            sp.wait_ge(S("blocks_known"), 1)
            n_blocks = NE + sp.value_load(blk_e[0:1, 63:64], min_val=0, max_val=MAX_EXTRA)
            expert_blocks(1, 1, range(4))
            with sp.Fori(1, n_blocks - 1) as b:
                e = sp.value_load(blk_e[0:1, bass.ds(b, 1)], min_val=0, max_val=NE - 1)
                e_next = sp.value_load(blk_e[0:1, bass.ds(b + 1, 1)], min_val=0, max_val=NE - 1)
                expert_blocks(e_next, b + 1, range(4))
                expert_blocks(e, b, range(4, RING))
            expert_blocks(sp.value_load(blk_e[0:1, bass.ds(n_blocks - 1, 1)], min_val=0, max_val=NE - 1), n_blocks - 1,
                          range(4, RING))
            for i in range(NT):
                sp.wait_ge(S("x_final"), i + 1)
                sp.dma_start(out[0, i * P:(i + 1) * P, :], x_res[:, i, :]).then_inc(S("out_stored"), 16)
            sp.wait_ge(S("out_stored"), 16 * NT)

        @block.gpsimd
        def _(pool):
            step = stepper(pool, "pool_step")
            step(nc.gpsimd.memset(ident[:], 0.0))
            step(nc.gpsimd.affine_select(out=ident[:], in_=ident[:], compare_op=ALU.not_equal, fill=1.0,
                                         base=0, pattern=[[-1, P]], channel_multiplier=1))
            step(nc.gpsimd.memset(ones[:], 1.0))
            step(nc.gpsimd.memset(before[:], 1.0))
            step(nc.gpsimd.affine_select(out=before[:], in_=before[:], compare_op=ALU.is_gt, fill=0.0,
                                         base=0, pattern=[[1, P]], channel_multiplier=-1))
            step(nc.gpsimd.memset(eps[:], EPS))
            step(nc.gpsimd.memset(mask_f, 1.0))
            step(nc.gpsimd.affine_select(out=mask_f, in_=mask_f, compare_op=ALU.is_ge, fill=0.0,
                                         base=0, pattern=[[0, NT], [1, P]], channel_multiplier=-1))
            step(nc.gpsimd.memset(mask_f[0:CH, :, CH:P], 0.0))
            step(nc.gpsimd.iota(dist, pattern=[[-P, NT], [-1, P]], base=(NT - 1) * P, channel_multiplier=1))
            step(nc.gpsimd.iota(step_i, pattern=[[1, SNC]], base=0, channel_multiplier=0))
            step(nc.gpsimd.iota(tok_id[:], pattern=[[P, NT]], base=0, channel_multiplier=1))
            step(nc.gpsimd.memset(zero, 0.0))
            step(nc.gpsimd.memset(chunk_go[:], 1.0))
            nc.gpsimd.memset(chunk_go[:, ::CH], 0.0).then_inc(S("constants"), 1)

            pool.wait_ge(S("conv_ready"), NL)
            pool.dma_start(slot_token.rearrange("(b s) o -> b (s o)", s=P), zero[0:MAX_BLOCKS + 1, 0:P].bitcast(I32))\
                .then_inc(S("slots_cleared"), 16)
            pool.dma_start(y_slots[NE * P:, :].rearrange("(s b) (h d) -> s (b h) d", s=P, h=2),
                           over(zero, 1, 2 * (SLOTS // P - NE))).then_inc(S("slots_cleared"), 16)
            pool.wait_ge(S("slots_cleared"), 32)
            pool.wait_ge(S("slots_known"), 1)
            for n in range(NT * TOPK):
                pool.indirect_dma_start(slot_token[:, :], bass.IndirectOffsetOnAxis(posi[:, n:n + 1], 0),
                                        tok_id[:, n // TOPK:n // TOPK + 1], None).then_inc(S("slots_filled"), 16)
            pool.wait_ge(S("slots_filled"), 16 * NT * TOPK)
            pool.wait_ge(S("xs_stored"), 16 * NT)
            pool.wait_ge(S("blocks_known"), 1)

            def gather(b):
                pool.dma_start(slot_idx[:], slot_token[bass.ds(b * P, P), :]).then_inc(S("idx_in"), 16)
                pool.wait_ge(S("idx_in"), 16 * b + 16)
                if not isinstance(b, int):
                    pool.wait_ge(S("xgT_full"), b)
                pool.sem_inc(S("gather_clear"), 1)
                pool.indirect_dma_start(xg, None, xs_dram[:, :], bass.IndirectOffsetOnAxis(slot_idx[:, 0:1], 0))\
                    .then_inc(S("xg_in"), 16)
                pool.wait_ge(S("xg_in"), 16 * b + 16)

            def gate_bias(e, b):
                pool.dma_start(bgu_row[0:1, :], a["exp_b_gu_2"][0, bass.ds(e, 1), :]).then_inc(S("bgu_in"), 16)
                pool.wait_ge(S("bgu_in"), 16 * b + 16)
                if not isinstance(b, int):
                    pool.wait_ge(S("gu_copied"), 4 * b)
                pool.sem_inc(S("gate_bias_clear"), 1)
                nc.gpsimd.partition_broadcast(bgu, bgu_row[0:1, :], P).then_inc(S("bgu_ready"), 1)
                pool.wait_ge(S("bgu_ready"), b + 1)

            def down_bias(e, b):
                pool.dma_start(bdn_row[0:1, :], a["exp_b_down_2"][0, bass.ds(e, 1), :]).then_inc(S("bdn_in"), 16)
                pool.wait_ge(S("bdn_in"), 16 * b + 16)
                pool.wait_ge(S("y_done"), 2 * b + 1)
                pool.sem_inc(S("down_bias_clear"), 1)
                nc.gpsimd.partition_broadcast(bdn, bdn_row[0:1, :], P).then_inc(S("bdn_ready"), 1)
                pool.wait_ge(S("bdn_ready"), b + 1)

            n_blocks = NE + pool.value_load(blk_e[0:1, 63:64], min_val=0, max_val=MAX_EXTRA)

            def expert(b):
                return pool.value_load(blk_e[0:1, bass.ds(b, 1)], min_val=0, max_val=NE - 1)

            gather(0)
            gate_bias(0, 0)
            with pool.Fori(1, n_blocks) as b:
                gather(b)
                gate_bias(expert(b), b)
                down_bias(expert(b - 1), b - 1)
            gather(n_blocks)
            down_bias(expert(n_blocks - 1), n_blocks - 1)
            pool.wait_ge(S("y_stored"), 16 * n_blocks + 16)
            pool.sem_inc(S("pick_clear"), 1)
            for n in range(NT * TOPK):
                pool.indirect_dma_start(y_pick[n], None, y_slots[:, :],
                                        bass.IndirectOffsetOnAxis(posi[:, n:n + 1], 0)).then_inc(S(f"y_in{n // TOPK}"), 16)
            for i in range(NT):
                pool.wait_ge(S(f"y_in{i}"), 16 * TOPK)

        @block.scalar
        def _(act):
            step = stepper(act, "act_step")
            af = nc.scalar.activation
            small = [(cols[:], a["cols"]), (par, a["s5_par"]), (b_r, a["s5_b_re"]), (b_i, a["s5_b_im"]),
                     (c_r, a["s5_c_re"]), (c_i, a["s5_c_im"]), (s5_d[:], a["s5_d"]), (w_gate[:, 0], a["w_rgate"]),
                     (w_gate[:, 1], a["w_igate"]), (w_alpha[:], a["w_alpha_2"][0]),
                     (gla_g[:], a["gla_norm_g_2"][0].partition_broadcast(P)),
                     (router_w[:], a["router_w_2"][0].rearrange("(k p) n -> p k n", p=P)),
                     (router_b[:], a["router_b_2"][0].partition_broadcast(P)),
                     (post_g[:, 0, :], a["mix_norm_post"][0].partition_broadcast(P)),
                     (post_g[:, 1, :], a["mlp_norm_post"][0].partition_broadcast(P)),
                     (w_a16[:], a["w_in_2"][0, :, 1536:1552].rearrange("(k p) n -> p k n", p=P))]
            assert len(small) == N_SMALL
            for dst, src in small:
                act.dma_start(dst, src).then_inc(S("small_in"), 16)

            def squares(s, dst, ready):
                for i in range(NT):
                    act.wait_ge(*ready(i))
                    if i:
                        act.wait_ge(S(f"norm{s}_sum"), i)
                    af(dst, x_res[:, i, :], ACT.Square, accum_out=st[:, ST_SS + i:ST_SS + i + 1])\
                        .then_inc(S(f"norm{s}_sum"), 1)
                act.wait_ge(S(f"norm{s}_sum"), NT)
                af(st[:, ST_R:ST_R + NT], st[:, ST_SS:ST_SS + NT], ACT.Sqrt, scale=1.0 / D, bias=eps[:, 0:1])\
                    .then_inc(S(f"norm{s}_root"), 1)

            act.wait_ge(S("constants"), 1)
            squares(1, junk, lambda i: (S(f"x_in{i}"), 16))
            act.wait_ge(S("small_in"), 16 * N_SMALL)
            af(silu_c[:], col("c_2", 0, KD), ACT.Silu).then_inc(S("silu_c"), 1)
            act.wait_ge(S("att_count"), 1)
            af(att_bias[:], cnt_t, ACT.Ln).then_inc(S("att_log"), 1)
            af(s5_s[:, 0, :], par[:, 0, :], ACT.Exp).then_inc(S("s5_dt"), 1)
            act.wait_ge(S("s5_pow"), 1)
            step(af(pw_l, pw_l, ACT.Exp))
            step(af(pw_i, pw_th, ACT.Sin))
            af(pw_r, pw_t, ACT.Sin).then_inc(S("s5_sin"), 1)
            act.wait_ge(S("s5_ang"), 1)
            af(turn[:, 1], ang_r, ACT.Sin).then_inc(S("s5_turn"), 1)
            act.wait_ge(S("s5_ang"), 2)
            af(turn[:, 0], ang_r, ACT.Sin).then_inc(S("s5_turn"), 1)
            act.wait_ge(S("s5_turn"), 3)
            act.dma_start(turn_dram, turn.rearrange("p a b c -> p (a b c)")).then_inc(S("turn_stored"), 16)
            for n in range(BLK // HALF):
                act.dma_start(s5_dram[1][:, n * HALF:(n + 1) * HALF], zero).then_inc(S("toeplitz_zero"), 16)
            act.wait_ge(S("ca_ready"), 1)
            ro = s5_dram[2].rearrange("p (q r n) -> p q r n", q=NQ, r=2)
            for ri, ca in enumerate((ca_r, ca_n)):
                act.dma_start(ro[:, :, ri, :], ca[:, :, 1:NPOW, :].rearrange("p q t h -> p q (t h)"))\
                    .then_inc(S("s5_const"), 16)
            act.wait_ge(S("turn_stored"), 16)
            for n in range(8):
                dst = inject.rearrange("p q r n -> p (q r) n")[:, 4 * n:4 * n + 4, :]
                src = full(act, ("s5b", n)).rearrange("p (a n) -> p a n", a=4)
                out_of(("s5b", n), af(dst, src, ACT.Copy))
            for n in range(8):
                copied(act, ("s5b", n))
            act.dma_start(s5_dram[0], inject.rearrange("p q r n -> p (q r n)")).then_inc(S("s5_const"), 16)
            act.wait_ge(S("taps_ready"), 1)
            act.wait_ge(S("toeplitz_zero"), 16 * (BLK // HALF))
            tz = s5_dram[1].rearrange("p (g n) -> p g n", g=SG)
            tp = taps.rearrange("p r q n -> p (r q) n")
            for j in range(SL):
                act.dma_start(tz[j * SC:(j + 1) * SC, :, j * SC:P], tp[0:SC, :, 0:P - j * SC])\
                    .then_inc(S("s5_const"), 16)
            act.wait_ge(S("s5_const"), 16 * N_S5)

            for m in range(4):
                out_of(("xr", m), af(xr[:, m, :], full(act, ("xr", m)), ACT.Copy))
            for m in range(4):
                out_of(("gr", m), af(gr[:, m, :], full(act, ("gr", m)), ACT.Gelu_apprx_tanh))
            for m in range(4):
                out_of(("q", m), af(qT[:, m, :], full(act, ("q", m)), ACT.Copy, scale=DH ** -0.5))
            for m in range(4):
                out_of(("k", m), af(kT[:, m, :], full(act, ("k", m)), ACT.Copy))
            for m in range(4):
                out_of(("v", m), af(v[:, m, :], full(act, ("v", m)), ACT.Copy))
            act.wait_ge(S("lam_ready"), 1)
            af(lam(1), lam(0), ACT.Exp, scale=-1.0).then_inc(S("lam_act"), 1)
            act.wait_ge(S("lam_ready"), 2)
            af(lam(3), lam(2), ACT.Ln).then_inc(S("lam_act"), 1)
            for m in range(NL):
                out_of(("gate", 0, m), af(lru_a[:, m, :], full(act, ("gate", 0, m)), ACT.Sigmoid,
                                          bias=col("b_rgate", m)))
                out_of(("gate", 1, m), af(xr[:, m, :], full(act, ("gate", 1, m)), ACT.Sigmoid,
                                          bias=col("b_igate", m)))
            act.wait_ge(S("lam_ready"), 3)
            for m in range(NL):
                copied(act, ("gate", 0, m))
                step(af(lru_u[:, m, :], lru_a[:, m, :], ACT.Tanh, scale=lam(1)[:, m:m + 1]))
                af(lru_a[:, m, :], lru_a[:, m, :], ACT.Exp, scale=lam(0)[:, m:m + 1]).then_inc(S("lru_decay"), 1)
            for m in range(NL):
                act.wait_ge(S("lru_square"), m + 1)
                af(lru_u[:, m, :], lru_u[:, m, :], ACT.Sqrt).then_inc(S("lru_root"), 1)
            for i in range(NT):
                n = (i + 1) * P
                for h in range(HEADS):
                    act.wait_ge(S("att_max"), HEADS * i + h + 1)
                    af(att_s[:, h % 4, 0:n], att_s[:, h % 4, 0:n], ACT.Exp,
                       bias=st[:, ST_MX + 8 + h:ST_MX + 9 + h],
                       accum_out=st[:, ST_DEN + h:ST_DEN + h + 1]).then_inc(S("att_exp"), 1)
                    bank = full(act, ("pt", i, h))
                    if h >= 2:
                        act.wait_ge(S("att_pv"), (HEADS - 1) * i + h - 1)
                    elif i and h == 0:
                        act.wait_ge(S("att_pv"), (HEADS - 1) * i)
                    elif i:
                        full(act, ("o", i - 1))
                    out_of(("pt", i, h), af(att_pt[:, h % 2, 0:i + 1, :],
                                            bank[:, 0:n].rearrange("p (j n) -> p j n", n=P), ACT.Copy))
                bank = full(act, ("at", i))
                out_of(("at", i), af(actT[:, 0:4, i * P:(i + 1) * P], bank.rearrange("p (m n) -> p m n", m=4),
                                     ACT.Copy))

            def post_squares(s, key):
                for n in range(2):
                    for i in range(NT):
                        bank = full(act, key(i, n))
                        c = ST_PS + NT * n + i
                        if c > ST_PS:
                            act.wait_ge(S(f"post{s}_sum"), NT * n + i)
                        af(post_tmp[:, 0, :], bank, ACT.Square, accum_out=st[:, c:c + 1])\
                            .then_inc(S(f"post{s}_sum"), 1)
                act.wait_ge(S(f"post{s}_both"), 1)
                af(st[:, ST_R:ST_R + NT], st[:, ST_R:ST_R + NT], ACT.Sqrt, scale=1.0 / D, bias=eps[:, 0:1])\
                    .then_inc(S(f"post{s}_root"), 1)

            post_squares(1, lambda i, n: ("wo", 1, i, n))
            squares(2, junk, lambda i: (S("x_mix1"), i + 1))
            for m in range(NF):
                copied(act, ("f1", m))
                af(hidT[:, m, :], hidT[:, m, :], ACT.Square).then_inc(S("hid_ready"), 1)
            post_squares(2, lambda i, n: ("f2", i, n))
            squares(3, junk, lambda i: (S("x_mlp"), i + 1))

            for m in range(2):
                out_of(("gq", m), af(gq[:, m, :], full(act, ("gq", m)), ACT.Copy, scale=GDK ** -0.5))
            for m in range(2):
                out_of(("gq", 2 + m), af(gk[:, m, :], full(act, ("gq", 2 + m)), ACT.Copy))
            for m in range(4):
                out_of(("u", m), af(uT[:, m, :].rearrange("p (j c) -> p j c", j=SL),
                                    full(act, ("u", m)).rearrange("p (c j) -> p j c", j=SL), ACT.Copy))
            for m in range(4):
                copied(act, ("u", m))
                act.dma_start(u_dram[m * P:(m + 1) * P, :], uT[:, m, :]).then_inc(S("u_stored"), 16)
            act.dma_start(s5_turn.rearrange("p a b c -> p (a b c)"), turn_dram).then_inc(S("turn_in"), 16)
            out_of("a16", af(a16[0:16, :], full(act, "a16")[0:16, :], ACT.Copy))
            act.wait_ge(S("u_stored"), 16 * 4)
            ud = u_dram.rearrange("(g h) (j c) -> j h g c", h=SC, j=SL)
            for j in range(SL):
                act.dma_start(s5_u[j * SC:(j + 1) * SC, :, :], ud[j]).then_inc(S("u_in"), 16)
            for i in range(NT):
                out_of(("gv", i), af(gv[:, i, :], full(act, ("gv", i)), ACT.Copy))
            for i in range(NT):
                out_of(("og", i), af(og[:, i, :], full(act, ("og", i)), ACT.Silu))
            act.wait_ge(S("gla_abs"), 1)
            step(af(g_b, g_b, ACT.Exp, scale=-1.0))
            af(g_b, g_b, ACT.Ln, bias=1.0).then_inc(S("gla_log"), 1)
            act.wait_ge(S("gla_cum"), 1)
            step(af(g_e, g_b, ACT.Exp, scale=-1.0 / TAU))
            af(g_t, g_b, ACT.Exp, scale=1.0 / TAU).then_inc(S("gla_exp"), 1)
            for i in range(NT):
                for par_ in range(2):
                    bank = full(act, ("go", i, par_))
                    for hh in range(2):
                        c = ST_GR + 4 * i + 2 * par_ + hh
                        step(af(a16[:, 0:GDV], bank[:, hh * GDV:(hh + 1) * GDV], ACT.Square,
                                accum_out=st[:, c:c + 1]))
                r = st[:, ST_GR + 4 * i:ST_GR + 4 * i + 4]
                af(r, r, ACT.Sqrt, scale=1.0 / GDV, bias=eps[:, 0:1]).then_inc(S("gla_root"), 1)
            for i in range(NT):
                out_of(("gt", i), af(actT[:, 0:4, i * P:(i + 1) * P],
                                     full(act, ("gt", i)).rearrange("p (m n) -> p m n", m=4), ACT.Copy))
            for par_ in range(2):
                for q8 in range(2):
                    bank = full(act, ("Y", par_, q8))
                    dst = s5_y.rearrange("p (q r) c -> p q r c", r=2)[:, q8 * 8:(q8 + 1) * 8, par_, :]
                    out_of(("Y", par_, q8), af(dst, bank.rearrange("p (q c) -> p q c", q=8), ACT.Copy))
            for par_ in range(2):
                for q8 in range(2):
                    copied(act, ("Y", par_, q8))
            yd = y_dram.rearrange("(g h) (j c) -> j h g c", h=SC, j=SL)
            for j in range(SL):
                act.dma_start(yd[j], s5_y[j * SC:(j + 1) * SC, :, :]).then_inc(S("y5_stored"), 16)
            act.wait_ge(S("y5_stored"), 16 * SL)
            act.dma_start(yT, y_dram.rearrange("(m p) n -> p m n", p=P)).then_inc(S("y5_in"), 16)
            act.wait_ge(S("y5_in"), 16)
            for m in range(4):
                af(yT[:, m, :], yT[:, m, :], ACT.Gelu_apprx_tanh).then_inc(S("y5_gelu"), 1)
            for m in range(4):
                bank = full(act, ("glu", m))
                if m >= 2:
                    act.wait_ge(S("s5_out"), m - 1)
                out_of(("glu", m), af(sig[:, m % 2, :], bank, ACT.Sigmoid, bias=col("s5_glu_b_2", m)))
            post_squares(3, lambda i, n: ("wo", 2, i, n))
            squares(4, junk4, lambda i: (S("x_mix2"), i + 1))
            for i in range(NT):
                act.wait_ge(S("xn4_ready"), i + 1)
                act.dma_start(xs_dram[i * P:(i + 1) * P, :], xs[:, i, :]).then_inc(S("xs_stored"), 16)
            act.wait_ge(S("top_diff"), 1)
            af(gate[:], gate[:], ACT.Exp).then_inc(S("top_exp"), 1)

            act.wait_ge(S("blocks_known"), 1)
            n_blocks = NE + act.value_load(blk_e[0:1, 63:64], min_val=0, max_val=MAX_EXTRA)

            def input_out(b):
                act.wait_ge(S("xgT_full"), b + 1)
                for k in range(KD):
                    ins = af(xgT[:, k, :], ps[:, 6 + k // 4, (k % 4) * P:(k % 4 + 1) * P], ACT.Identity,
                             scale=st[:, ST_MOD + 8 + k:ST_MOD + 9 + k], bias=col("ada_b_2", 3 * KD + k))
                ins.then_inc(S("xgT_ready"), 1)

            def gates(b):
                for hf in range(2):
                    act.wait_ge(S("sw_gate"), 2 * b + hf + 1)
                    if not isinstance(b, int) or hf:
                        act.wait_ge(S("sw_done"), 2 * b + hf)
                    af(sw_s, sw_g, ACT.Sigmoid, scale=SWI_ALPHA).then_inc(S("sw_sig"), 1)

            def hidden_out(b):
                act.wait_ge(S("hT_full"), b + 1)
                for half in range(2):
                    ins = af(hT[:, 4 * half:4 * half + 4, :], ps[:, 6 + half, :].rearrange("p (k s) -> p k s", k=4),
                             ACT.Copy)
                ins.then_inc(S("hT_ready"), 1)

            def store(b):
                act.wait_ge(S("y_done"), 2 * b + 3)
                act.dma_start(y_slots[bass.ds(b * P, P), :], y_row).then_inc(S("y_stored"), 16)

            act.sem_inc(S("y_stored"), 16)
            input_out(0)
            gates(0)
            input_out(1)
            hidden_out(0)
            with act.Fori(1, n_blocks) as b:
                gates(b)
                input_out(b + 1)
                store(b - 1)
                hidden_out(b)
            store(n_blocks - 1)
            for i in range(NT):
                act.wait_ge(S("ff_ready"), i + 1)
                r = st[:, ST_SS + i:ST_SS + i + 1]
                step(af(junk4, ff[:, i, :], ACT.Square, accum_out=r))
                af(r, r, ACT.Sqrt, scale=1.0 / D, bias=eps[:, 0:1]).then_inc(S("ff_root"), 1)
            act.wait_ge(S("ff_root"), NT)

        @block.vector
        def _(dve):
            step = stepper(dve, "dve_step")
            tt, ts, stt = nc.vector.tensor_tensor, nc.vector.tensor_scalar, nc.vector.scalar_tensor_tensor
            cp, scan = nc.vector.tensor_copy, nc.vector.tensor_tensor_scan

            dve.wait_ge(S("constants"), 1)
            step(cp(gla_mask[:], mask_f))
            step(cp(step_f, step_i))

            def norm(s, gain, shift=None):
                r = st[:, ST_R:ST_R + NT]
                dve.wait_ge(S(f"norm{s}_root"), 1)
                step(nc.vector.reciprocal(r, r))

                def rows(i):
                    if s < 4 and i >= 2:
                        full(dve, ("norm", s, i - 2, 1))
                    dst = xs[:, i, :] if s == 4 else xn[:, i % 2, :]
                    ts(dst, x_res[:, i, :], r[:, i:i + 1], None, ALU.mult).then_inc(S(f"xn{s}_ready"), 1)

                def transposed(i):
                    for h in range(2):
                        key = ("norm", s, i, h)
                        bank = full(dve, key).rearrange("p (k n) -> p k n", n=P)
                        dst = actT[:, 4 * h:4 * h + 4, i * P:(i + 1) * P]
                        out_of(key, tt(dst, bank, over(gain[:, 4 * h:4 * h + 4], 2, P), ALU.mult))
                        if shift is not None:
                            copied(dve, key)
                            tt(dst, dst, over(shift[:, 4 * h:4 * h + 4], 2, P), ALU.add)\
                                .then_inc(S(f"norm{s}_half"), 1)

                rows(0)
                for i in range(1, NT):
                    rows(i)
                    transposed(i - 1)
                transposed(NT - 1)

            dve.wait_ge(S("small_in"), 16 * N_SMALL)
            norm(1, col("mix_norm_pre", 0, KD))

            for bits, dst in ((15, cnt), (3, cnt_t)):
                step(ts(dist_i, dist, bits, None, ALU.bitwise_and))
                step(ts(dst, dist_i, 0.0, None, ALU.is_equal))
            step(tt(cnt, cnt, cnt_t, ALU.add))
            step(ts(cnt_t, dist, float(P), None, ALU.is_le))
            step(tt(cnt, cnt, cnt_t, ALU.add))
            step(ts(cnt_t, dist, 0.0, None, ALU.is_ge))
            step(tt(cnt, cnt, cnt_t, ALU.mult))
            ts(cnt_t, cnt, 1.0, None, ALU.max).then_inc(S("att_count"), 1)
            step(ts(cnt, cnt, 0.0, NEG, ALU.is_equal, ALU.mult))
            dve.wait_ge(S("att_log"), 1)
            step(tt(att_bias[:], att_bias[:], cnt, ALU.add))

            def reduced(dst, src, k, quarter):
                step(ts(k, src, 1.0 / TWO_PI, 0.25 * quarter, ALU.mult, ALU.add))
                step(ts(k, k, ROUND, None, ALU.add))
                step(ts(k, k, -ROUND, None, ALU.add))
                step(stt(dst, k, -PI_A, src, ALU.mult, ALU.add))
                step(stt(dst, k, -PI_B, dst, ALU.mult, ALU.add))
                step(stt(dst, k, -PI_C, dst, ALU.mult, ALU.add))
                if quarter:
                    step(ts(dst, dst, 0.5 * math.pi, None, ALU.add))
                return ts(dst, dst, PI_MAX, -PI_MAX, ALU.min, ALU.max)

            dt, s1, s2, s3, s4, s5, _ = (s5_s[:, n, :] for n in range(7))
            lr, li = par[:, 1, :], par[:, 2, :]
            dve.wait_ge(S("s5_dt"), 1)
            step(tt(s1, lr, dt, ALU.mult))
            step(tt(s2, li, dt, ALU.mult))
            step(reduced(s3, s2, s4, 0))
            taus = over(step_f[:, 0:NPOW], 2, NQ)
            step(tt(pw_l[:, 0:NPOW], taus, over(s1, 1, NPOW), ALU.mult))
            step(tt(pw_k[:, 0:NPOW], taus, over(s3, 1, NPOW), ALU.mult))
            step(reduced(pw_t[:, 0:NPOW], pw_k[:, 0:NPOW], pw_i[:, 0:NPOW], 1))
            reduced(pw_th[:, 0:NPOW], pw_k[:, 0:NPOW], pw_i[:, 0:NPOW], 0).then_inc(S("s5_pow"), 1)
            dve.wait_ge(S("s5_sin"), 1)
            ar, ai = pw_r, pw_i
            step(tt(ar[:, 0:NPOW], ar[:, 0:NPOW], pw_l[:, 0:NPOW], ALU.mult))
            step(tt(ai[:, 0:NPOW], ai[:, 0:NPOW], pw_l[:, 0:NPOW], ALU.mult))
            step(tt(ang, over(pw_th[:, SL, :], 2, SNC), over(step_f, 1, NQ), ALU.mult))
            reduced(ang_r, ang, ang_k, 0).then_inc(S("s5_ang"), 1)
            step(cp(turn[:, 2], over(pw_l[:, SL, :], 2, SNC)))
            nc.vector.memset(turn[:, 2, :, 0:1], 0.0).then_inc(S("s5_turn"), 1)
            dve.wait_ge(S("s5_turn"), 2)
            reduced(ang_r, ang, ang_k, 1).then_inc(S("s5_ang"), 1)
            step(tt(s1, lr, lr, ALU.mult))
            step(tt(s2, li, li, ALU.mult))
            step(tt(s1, s1, s2, ALU.add))
            step(nc.vector.reciprocal(s1, s1))
            step(ts(s2, ar[:, 1, :], -1.0, None, ALU.add))
            step(tt(s3, s2, lr, ALU.mult))
            step(tt(s4, ai[:, 1, :], li, ALU.mult))
            step(tt(s3, s3, s4, ALU.add))
            step(tt(s3, s3, s1, ALU.mult))
            step(tt(s4, ai[:, 1, :], lr, ALU.mult))
            step(tt(s5, s2, li, ALU.mult))
            step(tt(s4, s4, s5, ALU.subtract))
            step(tt(s4, s4, s1, ALU.mult))
            fr, fi = over(s3, 2, SC), over(s4, 2, SC)
            step(tt(bb_r, fr, b_r, ALU.mult))
            step(tt(bb_t, fi, b_i, ALU.mult))
            step(tt(bb_r, bb_r, bb_t, ALU.subtract))
            step(tt(bb_i, fr, b_i, ALU.mult))
            step(tt(bb_t, fi, b_r, ALU.mult))
            step(tt(bb_i, bb_i, bb_t, ALU.add))
            c9r, c9i = over(c_r, 2, NPOW), over(c_i, 2, NPOW)
            a9r, a9i = (over(x[:, 0:NPOW].rearrange("p t q -> p q t"), 3, SC) for x in (ar, ai))
            step(tt(ca_r, c9r, a9r, ALU.mult))
            step(tt(ca_t, c9i, a9i, ALU.mult))
            step(tt(ca_r, ca_r, ca_t, ALU.subtract))
            step(tt(ca_n, c9r, a9i, ALU.mult))
            step(tt(ca_t, c9i, a9r, ALU.mult))
            step(stt(ca_n, ca_n, -1.0, ca_t, ALU.mult, ALU.subtract))
            for j in range(SL):
                cp(pw_t[:, j, :], ar[:, SL - 1 - j, :])
                ins = cp(pw_th[:, j, :], ai[:, SL - 1 - j, :])
            ins.then_inc(S("ca_ready"), 1)
            dve.wait_ge(S("ca_ready"), 1)
            dve.wait_ge(S("s5_turn"), 3)
            b8r, b8i = over(bb_r, 2, SL), over(bb_i, 2, SL)
            a8r, a8i = (over(x[:, 0:SL].rearrange("p t q -> p q t"), 3, SC) for x in (pw_t, pw_th))
            tmp8 = ca_t[:, :, 0:SL, :]
            step(tt(bx_r, b8r, a8r, ALU.mult))
            step(tt(tmp8, b8i, a8i, ALU.mult))
            step(tt(bx_r, bx_r, tmp8, ALU.subtract))
            step(tt(bx_i, b8r, a8i, ALU.mult))
            step(tt(tmp8, b8i, a8r, ALU.mult))
            tt(bx_i, bx_i, tmp8, ALU.add).then_inc(S("bx_ready"), 1)
            bank = full(dve, "ada")
            mod = col("ada_b_2", 0, 6 * KD)
            out_of("ada", tt(mod, bank[:, 0:6 * KD], mod, ALU.add))
            copied(dve, "ada")
            for s, name in enumerate(("mix_pre_g_2", "ffn_pre_g_2")):
                step(stt(st[:, ST_MOD + KD * s:ST_MOD + KD * (s + 1)], mod[:, (3 * s + 1) * KD:(3 * s + 2) * KD], 1.0,
                         col(name, 0, KD), ALU.add, ALU.mult))
            for s, name in enumerate(("mix_post_g_2", "ffn_post_g_2")):
                step(tt(st[:, ST_PG + KD * s:ST_PG + KD * (s + 1)], mod[:, (3 * s + 2) * KD:(3 * s + 3) * KD],
                        col(name, 0, KD), ALU.mult))

            for par_ in range(2):
                for q4 in range(4):
                    key = ("s5k", par_, q4)
                    bank = full(dve, key)[0:SC, :].rearrange("p (q n) -> p q n", q=4)
                    out_of(key, cp(taps[0:SC, par_, 4 * q4:4 * q4 + 4, :], bank))
            for par_ in range(2):
                for q4 in range(4):
                    copied(dve, ("s5k", par_, q4))
            direct = ca_t.rearrange("p q t h -> p (q t h)")[0:SC, 0:SG * SC].rearrange("p (g h) -> p g h", g=SG)
            first = taps.rearrange("p r q n -> p (r q) n")[0:SC, :, 0:SC]
            step(tt(direct, over(ident[0:SC, 0:SC], 1, SG), over(s5_d[:].rearrange("p r q -> p (r q)"), 2, SC), ALU.mult))
            tt(first, first, direct, ALU.add).then_inc(S("taps_ready"), 1)

            for m in range(NL):
                copied(dve, ("xr", m))
                w = lambda t: col("conv_w", 4 * t + m)
                step(ts(xc[:, m, :], xr[:, m, :], w(CONV - 1), col("conv_b", m), ALU.mult, ALU.add))
                for t in range(CONV - 1):
                    back = CONV - 1 - t
                    ins = stt(xc[:, m, back:], xr[:, m, 0:T - back], w(t), xc[:, m, back:], ALU.mult, ALU.add)
                    if t < CONV - 2:
                        step(ins)
                ins.then_inc(S("conv_ready"), 1)
            lm = col("lru_lambda", 0, NL)
            step(ts(lam(5), lm, -1.0, None, ALU.mult))
            tt(lam(0), lm, lam(5), ALU.max).then_inc(S("lam_ready"), 1)
            dve.wait_ge(S("lam_act"), 1)
            ts(lam(2), lam(1), 1.0, None, ALU.add).then_inc(S("lam_ready"), 1)
            dve.wait_ge(S("lam_ready"), 2)
            step(ts(lam(4), lam(2), -1.0, None, ALU.add))
            step(ts(lam(5), lam(4), 0.0, None, ALU.is_equal))
            step(tt(lam(4), lam(4), lam(5), ALU.add))
            step(nc.vector.reciprocal(lam(4), lam(4)))
            step(tt(lam(4), lam(4), lam(1), ALU.mult))
            step(tt(lam(5), lam(5), lam(1), ALU.mult))
            dve.wait_ge(S("lam_act"), 2)
            step(tt(lam(3), lam(3), lam(4), ALU.mult))
            step(tt(lam(3), lam(3), lam(5), ALU.add))
            step(ts(lam(6), lm, -1.0, 0.0, ALU.mult, ALU.max))
            step(tt(lam(6), lam(6), lam(3), ALU.add))
            step(ts(lam(0), lam(6), -LRU_C, None, ALU.mult))
            ts(lam(1), lam(6), LRU_C, None, ALU.mult).then_inc(S("lam_ready"), 1)
            lru_t = att_pt.rearrange("p b j n -> p (b j n)")[:, 0:T]
            for m in range(NL):
                dve.wait_ge(S("lru_decay"), m + 1)
                step(tt(lru_t, lru_a[:, m, :], lru_a[:, m, :], ALU.mult))
                stt(lru_u[:, m, :], lru_t, 1.0, lru_u[:, m, :], ALU.add, ALU.mult).then_inc(S("lru_square"), 1)
                dve.wait_ge(S("lru_square"), m + 1)
            for m in range(NL):
                copied(dve, ("gate", 1, m))
                step(tt(xr[:, m, :], xr[:, m, :], xc[:, m, :], ALU.mult))
                dve.wait_ge(S("lru_root"), m + 1)
                step(tt(lru_u[:, m, :], lru_u[:, m, :], xr[:, m, :], ALU.mult))
                step(scan(xc[:, m, :], lru_a[:, m, :], lru_u[:, m, :], 0.0, ALU.mult, ALU.add))
                copied(dve, ("gr", m))
                tt(actT[:, 4 + m, :], xc[:, m, :], gr[:, m, :], ALU.mult).then_inc(S("rec_ready"), 1)

            mx, nmx = st[:, ST_MX:ST_MX + 8], st[:, ST_MX + 8:ST_MX + 16]
            den, rden = st[:, ST_DEN:ST_DEN + 8], st[:, ST_DEN + 8:ST_DEN + 16]
            for i in range(NT):
                n = (i + 1) * P
                bias = att_bias[:, NT - 1 - i:NT, :].rearrange("p r n -> p (r n)")
                for h in range(HEADS):
                    if h >= 4:
                        full(dve, ("pt", i, h - 4))
                    elif i:
                        full(dve, ("pt", i - 1, h + 4))
                    key = ("s", i, h)
                    bank = full(dve, key)
                    out_of(key, nc.vector.tensor_tensor_reduce(
                        out=att_s[:, h % 4, 0:n], in0=bank[:, 0:n], in1=bias, scale=1.0, scalar=NEG,
                        op0=ALU.add, op1=ALU.max, accum_out=mx[:, h:h + 1]))
                    copied(dve, key)
                    ts(nmx[:, h:h + 1], mx[:, h:h + 1], -1.0, None, ALU.mult).then_inc(S("att_max"), 1)
                dve.wait_ge(S("att_exp"), HEADS * (i + 1))
                step(nc.vector.reciprocal(rden, den))
                if i:
                    full(dve, ("at", i - 1))
                bank = full(dve, ("o", i))
                out_of(("o", i), tt(att_row.rearrange("p (h d) -> p h d", h=HEADS),
                                    bank.rearrange("p (h d) -> p h d", h=HEADS), over(rden, 2, DH), ALU.mult))

            def post(s, key, gain, done):
                r = st[:, ST_R:ST_R + NT]
                dve.wait_ge(S(f"post{s}_sum"), 2 * NT)
                tt(r, st[:, ST_PS:ST_PS + NT], st[:, ST_PS + NT:ST_PS + 2 * NT], ALU.add)\
                    .then_inc(S(f"post{s}_both"), 1)
                dve.wait_ge(S(f"post{s}_root"), 1)
                step(nc.vector.reciprocal(r, r))
                for i in range(NT):
                    for n in range(2):
                        half = slice(n * HALF, (n + 1) * HALF)
                        out_of(key(i, n), stt(post_tmp[:, n, :], ps[:, plan[key(i, n)][0], :], r[:, i:i + 1],
                                              gain[:, half], ALU.mult, ALU.mult))
                        copied(dve, key(i, n))
                        ins = tt(x_res[:, i, half], x_res[:, i, half], post_tmp[:, n, :], ALU.add)
                        if n == 0:
                            step(ins)
                    ins.then_inc(S(done), 1)
                    dve.wait_ge(S(done), i + 1)

            post(1, lambda i, n: ("wo", 1, i, n), post_g[:, 0, :], "x_mix1")
            norm(2, col("mlp_norm_pre", 0, KD))
            for m in range(NF):
                out_of(("f1", m), ts(hidT[:, m, :], full(dve, ("f1", m)), 0.0, None, ALU.max))
            post(2, lambda i, n: ("f2", i, n), post_g[:, 1, :], "x_mlp")
            norm(3, st[:, ST_MOD:ST_MOD + KD], mod[:, 0:KD])
            for s in range(2):
                for k in range(KD):
                    ins = ts(diag[:, k, :], ident[:], st[:, ST_PG + KD * s + k:ST_PG + KD * s + k + 1], None, ALU.mult)
                ins.then_inc(S("diag_ready"), 1)
                for n in range(2):
                    out_of(("pg", s, n), cp(post_g[:, s, n * HALF:(n + 1) * HALF], full(dve, ("pg", s, n))))

            for m in range(2):
                out_of(("za", m), ts(g_t[:, m, :], full(dve, ("za", m)), col("b_alpha_2", m), None, ALU.add))
            for m in range(2):
                copied(dve, ("za", m))
            stt(g_b, g_t, -1.0, g_t, ALU.mult, ALU.max).then_inc(S("gla_abs"), 1)
            dve.wait_ge(S("gla_abs"), 1)
            step(ts(g_t, g_t, -1.0, 0.0, ALU.mult, ALU.max))
            dve.wait_ge(S("gla_log"), 1)
            step(tt(g_t, g_t, g_b, ALU.add))
            step(scan(g_b[:, 0, :], chunk_go[:], g_t[:, 0, :], 0.0, ALU.mult, ALU.add))
            scan(g_b[:, 1, :], chunk_go[:], g_t[:, 1, :], 0.0, ALU.mult, ALU.add).then_inc(S("gla_cum"), 1)
            dve.wait_ge(S("gla_exp"), 1)
            for m in range(4):
                copied(dve, ("gq", m))
            step(tt(gq, gq, g_e, ALU.mult))
            step(tt(gk, gk, g_t, ALU.mult))
            dec = st[:, ST_DEC:ST_DEC + 2 * NCH]
            step(cp(dec.rearrange("p (m c) -> p m c", m=2), g_e[:, :, CH - 1::CH]))
            ends = lambda x: x.rearrange("p m (c t) -> p (m c) t", t=CH)
            tt(ends(g_end), ends(gk), over(dec, 2, CH), ALU.mult).then_inc(S("gla_keys"), 1)
            for ri in range(2):
                for q8 in range(2):
                    key = ("D", ri, q8)
                    out_of(key, cp(s5_x[ri][:, q8 * 8:(q8 + 1) * 8, :],
                                   full(dve, key).rearrange("p (q c) -> p q c", q=8)))
            full(dve, ("og", NT - 1))
            step(nc.vector.memset(g_sT, 0.0))
            for i in range(NT):
                out_of(("ke", i), cp(g_endr[:, i, :], full(dve, ("ke", i))[:, 0:GH * GDK]))
            for h in range(GH):
                out_of(("gs", h), nc.vector.copy_predicated(g_sT[:, h, :], gla_mask[:].rearrange("p i n -> p (i n)"),
                                                            full(dve, ("gs", h))))
            for c in range(NCH - 1):
                for pair in range(2):
                    key = ("gd", pair, c % 2)
                    src = full(dve, key)[:, (c // 2) * GDV:(c // 2 + 1) * GDV]
                    if c == 0:
                        ins = cp(g_st[:, pair, 0, :], src)
                    else:
                        ins = stt(g_st[:, pair, c, :], g_st[:, pair, c - 1, :],
                                  dec[:, NCH * pair + c:NCH * pair + c + 1], src, ALU.mult, ALU.add)
                    if c >= NCH - 3:
                        out_of(key, ins)
                        copied(dve, key)
                    else:
                        step(ins)
            for ri in range(2):
                for q8 in range(2):
                    copied(dve, ("D", ri, q8))
            dve.wait_ge(S("turn_in"), 16)
            cos, sin, decay = (s5_turn[:, n] for n in range(3))
            x0, x1, v0, v1 = s5_x[0], s5_x[1], s5_v[0], s5_v[1]
            flat = lambda x: x.rearrange("p q c -> p (q c)")
            step(tt(v0, x0, cos, ALU.mult))
            step(tt(s5_tmp, x1, sin, ALU.mult))
            step(tt(v0, v0, s5_tmp, ALU.add))
            step(tt(v1, x1, cos, ALU.mult))
            step(tt(s5_tmp, x0, sin, ALU.mult))
            step(tt(v1, v1, s5_tmp, ALU.subtract))
            step(scan(flat(x0), flat(decay), flat(v0), 0.0, ALU.mult, ALU.add))
            step(scan(flat(x1), flat(decay), flat(v1), 0.0, ALU.mult, ALU.add))
            step(tt(v0, x0, cos, ALU.mult))
            step(tt(s5_tmp, x1, sin, ALU.mult))
            step(tt(v0, v0, s5_tmp, ALU.subtract))
            step(tt(v1, x0, sin, ALU.mult))
            step(tt(s5_tmp, x1, cos, ALU.mult))
            tt(v1, v1, s5_tmp, ALU.add).then_inc(S("s5_states"), 1)
            for i in range(NT):
                copied(dve, ("og", i))
            og_h = og.rearrange("p i (h d) -> p (i h) d", h=GH)
            step(tt(og_h, og_h, over(gla_g[:], 1, NT * GH), ALU.mult))
            for i in range(NT):
                r = st[:, ST_GR + 4 * i:ST_GR + 4 * i + 4]
                dve.wait_ge(S("gla_root"), i + 1)
                step(nc.vector.reciprocal(r, r))
                if i >= 2:
                    full(dve, ("gt", i - 2))
                for par_ in range(2):
                    bank = ps[:, plan[("go", i, par_)][0], :]
                    for hh in range(2):
                        h = 2 * hh + par_
                        ins = stt(g_row[:, i % 2, h * GDV:(h + 1) * GDV], bank[:, hh * GDV:(hh + 1) * GDV],
                                  r[:, 2 * par_ + hh:2 * par_ + hh + 1], og[:, i, h * GDV:(h + 1) * GDV],
                                  ALU.mult, ALU.mult)
                    out_of(("go", i, par_), ins)
            for m in range(4):
                copied(dve, ("glu", m))
                tt(actT[:, 4 + m, :].rearrange("p (c j) -> p j c", j=SL),
                   yT[:, m, :].rearrange("p (j c) -> p j c", j=SL),
                   sig[:, m % 2, :].rearrange("p (j c) -> p j c", j=SL), ALU.mult).then_inc(S("s5_out"), 1)
            post(3, lambda i, n: ("wo", 2, i, n), post_g[:, 0, :], "x_mix2")
            norm(4, st[:, ST_MOD + KD:ST_MOD + 2 * KD], mod[:, 3 * KD:4 * KD])

            out_of("lg", tt(lg, full(dve, "lg")[:, 0:NT * NE].rearrange("p (i e) -> p i e", i=NT),
                            over(router_b[:], 1, NT), ALU.add))
            copied(dve, "lg")
            for i in range(NT):
                step(nc.vector.max(out=top_v[:, i, :], in_=lg[:, i, :]))
                step(nc.vector.max_index(out=top_i[:, i, :], in_max=top_v[:, i, :], in_values=lg[:, i, :]))
            tt(gate[:], top_v[:, :, 0:TOPK], over(top_v[:, :, 0], 2, TOPK), ALU.subtract).then_inc(S("top_diff"), 1)
            dve.wait_ge(S("slots_cleared"), 32)
            step(cp(top_f, top_i))
            e_f = step_f[:, 0:NE]
            for i in range(NT):
                step(tt(pick[:, i], over(e_f, 1, TOPK), over(top_f[:, i, 0:TOPK], 2, NE), ALU.is_equal))
                nc.vector.tensor_reduce(mask[:, i, :], pick[:, i].rearrange("p k e -> p e k"), AX.X, ALU.add)\
                    .then_inc(S("mask_ready"), 1)
            bank = full(dve, "rk")
            step(cp(rank.rearrange("p i e -> p (i e)"), bank[:, 0:NT * NE]))
            out_of("rk", cp(cnt_e, bank[:, NT * NE:(NT + 1) * NE]))
            copied(dve, "rk")
            step(ts(ov, cnt_e, float(P), None, ALU.is_gt))
            step(stt(ov, cnt_e, float(2 * P), ov, ALU.is_gt, ALU.add))
            step(stt(ov, cnt_e, float(3 * P), ov, ALU.is_gt, ALU.add))
            step(scan(ov_in, ones[:, 0:NE], ov, 0.0, ALU.mult, ALU.add))
            step(tt(base_hi, ov_in, ov, ALU.subtract))
            step(ts(base_hi, base_hi, float(NE - 1), float(P), ALU.add, ALU.mult))
            step(stt(base_d, e_f, float(P), base_hi, ALU.mult, ALU.subtract))
            step(ts(pos, rank, float(P), None, ALU.is_lt))
            step(tt(pos, pos, over(base_d, 1, NT), ALU.mult))
            step(tt(pos, pos, over(base_hi, 1, NT), ALU.add))
            step(tt(pos, pos, rank, ALU.add))
            for i in range(NT):
                step(tt(prod[:, i], pick[:, i], over(pos[:, i, :], 1, TOPK), ALU.mult))
            step(nc.vector.tensor_reduce(posf, prod.rearrange("p i k e -> p (i k) e"), AX.X, ALU.add))
            cp(posi[:], posf).then_inc(S("slots_known"), 1)
            step(tt(le_f[0:1], over(ov_in[0:1], 1, MAX_EXTRA + 1), over(step_f[0:1, 0:MAX_EXTRA + 1], 2, NE), ALU.is_le))
            step(nc.vector.tensor_reduce(blk_f[0:1, 0:MAX_EXTRA + 1], le_f[0:1], AX.X, ALU.add))
            step(ts(blk_f[0:1, 0:MAX_EXTRA + 1], blk_f[0:1, 0:MAX_EXTRA + 1], float(NE - 1), None, ALU.min))
            step(cp(blk_e[0:1, 0:NE], e_f[0:1]))
            step(cp(blk_e[0:1, NE:NE + MAX_EXTRA + 1], blk_f[0:1, 0:MAX_EXTRA + 1]))
            dve.wait_ge(S("top_exp"), 1)
            step(nc.vector.tensor_reduce(gsum, gate[:], AX.X, ALU.add))
            step(nc.vector.reciprocal(gsum, gsum))
            step(tt(gate[:], gate[:], over(gsum, 2, TOPK), ALU.mult))
            cp(blk_e[0:1, 63:64], ov_in[0:1, NE - 1:NE]).then_inc(S("blocks_known"), 1)
            dve.wait_ge(S("blocks_known"), 1)

            n_blocks = NE + dve.value_load(blk_e[0:1, 63:64], min_val=0, max_val=MAX_EXTRA)

            def swiglu(b):
                dve.wait_ge(S("bgu_ready"), b + 1)
                for hf in range(2):
                    half = slice(hf * HALF, (hf + 1) * HALF)
                    dve.wait_ge(S("gu_full"), 4 * b + 2 * hf + 1)
                    tt(sw_t, ps[:, 2 * hf, :], bgu[:, half], ALU.add).then_inc(S("gu_copied"), 1)
                    dve.wait_ge(S("gu_copied"), 4 * b + 2 * hf + 1)
                    ts(sw_g, sw_t, SWI_LIMIT, None, ALU.min).then_inc(S("sw_gate"), 1)
                    dve.wait_ge(S("gu_full"), 4 * b + 2 * hf + 2)
                    tt(sw_u, ps[:, 2 * hf + 1, :], bgu[:, D + hf * HALF:D + (hf + 1) * HALF], ALU.add)\
                        .then_inc(S("gu_copied"), 1)
                    dve.wait_ge(S("gu_copied"), 4 * b + 2 * hf + 2)
                    ts(sw_u, sw_u, SWI_LIMIT, -SWI_LIMIT, ALU.min, ALU.max).then_inc(S("sw_clip"), 1)
                    dve.wait_ge(S("sw_clip"), 2 * b + hf + 1)
                    dve.wait_ge(S("sw_gate"), 2 * b + hf + 1)
                    stt(sw_p, sw_u, 1.0, sw_g, ALU.add, ALU.mult).then_inc(S("sw_up"), 1)
                    dve.wait_ge(S("sw_up"), 2 * b + hf + 1)
                    dve.wait_ge(S("sw_sig"), 2 * b + hf + 1)
                    if not isinstance(b, int):
                        dve.wait_ge(S("hT_full"), b)
                    tt(h_row[:, half], sw_p, sw_s, ALU.mult).then_inc(S("sw_done"), 1)

            def outputs(b):
                dve.wait_ge(S("bdn_ready"), b + 1)
                dve.wait_ge(S("y_stored"), 16 * b + 16)
                for n in range(2):
                    half = slice(n * HALF, (n + 1) * HALF)
                    dve.wait_ge(S("dn_full"), 2 * b + n + 1)
                    tt(y_row[:, half], ps[:, 4 + n, :], bdn[:, half], ALU.add).then_inc(S("y_done"), 1)

            dve.sem_inc(S("y_done"), 1)
            swiglu(0)
            with dve.Fori(1, n_blocks) as b:
                swiglu(b)
                outputs(b - 1)
            outputs(n_blocks - 1)
            for i in range(NT):
                dve.wait_ge(S(f"y_in{i}"), 16 * TOPK)
                step(ts(ff[:, i, :], y_pick[TOPK * i], gate[:, i, 0:1], None, ALU.mult))
                for k in range(1, TOPK):
                    ins = stt(ff[:, i, :], y_pick[TOPK * i + k], gate[:, i, k:k + 1], ff[:, i, :], ALU.mult, ALU.add)
                    if k < TOPK - 1:
                        step(ins)
                ins.then_inc(S("ff_ready"), 1)
            for i in range(NT):
                r = st[:, ST_SS + i:ST_SS + i + 1]
                dve.wait_ge(S("ff_root"), i + 1)
                step(nc.vector.reciprocal(r, r))
                step(stt(ff[:, i, :], ff[:, i, :], r, post_g[:, 1, :], ALU.mult, ALU.mult))
                tt(x_res[:, i, :], x_res[:, i, :], ff[:, i, :], ALU.add).then_inc(S("x_final"), 1)
            dve.wait_ge(S("x_final"), NT)

        @block.tensor
        def _(pe):
            mm = nc.tensor.matmul

            def take(key):
                b, turn_no = plan[key]
                if turn_no:
                    pe.wait_ge(bank_copied[b], turn_no)
                return ps[:, b, :]

            def done(key, ins):
                ins.then_inc(bank_full[plan[key][0]], 1)

            def weights(key, k=KD):
                n = block_no[key]
                pe.wait_ge(S(f"block_in{n % DRING}"), 16 * (n // DRING + 1))
                w = slot(n % DRING)
                return w.rearrange("p (k n) -> p k n", k=k) if key[0] != "s5_glu" else \
                    w[:, 0:4 * HALF].rearrange("p (k n) -> p k n", k=4)

            def transposes(s):
                for i in range(NT):
                    pe.wait_ge(S(f"xn{s}_ready"), i + 1)
                    row = xs[:, i, :] if s == 4 else xn[:, i % 2, :]
                    for h in range(2):
                        key = ("norm", s, i, h)
                        bank = take(key)
                        for k in range(4):
                            ins = nc.tensor.transpose(bank[:, k * P:(k + 1) * P],
                                                      row[:, (4 * h + k) * P:(4 * h + k + 1) * P], ident[:])
                        done(key, ins)

            def normed(s):
                if s in (3, 4):
                    pe.wait_ge(S(f"norm{s}_half"), 2 * NT)
                else:
                    for i in range(NT):
                        for h in range(2):
                            copied(pe, ("norm", s, i, h))

            def by_channel(w, keys):
                for m, key in enumerate(keys):
                    bank = take(key)
                    for k in range(KD):
                        ins = mm(bank, w[:, k, m * P:(m + 1) * P], actT[:, k, :], start=(k == 0), stop=(k == KD - 1))
                    done(key, ins)
                return ins

            def by_token(w, keys):
                for i, key in enumerate(keys):
                    bank = take(key)
                    for k in range(KD):
                        ins = mm(bank, actT[:, k, i * P:(i + 1) * P], w[:, k, :], start=(k == 0), stop=(k == KD - 1))
                    done(key, ins)
                return ins

            pe.wait_ge(S("constants"), 1)
            transposes(1)
            pe.wait_ge(S("silu_c"), 1)
            bank = take("ada")
            for c in range(12):
                w = weights(("ada", c))
                for m in range(4):
                    o = bank[:, 4 * c + m:4 * c + m + 1]
                    for k in range(KD):
                        ins = mm(o, w[:, k, m * P:(m + 1) * P], silu_c[:, k:k + 1], start=(k == 0), stop=(k == KD - 1))
                if c < 11:
                    ins.then_inc(S("ada_used"), 1)
            done("ada", ins)
            pe.wait_ge(S("bx_ready"), 1)
            for n in range(8):
                bank = take(("s5b", n))
                for x in range(4):
                    q, ri = divmod(4 * n + x, 2)
                    src = (bx_r, bx_i)[ri][:, q].rearrange("p j h -> p (j h)")
                    ins = nc.tensor.transpose(bank[:, x * P:(x + 1) * P], src, ident[:])
                done(("s5b", n), ins)
            for par_ in range(2):
                half = slice(SS * par_, SS * (par_ + 1))
                for q4 in range(4):
                    bank = take(("s5k", par_, q4))
                    for x in range(4):
                        q = 4 * q4 + x
                        o = bank[0:SC, x * P:(x + 1) * P]
                        mm(o, bb_r[half, q, :], ca_r[half, q, 0:SL, :].rearrange("p t h -> p (t h)"),
                           start=True, stop=False)
                        ins = mm(o, bb_i[half, q, :], ca_n[half, q, 0:SL, :].rearrange("p t h -> p (t h)"),
                                 start=False, stop=True)
                    done(("s5k", par_, q4), ins)
            normed(1)
            for name, c in (("xr", 3), ("gr", 4), ("q", 0), ("k", 1)):
                by_channel(weights(("w_in", c)), [(name, m) for m in range(4)])
            by_token(weights(("w_in", 2)), [("v", i) for i in range(NT)])
            for m in range(NL):
                pe.wait_ge(S("conv_ready"), m + 1)
                for g in range(2):
                    done(("gate", g, m), mm(take(("gate", g, m)), w_gate[:, g, m, :], xc[:, m, :], start=True, stop=True))
            for m in range(4):
                copied(pe, ("q", m))
                copied(pe, ("k", m))
                copied(pe, ("v", m))

            def scores(i, h):
                half, n = slice(DH * (h % 2), DH * (h % 2 + 1)), (i + 1) * P
                done(("s", i, h), mm(take(("s", i, h))[:, 0:n], qT[half, h // 2, i * P:(i + 1) * P], kT[half, h // 2, 0:n],
                                     start=True, stop=True))

            for i in range(NT):
                scores(i, 0)
                scores(i, 1)
                for h in range(HEADS):
                    if h + 2 < HEADS:
                        scores(i, h + 2)
                    pe.wait_ge(S("att_exp"), HEADS * i + h + 1)
                    bank = take(("pt", i, h))
                    for j in range(i + 1):
                        ins = nc.tensor.transpose(bank[:, j * P:(j + 1) * P], att_s[:, h % 4, j * P:(j + 1) * P], ident[:])
                    done(("pt", i, h), ins)
                    o = take(("o", i)) if h == 0 else ps[:, 7, :]
                    copied(pe, ("pt", i, h))
                    for j in range(i + 1):
                        ins = mm(o[:, h * DH:(h + 1) * DH], att_pt[:, h % 2, j, :], v[:, j, h * DH:(h + 1) * DH],
                                 start=(j == 0), stop=(j == i))
                    if h < HEADS - 1:
                        ins.then_inc(S("att_pv"), 1)
                done(("o", i), ins)
                copied(pe, ("o", i))
                bank = take(("at", i))
                for m in range(4):
                    ins = nc.tensor.transpose(bank[:, m * P:(m + 1) * P], att_row[:, m * P:(m + 1) * P], ident[:])
                done(("at", i), ins)
            for i in range(NT):
                copied(pe, ("at", i))
            pe.wait_ge(S("rec_ready"), NL)
            for c in range(2):
                by_token(weights(("w_out", c)), [("wo", 1, i, c) for i in range(NT)])

            transposes(2)
            normed(2)
            for c in range(8):
                by_channel(weights(("ff_in", c)), [("f1", 4 * c + m) for m in range(4)])
            acc = {}
            for c in range(8):
                w = weights(("ff_out", c), 4)
                for k in range(4):
                    kk = 4 * c + k
                    pe.wait_ge(S("hid_ready"), kk + 1)
                    for i in range(NT):
                        for n in range(2):
                            key = ("f2", i, n)
                            if kk == 0:
                                acc[key] = take(key)
                            ins = mm(acc[key], hidT[:, kk, i * P:(i + 1) * P], w[:, k, n * HALF:(n + 1) * HALF],
                                     start=(kk == 0), stop=(kk == NF - 1))
                            if kk == NF - 1:
                                done(key, ins)
                if c < 7:
                    ins.then_inc(S("ff_out_used"), 1)
            transposes(3)
            for s in range(2):
                pe.wait_ge(S("diag_ready"), s + 1)
                for n in range(2):
                    bank = take(("pg", s, n))
                    for k in range(4):
                        ins = mm(bank[:, k * P:(k + 1) * P], ones[:], diag[:, 4 * n + k, :], start=True, stop=True)
                    done(("pg", s, n), ins)
            normed(3)
            by_channel(weights(("w_in_2", 0)), [("gq", m) for m in range(4)])
            by_channel(weights(("w_in_2", 3)), [("u", m) for m in range(4)])
            bank = take("a16")
            for k in range(KD):
                ins = mm(bank[0:16, :], w_a16[:, k, :], actT[:, k, :], start=(k == 0), stop=(k == KD - 1))
            done("a16", ins)
            copied(pe, "a16")
            for m in range(2):
                done(("za", m), mm(take(("za", m)), w_alpha[:, m * P:(m + 1) * P], a16[0:16, :], start=True, stop=True))
            by_token(weights(("w_in_2", 1)), [("gv", i) for i in range(NT)])
            by_token(weights(("w_in_2", 2)), [("og", i) for i in range(NT)])
            w = weights(("s5", 0), NQ).rearrange("p q (r n) -> p q r n", r=2)
            pe.wait_ge(S("u_in"), 16 * SL)
            for ri in range(2):
                for q8 in range(2):
                    bank = take(("D", ri, q8))
                    for x in range(8):
                        for par_ in range(2):
                            q = 8 * q8 + x
                            half = slice(SS * par_, SS * (par_ + 1))
                            ins = mm(bank[half, x * SNC:(x + 1) * SNC], w[:, q, ri, half], s5_u[:, 2 * q + par_, :],
                                     start=True, stop=True)
                    done(("D", ri, q8), ins)
            pe.wait_ge(S("gla_keys"), 1)
            for i in range(NT):
                bank = take(("ke", i))
                for m in range(2):
                    ins = nc.tensor.transpose(bank[:, m * P:(m + 1) * P], g_end[:, m, i * P:(i + 1) * P], ident[:])
                done(("ke", i), ins)
            for h in range(GH):
                half = slice(GDK * (h % 2), GDK * (h % 2 + 1))
                bank = take(("gs", h))
                for i in range(NT):
                    tile = slice(i * P, (i + 1) * P)
                    ins = mm(bank[:, tile], gk[half, h // 2, tile], gq[half, h // 2, tile], start=True, stop=True)
                done(("gs", h), ins)
            for i in range(NT):
                copied(pe, ("ke", i))
                copied(pe, ("gv", i))
            for pair in range(2):
                for cp_ in range(2):
                    bank = take(("gd", pair, cp_))
                    rows = slice(CH * cp_, CH * (cp_ + 1))
                    for c in range(cp_, NCH - 1, 2):
                        for hh in range(2):
                            h = 2 * pair + hh
                            ins = mm(bank[GDK * hh:GDK * (hh + 1), (c // 2) * GDV:(c // 2 + 1) * GDV],
                                     g_endr[rows, c // 2, h * GDK:(h + 1) * GDK], gv[rows, c // 2, h * GDV:(h + 1) * GDV],
                                     start=True, stop=True)
                    done(("gd", pair, cp_), ins)
            for h in range(GH):
                copied(pe, ("gs", h))
            for pair in range(2):
                for cp_ in range(2):
                    copied(pe, ("gd", pair, cp_))
            for i in range(NT):
                for par_ in range(2):
                    bank = take(("go", i, par_))
                    half = slice(GDK * par_, GDK * (par_ + 1))
                    for hh in range(2):
                        h = 2 * hh + par_
                        o = bank[:, hh * GDV:(hh + 1) * GDV]
                        mm(o, g_sT[:, h, i * P:(i + 1) * P], gv[:, i, h * GDV:(h + 1) * GDV], start=True, stop=True)
                        for x in range(2):
                            c = 2 * i + x
                            if c:
                                ins = mm(o[CH * x:CH * (x + 1), :], gq[half, hh, c * CH:(c + 1) * CH],
                                         g_st[half, hh, c - 1, :], start=False, stop=True, skip_group_check=True)
                    done(("go", i, par_), ins)
            for i in range(NT):
                copied(pe, ("go", i, 0))
                copied(pe, ("go", i, 1))
                bank = take(("gt", i))
                for m in range(4):
                    ins = nc.tensor.transpose(bank[:, m * P:(m + 1) * P], g_row[:, i % 2, m * P:(m + 1) * P], ident[:])
                done(("gt", i), ins)
            wt = weights(("s5", 1), SG)
            wr = weights(("s5", 2), NQ).rearrange("p q (r n) -> p q r n", r=2)
            pe.wait_ge(S("s5_states"), 1)
            for par_ in range(2):
                half = slice(SS * par_, SS * (par_ + 1))
                for q8 in range(2):
                    bank = take(("Y", par_, q8))
                    for x in range(8):
                        q = 8 * q8 + x
                        mm(bank[:, x * SNC:(x + 1) * SNC], wt[:, NQ * par_ + q, :], s5_u[:, 2 * q + par_, :],
                           start=True, stop=False)
                        for ri in range(2):
                            ins = mm(bank[:, x * SNC + 1:(x + 1) * SNC], wr[half, q, ri, :],
                                     s5_v[ri][half, q, 0:SNC - 1], start=False, stop=(ri == 1))
                    done(("Y", par_, q8), ins)
            w = weights(("s5_glu", 0))
            pe.wait_ge(S("y5_gelu"), 4)
            for m in range(4):
                bank = take(("glu", m))
                for k in range(4):
                    ins = mm(bank, w[:, k, m * P:(m + 1) * P], yT[:, k, :], start=(k == 0), stop=(k == 3))
                done(("glu", m), ins)
            for i in range(NT):
                copied(pe, ("gt", i))
            pe.wait_ge(S("s5_out"), 4)
            for c in range(2):
                by_token(weights(("w_out_2", c)), [("wo", 2, i, c) for i in range(NT)])
            transposes(4)
            normed(4)
            bank = take("lg")
            for i in range(NT):
                for k in range(KD):
                    ins = mm(bank[:, i * NE:(i + 1) * NE], actT[:, k, i * P:(i + 1) * P], router_w[:, k, :],
                             start=(k == 0), stop=(k == KD - 1))
            done("lg", ins)
            pe.wait_ge(S("mask_ready"), NT)
            bank = take("rk")
            for i in range(NT + 1):
                for j in range(min(i + 1, NT)):
                    ins = mm(bank[:, i * NE:(i + 1) * NE], before[:] if j == i else ones[:], mask[:, j, :],
                             start=(j == 0), stop=(j == min(i, NT - 1)))
            done("rk", ins)

            copied(pe, "rk")
            pe.wait_ge(S("blocks_known"), 1)
            n_blocks = NE + pe.value_load(blk_e[0:1, 63:64], min_val=0, max_val=MAX_EXTRA)

            def input_in(b):
                pe.wait_ge(S("xg_in"), 16 * b + 16)
                if not (isinstance(b, int) and b < 2):
                    pe.wait_ge(S("hT_ready"), b - 1)
                for k in range(KD):
                    ins = nc.tensor.transpose(ps[:, 6 + k // 4, (k % 4) * P:(k % 4 + 1) * P], xg[:, k * P:(k + 1) * P],
                                              ident[:])
                ins.then_inc(S("xgT_full"), 1)

            def gate_up(b):
                pe.wait_ge(S("xgT_ready"), b + 1)
                for j in range(4):
                    pe.wait_ge(S(f"part_in{j}"), 16 * b + 16)
                    if not isinstance(b, int):
                        pe.wait_ge(S("gu_copied"), 4 * b + j - 3)
                    w = slot(j).rearrange("p (k n) -> p k n", k=KD)
                    for k in range(KD):
                        ins = mm(ps[:, j, :], xgT[:, k, :], w[:, k, :], start=(k == 0), stop=(k == KD - 1))
                    ins.then_inc(S("gu_full"), 1)

            def down(b):
                pe.wait_ge(S("hT_ready"), b + 1)
                pe.wait_ge(S("y_done"), 2 * b + 1)
                for n in range(2):
                    pe.wait_ge(S(f"part_in{4 + n}"), 16 * b + 16)
                    w = slot(4 + n).rearrange("p (k n) -> p k n", k=KD)
                    for k in range(KD):
                        ins = mm(ps[:, 4 + n, :], hT[:, k, :], w[:, k, :], start=(k == 0), stop=(k == KD - 1))
                    ins.then_inc(S("dn_full"), 1)

            def hidden_in(b):
                pe.wait_ge(S("sw_done"), 2 * b + 2)
                pe.wait_ge(S("xgT_ready"), b + 2)
                for k in range(KD):
                    ins = nc.tensor.transpose(ps[:, 6 + k // 4, (k % 4) * P:(k % 4 + 1) * P], h_row[:, k * P:(k + 1) * P],
                                              ident[:])
                ins.then_inc(S("hT_full"), 1)

            input_in(0)
            gate_up(0)
            input_in(1)
            hidden_in(0)
            with pe.Fori(1, n_blocks) as b:
                gate_up(b)
                input_in(b + 1)
                down(b - 1)
                hidden_in(b)
            down(n_blocks - 1)



_LARGE = ["x", "mix_norm_post", "mlp_norm_post", "w_in", "w_out", "w_ff_in", "w_ff_out", "ada_w_2", "w_in_2",
          "w_alpha_2", "gla_norm_g_2", "s5_glu_w_2", "w_out_2", "router_w_2", "router_b_2", "exp_w_gu_2",
          "exp_b_gu_2", "exp_w_down_2", "exp_b_down_2"]


def laid_out(inputs):
    arrays = {name: np.ascontiguousarray(inputs[name]) for name in _LARGE}
    arrays["cols"] = np.ascontiguousarray(
        np.concatenate([np.asarray(inputs[name]).reshape(n, P) for name, n in VECS]).T)

    def states(x):
        x = np.asarray(x).reshape(NQ, 2 * SS, -1)
        return np.ascontiguousarray(x.transpose(1, 0, 2))

    step = np.broadcast_to(np.asarray(inputs["s5_log_dt_2"]).reshape(SG, 1), (SG, SS))
    arrays["s5_par"] = np.ascontiguousarray(np.concatenate(
        [states(x) for x in (step, inputs["s5_lambda_re_2"], inputs["s5_lambda_im_2"])], axis=2).transpose(0, 2, 1))
    for name in ("s5_b_re", "s5_b_im"):
        arrays[name] = states(inputs[name + "_2"])
    for name in ("s5_c_re", "s5_c_im"):
        arrays[name] = states(np.asarray(inputs[name + "_2"])[0].transpose(0, 2, 1))
    arrays["s5_d"] = np.ascontiguousarray(np.asarray(inputs["s5_d_2"]).reshape(NQ, 2, SC).transpose(2, 1, 0))
    for name in ("w_rgate", "w_igate"):
        w = np.asarray(inputs[name])[0]
        n = w.shape[1]
        two = np.zeros((P, NL, P), w.dtype)
        for g in range(2):
            two[g * n:(g + 1) * n, :, g * n:(g + 1) * n] = w[g::2].transpose(1, 0, 2)
        arrays[name] = two
    return arrays


def kernel(**inputs):
    import concourse.bacc as bacc
    from concourse.bass_utils import run_bass_kernel_spmd

    nc = bacc.Bacc("TRN2", target_bir_lowering=False, num_devices=1)
    arrays = {f"in_{name}": x for name, x in laid_out(inputs).items()}
    handles = {name[3:]: nc.dram_tensor(name, x.shape, mybir.dt.from_np(x.dtype), kind="ExternalInput").ap()
               for name, x in arrays.items()}
    out = nc.dram_tensor("out", (1, T, D), F32, kind="ExternalOutput").ap()
    program(nc, handles, out)
    result = run_bass_kernel_spmd(nc, [arrays], core_ids=[0])
    return result.results[0]["out"]
```

```python
import math
from contextlib import ExitStack

import numpy as np

import concourse.bass as bass
from concourse import mybir

F32 = mybir.dt.float32
F32R = mybir.dt.float32r
I32 = mybir.dt.int32
U32 = mybir.dt.uint32
ALU = mybir.AluOpType
ACT = mybir.ActivationFunctionType
AX = mybir.AxisListType

P = 128
T = 512
NT = T // P
D = 1024
KD = D // P
EPS = 1e-6
HALF = 512
FF = 4 * D
NF = FF // P
HEADS, DH = 8, 64
NEG = -1.0e30
LRU_C = 8.0
CONV = 4
NL = 4
GH, GDK, GDV, CH = 4, 64, 128, 64
NCH = T // CH
TAU = 16.0
SG, SC, SS = 32, 16, 64
NQ = SG // 2
SL = 8
SNC = T // SL
NPOW = SL + 1
TWO_PI = 2.0 * math.pi
PI_A = 6.28125
PI_B = 0.0019350051879882812
PI_C = TWO_PI - PI_A - PI_B
ROUND = 12582912.0
PI_MAX = 3.1415925
NE, TOPK = 32, 4
SWI_ALPHA, SWI_LIMIT = 1.702, 7.0
MAX_EXTRA = (T * TOPK - 1) // P
MAX_BLOCKS = NE + MAX_EXTRA
SLOTS = (MAX_BLOCKS + 1) * P
RING = 6
BLK = KD * HALF
PIECE = BLK // 2
NG = PIECE // HALF
SCR = 21760
NADA = 6 * D // HALF

VECS = [("mix_norm_pre", 8), ("mlp_norm_pre", 8), ("mix_pre_g_2", 8), ("ffn_pre_g_2", 8),
        ("mix_post_g_2", 8), ("ffn_post_g_2", 8), ("conv_w", 16), ("conv_b", 4), ("b_rgate", 4),
        ("b_igate", 4), ("lru_lambda", 4), ("b_alpha_2", 2), ("s5_glu_b_2", 4), ("c_2", 8),
        ("ada_b_2", 48)]
NVEC = sum(n for _, n in VECS)
COL = {}
for _i, (_name, _n) in enumerate(VECS):
    COL[_name] = (sum(n for _, n in VECS[:_i]), _n)

N_SMALL = 16
N_S5 = 4 + 1 + 2 * SL

ST_SS, ST_R, ST_PS, ST_DEN, ST_MX = 0, 4, 8, 16, 32
ST_LAM, ST_MOD, ST_PG, ST_GR, ST_DEC = 64, 96, 112, 128, 160
ST_RDEN = 176
ST_N = 192


def bank_plan():
    turns, plan, count = [0] * 8, {}, [0]

    def give(key, bank=None):
        if bank is None:
            bank, count[0] = count[0] % 8, count[0] + 1
        plan[key] = (bank, turns[bank])
        turns[bank] += 1

    def norm(s):
        for i in range(NT):
            for h in range(2):
                give(("norm", s, i, h), 2 * i + h)

    def rows(*key):
        for i in range(NT):
            for n in range(2):
                give((*key, i, n), 2 * i + n)

    norm(1)
    for c in range(NADA):
        if c % 4 == 0:
            give(("ada", c // 4), c // 4)
    for j in range(4):
        give(("mod", j), 4 + j)
    keys = [("s5b", n) for n in range(8)]
    keys += [("s5k", par, q4) for par in range(2) for q4 in range(4)]
    keys += [(w, m) for w in ("xr", "gr", "q", "k", "v") for m in range(4)]
    keys += [("gate", g, m) for m in range(NL) for g in range(2)]
    for key in keys:
        give(key)
    for i in range(NT):
        give(("o", i), 7)
        for h in range(HEADS):
            give(("s", i, h), h % 4)
            give(("pt", i, h), 4 + h % 2)
        give(("at", i), 6)
    rows("wo", 1)
    norm(2)
    for m in range(NF):
        give(("f1", m), m % 8)
    rows("f2")
    norm(3)
    count[0] = 0
    keys = [("pg", s, n) for s in range(2) for n in range(2)]
    keys += [("gq", m) for m in range(4)] + [("u", m) for m in range(4)] + ["a16"]
    keys += [("za", m) for m in range(2)] + [("gv", i) for i in range(NT)] + [("og", i) for i in range(NT)]
    keys += [("D", ri, q8) for q8 in range(2) for ri in range(2)]
    keys += [("ke", i) for i in range(NT)] + [("gs", h) for h in range(GH)]
    keys += [("gd", pair, cp) for pair in range(2) for cp in range(2)]
    keys += [("Y", par, q8) for q8 in range(2) for par in range(2)]
    keys += [("go", i, par) for i in range(NT) for par in range(2)] + [("gt", i) for i in range(NT)]
    keys += [("glu", m) for m in range(4)]
    for key in keys:
        give(key)
    rows("wo", 2)
    norm(4)
    for key in ("lg", "rk"):
        give(key)
    return plan


def weight_plan():
    def columns(name, c, last):
        return [(name, c, 0, None), (name, c, 1, last)]

    def rows(name, n, last):
        return [(name, c, h, last if c == n - 1 else None) for c in range(n) for h in range(2)]

    plan = []
    for c in (3, 4, 0, 1, 2):
        plan += columns("w_in", c, (("q", "k", "v", "xr", "gr")[c], 3))
    plan += rows("w_out", 2, ("wo", 1, NT - 1, 1))
    for c in range(8):
        plan += columns("ff_in", c, ("f1", 4 * c + 3))
    plan += rows("ff_out", 8, ("f2", NT - 1, 1))
    for c in (0, 3, 1, 2):
        plan += columns("w_in_2", c, (("gq", "gv", "og", "u")[c], 3))
    return plan + rows("w_out_2", 2, ("wo", 2, NT - 1, 1))


def program(nc, a, out):
    plan = bank_plan()
    pieces = weight_plan()
    piece_no = {piece[:3]: n for n, piece in enumerate(pieces)}
    after_s5 = piece_no["w_out_2", 0, 0]

    with ExitStack() as ctx:
        def sb(name, shape, dt=F32):
            return ctx.enter_context(nc.sbuf_tensor(name, shape, dt))

        with ExitStack() as rounded:
            def fr(name, shape):
                return rounded.enter_context(nc.sbuf_tensor(name, shape, F32))

            split = fr("split", [P, 4 * PIECE])
            actT = fr("actT", [P, KD, T])
            actL = fr("actL", [P, KD, T])

        def scratch(name, shape, dt=F32):
            return nc.dram_tensor(name, shape, dt, kind="Internal").ap()

        sems = {}

        def S(name):
            if name not in sems:
                sems[name] = ctx.enter_context(nc.semaphore(name))
            return sems[name]

        inject_dram = scratch("s5_inject", (P, BLK))
        s5_dram = [scratch(f"s5_response{q8}", (P, BLK)) for q8 in range(2)]
        turn_dram = scratch("s5_turn", (P, 3 * NQ * SNC))
        u_dram = scratch("u_dram", (T, T))
        y_dram = scratch("y_dram", (T, T))
        xs_dram = scratch("xs_dram", (T, D))
        slot_token = scratch("slot_token", (SLOTS, 1), I32)
        y_slots = scratch("y_slots", (SLOTS, D))

        plain = sb("plain", [P, 4 * PIECE + 2 * KD * T])
        plain_actT = plain[:, 4 * PIECE:4 * PIECE + KD * T].rearrange("p (k t) -> p k t", k=KD)
        ring = sb("ring", [P, 2 * PIECE])
        x_res = sb("x_res", [P, NT, D])
        scr = sb("scr", [P, SCR])
        ident = sb("ident", [P, P])
        ones = sb("ones", [P, P])
        masks = sb("masks", [P, 2, T])
        att_bias = masks[:, 0].rearrange("p (i n) -> p i n", i=NT)
        gla_mask = masks[:, 1].rearrange("p (i n) -> p i n", i=NT).bitcast(I32)
        zero = sb("zero", [P, 256])
        step_f = sb("step_f", [P, SNC])
        chunk_go = sb("chunk_go", [P, T])
        before = sb("before", [P, P])
        cols = sb("cols", [P, NVEC])
        silu_c = sb("silu_c", [P, KD])
        post_g = sb("post_g", [P, 2, D])
        st = sb("st", [P, ST_N])
        eps = sb("eps", [P, 1])
        w_a16 = sb("w_a16", [P, KD, 16])
        w_alpha = sb("w_alpha", [16, GH * GDK])
        w_gate = sb("w_gate", [P, 2, NL, P])
        gla_g = sb("gla_g", [P, GDV])
        router_w = sb("router_w", [P, KD, NE])
        router_b = sb("router_b", [P, NE])
        tok_id = sb("tok_id", [P, NT], I32)

        def view(at, *shape, of=scr):
            ap = of[:, at:at + math.prod(shape)]
            if len(shape) == 1:
                return ap
            names = "abcd"[:len(shape)]
            return ap.rearrange(f"p ({' '.join(names)}) -> p {' '.join(names)}",
                                **dict(zip(names, shape)))

        def col(name, k=0, n=1):
            return cols[:, COL[name][0] + k:COL[name][0] + k + n]

        def over(ap, axis, n):
            ap = ap.unsqueeze(axis)
            shape = list(ap.shape)
            shape[axis] = n
            return ap.broadcast_to(shape)

        def slot(s):
            return ring[:] if s == 0 else scr[:, (s - 1) * BLK:s * BLK]

        def piece(s):
            return ring[:, s * PIECE:(s + 1) * PIECE] if s < 2 else scr[:, 17664 + (s - 2) * PIECE:17664 + (s - 1) * PIECE]

        def part(n, low):
            at = (2 * (n % 2) + low) * PIECE
            return split[:, at:at + PIECE]

        def r32(ap):
            return ap.bitcast(F32R)

        xn, junk, post_tmp = view(0, 2, D), view(2048, D), view(3072, 2, HALF)
        mask_f, dist = view(11264, NT, P), view(11776, NT, P).bitcast(I32)
        dist_i, cnt, cnt_t = view(12288, NT, P).bitcast(I32), view(12800, NT, P), view(13568, NT, P)
        par = view(3072, 3, NQ)
        b_r, b_i, c_r, c_i = (view(3120 + 256 * n, NQ, SC) for n in range(4))
        bb_r, bb_i, bb_t = (view(4144 + 256 * n, NQ, SC) for n in range(3))
        pw_l, pw_th, pw_k, pw_t, pw_r, pw_i = (view(4912 + 272 * n, NPOW, NQ) for n in range(6))
        s5_s = view(6544 - 0, 7, NQ)
        ca_r, ca_n, ca_t = view(6656, NQ, NPOW, SC), view(8960, NQ, NPOW, SC), view(11264, NQ, NPOW, SC)
        bx_r, bx_i = view(13568, NQ, SL, SC), view(15616, NQ, SL, SC)
        inject = view(17664, NQ, 2, P)
        taps = view(13568, 2, 2, NQ // 2, P)
        turn = view(0, 3, NQ, SNC, of=plain)
        mod_row = view(3 * NQ * SNC, NADA // 4, HALF, of=plain)
        ang, ang_k, ang_r = (view(13568 + 1024 * n, NQ, SNC) for n in range(3))
        step_i = view(14080, SNC).bitcast(I32)
        s5_d = sb("s5_d", [SC, SG])
        att_s, att_pt, att_row = view(0, 4, T), view(2048, 2, NT, P), view(3072, T)
        qT, kT, v = view(4096, 4, T), view(6144, 4, T), view(8192, NT, T)
        xr, gr, xc = view(10240, NL, T), view(12288, NL, T), view(14336, NL, T)
        lru_a, lru_u = view(16384, NL, T), view(18432, NL, T)
        hidT = view(4096, NF, T)
        hid_h, hid_l = actT[:, 0:4, :], actT[:, 4:8, :]
        diag = view(20480, KD, P)
        gq, gk, g_t, g_b, g_e = (view(4096 + 1024 * n, 2, T) for n in range(5))
        g_end, g_endr, g_row = g_b, view(8192, NT, GH * GDK), view(6144, 2, T)
        gv, og = view(9216, NT, T), view(11264, NT, T)
        g_st = view(13312, 2, NCH - 1, GDV)
        a16 = view(15360, T)
        g_sT = plain_actT[:, 0:4, :]
        uT = view(17920, 4, T)
        s5_u = view(15872, SG, SNC)
        s5_x = [view(17920 + 1024 * ri, NQ, SNC) for ri in range(2)]
        s5_v = [plain_actT[:, 4 + 2 * ri:6 + 2 * ri, :].rearrange("p a (b c) -> p (a b) c", c=SNC) for ri in range(2)]
        s5_turn = view(0, 3, NQ, SNC)
        s5_tmp = view(19968, NQ, SNC)
        s5_y = view(17920, SG, SNC)
        yT = view(15872, 4, T)
        sig = view(19968, 2, T)
        xs = view(8192, NT, D)
        y4 = view(12288, D)
        junk4 = view(20480, D)
        lg, mask = view(0, NT, NE, of=plain), view(128, NT, NE, of=plain)
        pick, prod = view(256, NT, TOPK, NE, of=plain), view(768, NT, TOPK, NE, of=plain)
        rank, pos = view(1280, NT, NE, of=plain), view(1408, NT, NE, of=plain)
        cnt_e, ov, ov_in, base_hi, base_d = (view(1536 + 32 * n, NE, of=plain) for n in range(5))
        le_f = view(1728, MAX_EXTRA + 1, NE, of=plain)
        top_v, top_f = view(2240, NT, 8, of=plain), view(2304, NT, 8, of=plain)
        top_i = view(2272, NT, 8, of=plain).bitcast(U32)
        gsum, posf, blk_f = view(2336, NT, of=plain), view(2344, NT * TOPK, of=plain), view(2360, NE, of=plain)
        gate = sb("gate", [P, NT, TOPK])
        posi = sb("posi", [P, NT * TOPK], I32)
        blk_e = sb("blk_e", [1, 64], I32)
        bgu, bdn, y_row = view(0, 2 * D, of=plain), view(2 * D, D, of=plain), view(3 * D, D, of=plain)
        sw_t, sw_g, sw_s, sw_u, sw_p = (view(4 * D + HALF * n, HALF, of=plain) for n in range(5))
        bg_row, bu_row = view(20480, D), w_gate[:].rearrange("p a b c -> p (a b c)")
        bdn_row = masks[:].rearrange("p a b -> p (a b)")
        slot_idx = sb("slot_idx", [P, 1], I32)
        xg = post_g[:, 0, :]
        xgT = plain_actT[:, 2:4, :].rearrange("p a (k s) -> p (a k) s", s=P)
        h_row = plain_actT[:, 4:6, :].rearrange("p a b -> p (a b)")
        hT = plain_actT[:, 6:8, :].rearrange("p a (k s) -> p (a k) s", s=P)
        y_pick = [view(n * D, D) for n in range(NT * TOPK)]
        ff = view(NT * TOPK * D, NT, D)

        ps = ctx.enter_context(nc.psum_tensor("ps", [P, 8, HALF], F32))
        bank_full = [S(f"bank_full{b}") for b in range(8)]
        bank_copied = [S(f"bank_copied{b}") for b in range(8)]

        def full(eng, key):
            b, turn_no = plan[key]
            eng.wait_ge(bank_full[b], turn_no + 1)
            return ps[:, b, :]

        def copied(eng, key):
            b, turn_no = plan[key]
            eng.wait_ge(bank_copied[b], turn_no + 1)

        def out_of(key, ins):
            ins.then_inc(bank_copied[plan[key][0]], 1)

        def lam(n):
            return st[:, ST_LAM + NL * n:ST_LAM + NL * (n + 1)]

        def stepper(eng, name):
            n = [0]

            def step(ins):
                n[0] += 1
                ins.then_inc(S(name), 1)
                eng.wait_ge(S(name), n[0])
            return step

        def used_count(n):
            return sum(last is None for *_, last in pieces[:n + 1])

        block = ctx.enter_context(nc.Block())

        @block.sync
        def _(sp):
            for i in range(NT):
                sp.dma_start(x_res[:, i, :], a["x"][0, i * P:(i + 1) * P, :]).then_inc(S(f"x_in{i}"), 16)
            sp.wait_ge(S("small_in"), 16 * N_SMALL)

            def ada_free(n):
                if n % 8 == 7:
                    full(sp, ("ada", n // 8))
                else:
                    sp.wait_ge(S("ada_used"), n - n // 8 + 1)

            for n in range(2 * NADA):
                if n >= 4:
                    ada_free(n - 4)
                c, h = divmod(n, 2)
                src = a["ada_w_2"][0, h * NG * P:(h + 1) * NG * P, c * HALF:(c + 1) * HALF]
                sp.dma_start(piece(n % 4).rearrange("p (k n) -> p k n", k=NG), src.rearrange("(k p) n -> p k n", p=P))\
                    .then_inc(S(f"ada_in{n % 4}"), 16)

            def load_piece(n):
                name, c, h, _ = pieces[n]
                if name in ("w_out", "ff_out", "w_out_2"):
                    w, row = a["w_ff_out" if name == "ff_out" else name], (2 * c + h) * 2 * P
                    src = w[0, row:row + 2 * P, :]
                else:
                    w, at = a["w_ff_in" if name == "ff_in" else name], c * HALF
                    if (name, c) == ("w_in_2", 3):
                        at += 16
                    src = w[0, h * NG * P:(h + 1) * NG * P, at:at + HALF]
                src = src.rearrange("(k p) n -> p k n", p=P)
                sp.dma_start(piece(n % 2).rearrange("p (k n) -> p k n", k=src.shape[1]), src)\
                    .then_inc(S(f"piece_in{n % 2}"), 16)

            for n in range(after_s5):
                if n < 2:
                    ada_free(2 * NADA - 4 + n)
                else:
                    sp.wait_ge(S("split_ready"), n - 1)
                load_piece(n)
            sp.wait_ge(S("s5_const"), 16 * N_S5)
            for q8 in range(2):
                sp.wait_ge(S("split_ready"), after_s5 - 1 + q8)
                sp.dma_start(piece(q8), inject_dram[:, q8 * PIECE:(q8 + 1) * PIECE]).then_inc(S(f"inject_in{q8}"), 16)
            for q8 in range(2):
                full(sp, ("Y", 1, 0) if q8 else ("D", 1, 1))
                sp.dma_start(ring[:], s5_dram[q8]).then_inc(S("s5_in"), 16)
            full(sp, ("Y", 1, 1))
            sp.dma_start(piece(1).rearrange("p (k n) -> p k n", k=NG),
                         a["s5_glu_w_2"][0].rearrange("(k p) n -> p k n", p=P)).then_inc(S("glu_in"), 16)
            assert after_s5 % 2 == 0
            load_piece(after_s5)
            sp.wait_ge(S("y5_stored"), 16 * SL)
            sp.dma_start(yT, y_dram.rearrange("(m p) n -> p m n", p=P)).then_inc(S("y5_in"), 16)
            full(sp, ("glu", 3))
            load_piece(after_s5 + 1)
            for n in range(after_s5 + 2, len(pieces)):
                sp.wait_ge(S("split_ready"), n - 1)
                load_piece(n)

            def expert_blocks(e, b, js):
                for j in js:
                    if not (isinstance(b, int) and b == 0):
                        if j < 4:
                            sp.wait_ge(S("gu_full"), 4 * b + j - 3)
                        else:
                            sp.wait_ge(S("dn_full"), 2 * b + j - 5)
                    w = a["exp_w_gu_2"] if j < 4 else a["exp_w_down_2"]
                    at = (j % 2) * D + (j // 2) * HALF if j < 4 else (j - 4) * HALF
                    src = w[0, bass.ds(e, 1), :, at:at + HALF].rearrange("o (k p) n -> p (o k) n", p=P)
                    sp.dma_start(slot(j).rearrange("p (k n) -> p k n", k=KD), src).then_inc(S(f"part_in{j}"), 16)

            sp.wait_ge(S("split_ready"), len(pieces))
            sp.wait_ge(S("x_mix2"), NT)
            expert_blocks(0, 0, range(3))
            full(sp, "lg")
            sp.wait_ge(S("xs_stored"), 16 * NT)
            expert_blocks(0, 0, range(3, RING))
            sp.wait_ge(S("blocks_known"), 1)
            n_blocks = NE + sp.value_load(blk_e[0:1, 63:64], min_val=0, max_val=MAX_EXTRA)
            expert_blocks(1, 1, range(4))
            with sp.Fori(1, n_blocks - 1) as b:
                e = sp.value_load(blk_e[0:1, bass.ds(b, 1)], min_val=0, max_val=NE - 1)
                e_next = sp.value_load(blk_e[0:1, bass.ds(b + 1, 1)], min_val=0, max_val=NE - 1)
                expert_blocks(e_next, b + 1, range(4))
                expert_blocks(e, b, range(4, RING))
            expert_blocks(sp.value_load(blk_e[0:1, bass.ds(n_blocks - 1, 1)], min_val=0, max_val=NE - 1), n_blocks - 1,
                          range(4, RING))
            for i in range(NT):
                sp.wait_ge(S("x_final"), i + 1)
                sp.dma_start(out[0, i * P:(i + 1) * P, :], x_res[:, i, :]).then_inc(S("out_stored"), 16)
            sp.wait_ge(S("out_stored"), 16 * NT)

        @block.gpsimd
        def _(pool):
            step = stepper(pool, "pool_step")
            step(nc.gpsimd.memset(ident[:], 0.0))
            step(nc.gpsimd.affine_select(out=ident[:], in_=ident[:], compare_op=ALU.not_equal, fill=1.0,
                                         base=0, pattern=[[-1, P]], channel_multiplier=1))
            step(nc.gpsimd.memset(ones[:], 1.0))
            step(nc.gpsimd.memset(before[:], 1.0))
            step(nc.gpsimd.affine_select(out=before[:], in_=before[:], compare_op=ALU.is_gt, fill=0.0,
                                         base=0, pattern=[[1, P]], channel_multiplier=-1))
            step(nc.gpsimd.memset(eps[:], EPS))
            step(nc.gpsimd.memset(mask_f, 1.0))
            step(nc.gpsimd.affine_select(out=mask_f, in_=mask_f, compare_op=ALU.is_ge, fill=0.0,
                                         base=0, pattern=[[0, NT], [1, P]], channel_multiplier=-1))
            step(nc.gpsimd.memset(mask_f[0:CH, :, CH:P], 0.0))
            step(nc.gpsimd.iota(dist, pattern=[[-P, NT], [-1, P]], base=(NT - 1) * P, channel_multiplier=1))
            step(nc.gpsimd.iota(step_i, pattern=[[1, SNC]], base=0, channel_multiplier=0))
            step(nc.gpsimd.iota(tok_id[:], pattern=[[P, NT]], base=0, channel_multiplier=1))
            step(nc.gpsimd.memset(zero[:], 0.0))
            step(nc.gpsimd.memset(chunk_go[:], 1.0))
            nc.gpsimd.memset(chunk_go[:, ::CH], 0.0).then_inc(S("constants"), 1)

            def split_piece(n):
                pool.wait_ge(S(f"piece_in{n % 2}"), 16 * (n // 2 + 1))
                if n >= 2:
                    last = pieces[n - 2][3]
                    if last:
                        full(pool, last)
                    else:
                        pool.wait_ge(S("split_used"), used_count(n - 2))
                three = lambda ap: ap.rearrange("p (a b) -> p a b", b=P)
                nc.gpsimd.tensor_tensor(three(r32(part(n, 0))), three(piece(n % 2)), over(ones[:], 1, PIECE // P), ALU.mult)\
                    .then_inc(S("split_high"), 1)
                pool.wait_ge(S("split_high"), n + 1)
                nc.gpsimd.tensor_tensor(r32(part(n, 1)), piece(n % 2), part(n, 0), ALU.subtract)\
                    .then_inc(S("split_ready"), 1)

            pool.wait_ge(S("constants"), 1)
            pool.wait_ge(S("turn_stored"), 16)
            for j in range(4):
                full(pool, ("mod", j))
            for n in range(len(pieces)):
                split_piece(n)
                if n == piece_no["w_in", 2, 1]:
                    pool.dma_start(slot_token.rearrange("(b s) o -> b (s o)", s=P),
                                   zero[0:MAX_BLOCKS + 1, 0:P].bitcast(I32)).then_inc(S("slots_cleared"), 16)
                    pool.dma_start(y_slots[NE * P:, :].rearrange("(s b) (h d) -> s (b h) d", s=P, h=4),
                                   over(zero[:], 1, 4 * (SLOTS // P - NE))).then_inc(S("slots_cleared"), 16)
            pool.wait_ge(S("slots_cleared"), 32)
            pool.wait_ge(S("slots_known"), 1)
            for n in range(NT * TOPK):
                pool.indirect_dma_start(slot_token[:, :], bass.IndirectOffsetOnAxis(posi[:, n:n + 1], 0),
                                        tok_id[:, n // TOPK:n // TOPK + 1], None).then_inc(S("slots_filled"), 16)
            pool.wait_ge(S("slots_filled"), 16 * NT * TOPK)
            pool.wait_ge(S("xs_stored"), 16 * NT)
            pool.wait_ge(S("blocks_known"), 1)

            def gather(b):
                pool.dma_start(slot_idx[:], slot_token[bass.ds(b * P, P), :]).then_inc(S("idx_in"), 16)
                pool.wait_ge(S("idx_in"), 16 * b + 16)
                if not isinstance(b, int):
                    pool.wait_ge(S("xgT_full"), b)
                pool.sem_inc(S("gather_clear"), 1)
                pool.indirect_dma_start(xg, None, xs_dram[:, :], bass.IndirectOffsetOnAxis(slot_idx[:, 0:1], 0))\
                    .then_inc(S("xg_in"), 16)
                pool.wait_ge(S("xg_in"), 16 * b + 16)

            def gate_bias(e, b):
                pool.dma_start(bg_row[0:1, :], a["exp_b_gu_2"][0, bass.ds(e, 1), 0:D]).then_inc(S("bgu_in"), 16)
                pool.dma_start(bu_row[0:1, :], a["exp_b_gu_2"][0, bass.ds(e, 1), D:2 * D]).then_inc(S("bgu_in"), 16)
                pool.wait_ge(S("bgu_in"), 32 * b + 32)
                if not isinstance(b, int):
                    pool.wait_ge(S("gu_copied"), 4 * b)
                pool.sem_inc(S("gate_bias_clear"), 1)
                nc.gpsimd.partition_broadcast(bgu[:, 0:D], bg_row[0:1, :], P).then_inc(S("bgu_ready"), 1)
                nc.gpsimd.partition_broadcast(bgu[:, D:], bu_row[0:1, :], P).then_inc(S("bgu_ready"), 1)
                pool.wait_ge(S("bgu_ready"), 2 * b + 2)

            def down_bias(e, b):
                pool.dma_start(bdn_row[0:1, :], a["exp_b_down_2"][0, bass.ds(e, 1), :]).then_inc(S("bdn_in"), 16)
                pool.wait_ge(S("bdn_in"), 16 * b + 16)
                pool.wait_ge(S("y_done"), 2 * b + 1)
                pool.sem_inc(S("down_bias_clear"), 1)
                nc.gpsimd.partition_broadcast(bdn, bdn_row[0:1, :], P).then_inc(S("bdn_ready"), 1)
                pool.wait_ge(S("bdn_ready"), b + 1)

            n_blocks = NE + pool.value_load(blk_e[0:1, 63:64], min_val=0, max_val=MAX_EXTRA)

            def expert(b):
                return pool.value_load(blk_e[0:1, bass.ds(b, 1)], min_val=0, max_val=NE - 1)

            gather(0)
            gate_bias(0, 0)
            with pool.Fori(1, n_blocks) as b:
                gather(b)
                gate_bias(expert(b), b)
                down_bias(expert(b - 1), b - 1)
            gather(n_blocks)
            down_bias(expert(n_blocks - 1), n_blocks - 1)
            pool.wait_ge(S("y_stored"), 16 * n_blocks + 16)
            pool.sem_inc(S("pick_clear"), 1)
            for n in range(NT * TOPK):
                pool.indirect_dma_start(y_pick[n], None, y_slots[:, :],
                                        bass.IndirectOffsetOnAxis(posi[:, n:n + 1], 0)).then_inc(S(f"y_in{n // TOPK}"), 16)
            for i in range(NT):
                pool.wait_ge(S(f"y_in{i}"), 16 * TOPK)

        @block.scalar
        def _(act):
            step = stepper(act, "act_step")
            af = nc.scalar.activation
            small = [(cols[:], a["cols"]), (par, a["s5_par"]), (b_r, a["s5_b_re"]), (b_i, a["s5_b_im"]),
                     (c_r, a["s5_c_re"]), (c_i, a["s5_c_im"]), (s5_d[:], a["s5_d"]), (w_gate[:, 0], a["w_rgate"]),
                     (w_gate[:, 1], a["w_igate"]), (w_alpha[:], a["w_alpha_2"][0]),
                     (gla_g[:], a["gla_norm_g_2"][0].partition_broadcast(P)),
                     (router_w[:], a["router_w_2"][0].rearrange("(k p) n -> p k n", p=P)),
                     (router_b[:], a["router_b_2"][0].partition_broadcast(P)),
                     (post_g[:, 0, :], a["mix_norm_post"][0].partition_broadcast(P)),
                     (post_g[:, 1, :], a["mlp_norm_post"][0].partition_broadcast(P)),
                     (w_a16[:], a["w_in_2"][0, :, 1536:1552].rearrange("(k p) n -> p k n", p=P))]
            assert len(small) == N_SMALL
            for dst, src in small:
                act.dma_start(dst, src).then_inc(S("small_in"), 16)

            def squares(s, i, dst, *ready):
                act.wait_ge(*ready)
                if i:
                    act.wait_ge(S("norm_sum"), NT * (s - 1) + i)
                r = st[:, ST_SS + i:ST_SS + i + 1]
                af(dst, x_res[:, i, :], ACT.Square, accum_out=r).then_inc(S("norm_sum"), 1)
                act.wait_ge(S("norm_sum"), NT * (s - 1) + i + 1)
                af(r, r, ACT.Sqrt, scale=1.0 / D, bias=eps[:, 0:1]).then_inc(S("norm_root"), 1)

            def norm_rows(s, i):
                act.wait_ge(S("norm_inv"), NT * (s - 1) + i + 1)
                dst = xs[:, i, :] if s == 4 else xn[:, i % 2, :]
                if s < 4 and i >= 2:
                    act.wait_ge(S("norm_low"), NT * (s - 1) + i - 1)
                af(dst, x_res[:, i, :], ACT.Copy, scale=st[:, ST_SS + i:ST_SS + i + 1]).then_inc(S("xn_ready"), 1)

            def norm_high(s, i):
                y = (y4 if s == 4 else xn[:, i % 2, :]).rearrange("p (k n) -> p k n", n=P)
                act.wait_ge(S("norm_out"), NT * (s - 1) + i + 1)
                af(r32(actT[:, :, i * P:(i + 1) * P]), y, ACT.Copy).then_inc(S("norm_high"), 1)

            act.wait_ge(S("constants"), 1)
            for i in range(NT):
                squares(1, i, junk, S(f"x_in{i}"), 16)
                norm_rows(1, i)
                if i:
                    norm_high(1, i - 1)
            norm_high(1, NT - 1)
            act.wait_ge(S("small_in"), 16 * N_SMALL)
            af(silu_c[:], col("c_2", 0, KD), ACT.Silu).then_inc(S("silu_c"), 1)
            act.wait_ge(S("att_count"), 1)
            af(att_bias, cnt_t, ACT.Ln).then_inc(S("att_log"), 1)
            af(s5_s[:, 0, :], par[:, 0, :], ACT.Exp).then_inc(S("s5_dt"), 1)
            act.wait_ge(S("s5_pow"), 1)
            step(af(pw_l, pw_l, ACT.Exp))
            step(af(pw_i, pw_th, ACT.Sin))
            af(pw_r, pw_t, ACT.Sin).then_inc(S("s5_sin"), 1)
            act.wait_ge(S("s5_ang"), 1)
            af(turn[:, 1], ang_r, ACT.Sin).then_inc(S("s5_turn"), 1)
            act.wait_ge(S("s5_ang"), 2)
            af(turn[:, 0], ang_r, ACT.Sin).then_inc(S("s5_turn"), 1)
            act.wait_ge(S("s5_turn"), 3)
            act.dma_start(turn_dram, turn.rearrange("p a b c -> p (a b c)")).then_inc(S("turn_stored"), 16)
            for q8 in range(2):
                for n in range(PIECE // 256):
                    act.dma_start(s5_dram[q8][:, n * 256:(n + 1) * 256], zero[:]).then_inc(S("toeplitz_zero"), 16)
            act.wait_ge(S("ca_ready"), 1)
            for q8 in range(2):
                ro = s5_dram[q8][:, PIECE:].rearrange("p (q r n) -> p q r n", q=8, r=2)
                for ri, ca in enumerate((ca_r, ca_n)):
                    act.dma_start(ro[:, :, ri, :], ca[:, 8 * q8:8 * q8 + 8, 1:NPOW, :].rearrange("p q t h -> p q (t h)"))\
                        .then_inc(S("s5_const"), 16)
            for c in range(NADA):
                row = slice(32 * (c % 4), 32 * (c % 4) + 1)
                ins = af(mod_row[row, c // 4, :], full(act, ("ada", c // 4))[row, :], ACT.Copy)
                if c % 4 == 3:
                    out_of(("ada", c // 4), ins)
            act.wait_ge(S("turn_stored"), 16)
            for n in range(8):
                dst = inject.rearrange("p q r n -> p (q r) n")[:, 4 * n:4 * n + 4, :]
                src = full(act, ("s5b", n)).rearrange("p (a n) -> p a n", a=4)
                out_of(("s5b", n), af(dst, src, ACT.Copy))
            for n in range(8):
                copied(act, ("s5b", n))
            act.dma_start(inject_dram, inject.rearrange("p q r n -> p (q r n)")).then_inc(S("s5_const"), 16)
            act.wait_ge(S("taps_ready"), 1)
            act.wait_ge(S("toeplitz_zero"), 16 * 2 * (PIECE // 256))
            for q8 in range(2):
                tz = s5_dram[q8][:, 0:PIECE].rearrange("p (g n) -> p g n", g=NQ)
                tp = taps[0:SC, q8].rearrange("p r q n -> p (r q) n")
                for j in range(SL):
                    act.dma_start(tz[j * SC:(j + 1) * SC, :, j * SC:P], tp[:, :, 0:P - j * SC]).then_inc(S("s5_const"), 16)
            act.wait_ge(S("s5_const"), 16 * N_S5)

            for m in range(4):
                out_of(("xr", m), af(xr[:, m, :], full(act, ("xr", m)), ACT.Copy))
            for m in range(4):
                out_of(("gr", m), af(gr[:, m, :], full(act, ("gr", m)), ACT.Gelu_apprx_tanh))
            for m in range(4):
                out_of(("q", m), af(qT[:, m, :], full(act, ("q", m)), ACT.Copy, scale=DH ** -0.5))
            for m in range(4):
                out_of(("k", m), af(kT[:, m, :], full(act, ("k", m)), ACT.Copy))
            for m in range(4):
                out_of(("v", m), af(v[:, m, :], full(act, ("v", m)), ACT.Copy))
            act.wait_ge(S("lam_ready"), 1)
            af(lam(1), lam(0), ACT.Exp, scale=-1.0).then_inc(S("lam_act"), 1)
            act.wait_ge(S("lam_ready"), 2)
            af(lam(3), lam(2), ACT.Ln).then_inc(S("lam_act"), 1)
            for m in range(NL):
                out_of(("gate", 0, m), af(lru_a[:, m, :], full(act, ("gate", 0, m)), ACT.Sigmoid,
                                          bias=col("b_rgate", m)))
                out_of(("gate", 1, m), af(xr[:, m, :], full(act, ("gate", 1, m)), ACT.Sigmoid,
                                          bias=col("b_igate", m)))
            act.wait_ge(S("lam_ready"), 3)
            for m in range(NL):
                copied(act, ("gate", 0, m))
                step(af(lru_u[:, m, :], lru_a[:, m, :], ACT.Tanh, scale=lam(1)[:, m:m + 1]))
                af(lru_a[:, m, :], lru_a[:, m, :], ACT.Exp, scale=lam(0)[:, m:m + 1]).then_inc(S("lru_decay"), 1)
            for m in range(NL):
                act.wait_ge(S("lru_square"), m + 1)
                af(lru_u[:, m, :], lru_u[:, m, :], ACT.Sqrt).then_inc(S("lru_root"), 1)
            def probs(n):
                i, h = divmod(n, HEADS)
                act.wait_ge(S("att_max"), n + 1)
                s_row, d = att_s[:, h % 4, 0:(i + 1) * P], ST_DEN + 8 * (i % 2) + h
                af(s_row, s_row, ACT.Exp, bias=st[:, ST_MX + 8 + h:ST_MX + 9 + h], accum_out=st[:, d:d + 1])\
                    .then_inc(S("att_exp"), 1)

            def rows_high(i):
                bank = full(act, ("at", i)).rearrange("p (m n) -> p m n", m=4)
                af(r32(actT[:, 0:4, i * P:(i + 1) * P]), bank, ACT.Copy).then_inc(S("at_high"), 1)

            probs(0)
            for n in range(NT * HEADS):
                if n + 1 < NT * HEADS:
                    probs(n + 1)
                i, h = divmod(n, HEADS)
                out_of(("pt", i, h), af(att_pt[:, h % 2, 0:i + 1, :],
                                        full(act, ("pt", i, h))[:, 0:(i + 1) * P].rearrange("p (j n) -> p j n", n=P),
                                        ACT.Copy))
                if n >= HEADS and n % HEADS == 2:
                    rows_high(n // HEADS - 1)
            rows_high(NT - 1)

            def post_squares(s, i, key):
                c = [st[:, ST_PS + 2 * i + n:ST_PS + 2 * i + n + 1] for n in range(2)]
                for n in range(2):
                    bank = full(act, key(i, n))
                    step(af(post_tmp[:, 0, :], bank, ACT.Square, scale=D ** -0.5, accum_out=c[n]))
                step(af(c[0], c[0], ACT.Identity, bias=eps[:, 0:1]))
                af(c[1], c[1], ACT.Sqrt, bias=c[0]).then_inc(S("post_root"), 1)

            for i in range(NT):
                post_squares(1, i, lambda i, n: ("wo", 1, i, n))
                squares(2, i, junk, S("x_mix1"), i + 1)
                norm_rows(2, i)
                if i:
                    norm_high(2, i - 1)
            norm_high(2, NT - 1)
            for m in range(NF):
                copied(act, ("f1", m))
                af(hidT[:, m, :], hidT[:, m, :], ACT.Square).then_inc(S("hid_ready"), 1)
            for i in range(NT):
                post_squares(2, i, lambda i, n: ("f2", i, n))
                squares(3, i, junk, S("x_mlp"), i + 1)
                norm_rows(3, i)
                if i:
                    norm_high(3, i - 1)
            norm_high(3, NT - 1)

            for m in range(2):
                out_of(("gq", m), af(gq[:, m, :], full(act, ("gq", m)), ACT.Copy, scale=GDK ** -0.5))
            for m in range(2):
                out_of(("gq", 2 + m), af(gk[:, m, :], full(act, ("gq", 2 + m)), ACT.Copy))
            for m in range(4):
                out_of(("u", m), af(uT[:, m, :].rearrange("p (j c) -> p j c", j=SL),
                                    full(act, ("u", m)).rearrange("p (c j) -> p j c", j=SL), ACT.Copy))
            for m in range(4):
                copied(act, ("u", m))
                act.dma_start(u_dram[m * P:(m + 1) * P, :], uT[:, m, :]).then_inc(S("u_stored"), 16)
            act.dma_start(s5_turn.rearrange("p a b c -> p (a b c)"), turn_dram).then_inc(S("turn_in"), 16)
            out_of("a16", af(a16[0:16, :], full(act, "a16")[0:16, :], ACT.Copy))
            act.wait_ge(S("u_stored"), 16 * 4)
            ud = u_dram.rearrange("(g h) (j c) -> j h g c", h=SC, j=SL)
            for j in range(SL):
                act.dma_start(s5_u[j * SC:(j + 1) * SC, :, :], ud[j]).then_inc(S("u_in"), 16)
            for i in range(NT):
                out_of(("gv", i), af(gv[:, i, :], full(act, ("gv", i)), ACT.Copy))
            for i in range(NT):
                out_of(("og", i), af(og[:, i, :], full(act, ("og", i)), ACT.Silu))
            act.wait_ge(S("gla_abs"), 1)
            step(af(g_b, g_b, ACT.Exp, scale=-1.0))
            af(g_b, g_b, ACT.Ln, bias=1.0).then_inc(S("gla_log"), 1)
            act.wait_ge(S("gla_cum"), 1)
            step(af(g_e, g_b, ACT.Exp, scale=-1.0 / TAU))
            af(g_t, g_b, ACT.Exp, scale=1.0 / TAU).then_inc(S("gla_exp"), 1)
            for q8 in range(2):
                for par_ in range(2):
                    bank = full(act, ("Y", par_, q8))
                    dst = s5_y.rearrange("p (q r) c -> p q r c", r=2)[:, q8 * 8:(q8 + 1) * 8, par_, :]
                    out_of(("Y", par_, q8), af(dst, bank.rearrange("p (q c) -> p q c", q=8), ACT.Copy))
            for par_ in range(2):
                for q8 in range(2):
                    copied(act, ("Y", par_, q8))
            yd = y_dram.rearrange("(g h) (j c) -> j h g c", h=SC, j=SL)
            for j in range(SL):
                act.dma_start(yd[j], s5_y[j * SC:(j + 1) * SC, :, :]).then_inc(S("y5_stored"), 16)
            for i in range(NT):
                for par_ in range(2):
                    bank = full(act, ("go", i, par_))
                    for hh in range(2):
                        c = ST_GR + 4 * i + 2 * par_ + hh
                        step(af(a16[:, 0:GDV], bank[:, hh * GDV:(hh + 1) * GDV], ACT.Square,
                                accum_out=st[:, c:c + 1]))
                r = st[:, ST_GR + 4 * i:ST_GR + 4 * i + 4]
                af(r, r, ACT.Sqrt, scale=1.0 / GDV, bias=eps[:, 0:1]).then_inc(S("gla_root"), 1)
            for i in range(NT):
                bank = full(act, ("gt", i)).rearrange("p (m n) -> p m n", m=4)
                af(r32(actT[:, 0:4, i * P:(i + 1) * P]), bank, ACT.Copy).then_inc(S("gt_high"), 1)
            act.wait_ge(S("y5_in"), 16)
            for m in range(4):
                af(yT[:, m, :], yT[:, m, :], ACT.Gelu_apprx_tanh).then_inc(S("y5_gelu"), 1)
            for m in range(4):
                bank = full(act, ("glu", m))
                if m >= 2:
                    act.wait_ge(S("s5_out"), m - 1)
                out_of(("glu", m), af(sig[:, m % 2, :], bank, ACT.Sigmoid, bias=col("s5_glu_b_2", m)))
            for i in range(NT):
                post_squares(3, i, lambda i, n: ("wo", 2, i, n))
                squares(4, i, junk4, S("x_mix2"), i + 1)
                norm_rows(4, i)
                if i:
                    norm_high(4, i - 1)
            norm_high(4, NT - 1)
            for i in range(NT):
                act.wait_ge(S("xn_ready"), 3 * NT + i + 1)
                act.dma_start(xs_dram[i * P:(i + 1) * P, :], xs[:, i, :]).then_inc(S("xs_stored"), 16)
            act.wait_ge(S("top_diff"), 1)
            af(gate[:], gate[:], ACT.Exp).then_inc(S("top_exp"), 1)

            act.wait_ge(S("blocks_known"), 1)
            n_blocks = NE + act.value_load(blk_e[0:1, 63:64], min_val=0, max_val=MAX_EXTRA)

            def input_out(b):
                act.wait_ge(S("xgT_full"), b + 1)
                for k in range(KD):
                    ins = af(xgT[:, k, :], ps[:, 6 + k // 4, (k % 4) * P:(k % 4 + 1) * P], ACT.Identity,
                             scale=st[:, ST_MOD + 8 + k:ST_MOD + 9 + k], bias=col("ada_b_2", 3 * KD + k))
                ins.then_inc(S("xgT_ready"), 1)

            def gates(b):
                for hf in range(2):
                    act.wait_ge(S("sw_gate"), 2 * b + hf + 1)
                    if not isinstance(b, int) or hf:
                        act.wait_ge(S("sw_done"), 2 * b + hf)
                    af(sw_s, sw_g, ACT.Sigmoid, scale=SWI_ALPHA).then_inc(S("sw_sig"), 1)

            def hidden_out(b):
                act.wait_ge(S("hT_full"), b + 1)
                for half in range(2):
                    ins = af(hT[:, 4 * half:4 * half + 4, :], ps[:, 6 + half, :].rearrange("p (k s) -> p k s", k=4),
                             ACT.Copy)
                ins.then_inc(S("hT_ready"), 1)

            def store(b):
                act.wait_ge(S("y_done"), 2 * b + 3)
                act.dma_start(y_slots[bass.ds(b * P, P), :], y_row).then_inc(S("y_stored"), 16)

            act.sem_inc(S("y_stored"), 16)
            input_out(0)
            gates(0)
            input_out(1)
            hidden_out(0)
            with act.Fori(1, n_blocks) as b:
                gates(b)
                input_out(b + 1)
                store(b - 1)
                hidden_out(b)
            store(n_blocks - 1)
            for i in range(NT):
                act.wait_ge(S("ff_ready"), i + 1)
                r = st[:, ST_SS + i:ST_SS + i + 1]
                step(af(junk4, ff[:, i, :], ACT.Square, accum_out=r))
                af(r, r, ACT.Sqrt, scale=1.0 / D, bias=eps[:, 0:1]).then_inc(S("ff_root"), 1)
            act.wait_ge(S("ff_root"), NT)

        @block.vector
        def _(dve):
            step = stepper(dve, "dve_step")
            tt, ts, stt = nc.vector.tensor_tensor, nc.vector.tensor_scalar, nc.vector.scalar_tensor_tensor
            cp, scan = nc.vector.tensor_copy, nc.vector.tensor_tensor_scan

            dve.wait_ge(S("constants"), 1)
            step(cp(gla_mask, mask_f))
            step(cp(step_f[:], step_i))

            def norm_inverse(s, i):
                r = st[:, ST_SS + i:ST_SS + i + 1]
                dve.wait_ge(S("norm_root"), NT * (s - 1) + i + 1)
                nc.vector.reciprocal(r, r).then_inc(S("norm_inv"), 1)

            def norm_out(s, i, gain, shift=None):
                y = (y4 if s == 4 else xn[:, i % 2, :]).rearrange("p (k n) -> p k n", n=P)
                if s == 4 and i:
                    dve.wait_ge(S("norm_low"), NT * (s - 1) + i)
                tile = slice(i * P, (i + 1) * P)
                for h in range(2):
                    full(dve, ("norm", s, i, h))
                for h in range(2):
                    key = ("norm", s, i, h)
                    bank = ps[:, plan[key][0], :].rearrange("p (k n) -> p k n", n=P)
                    out_of(key, tt(y[:, 4 * h:4 * h + 4], bank, over(gain[:, 4 * h:4 * h + 4], 2, P), ALU.mult))
                for h in range(2):
                    copied(dve, ("norm", s, i, h))
                if shift is not None:
                    tt(y, y, over(shift, 2, P), ALU.add).then_inc(S("norm_out"), 1)
                else:
                    dve.sem_inc(S("norm_out"), 1)
                dve.wait_ge(S("norm_high"), NT * (s - 1) + i + 1)
                tt(r32(actL[:, :, tile]), y, actT[:, :, tile], ALU.subtract).then_inc(S("norm_low"), 1)

            dve.wait_ge(S("small_in"), 16 * N_SMALL)
            gain = col("mix_norm_pre", 0, KD)
            norm_inverse(1, 0)
            for i in range(1, NT):
                norm_inverse(1, i)
                norm_out(1, i - 1, gain)
            norm_out(1, NT - 1, gain)

            for bits, dst in ((15, cnt), (3, cnt_t)):
                step(ts(dist_i, dist, bits, None, ALU.bitwise_and))
                step(ts(dst, dist_i, 0.0, None, ALU.is_equal))
            step(tt(cnt, cnt, cnt_t, ALU.add))
            step(ts(cnt_t, dist, float(P), None, ALU.is_le))
            step(tt(cnt, cnt, cnt_t, ALU.add))
            step(ts(cnt_t, dist, 0.0, None, ALU.is_ge))
            step(tt(cnt, cnt, cnt_t, ALU.mult))
            ts(cnt_t, cnt, 1.0, None, ALU.max).then_inc(S("att_count"), 1)
            step(ts(cnt, cnt, 0.0, NEG, ALU.is_equal, ALU.mult))
            dve.wait_ge(S("att_log"), 1)
            step(tt(att_bias, att_bias, cnt, ALU.add))

            def reduced(dst, src, k, quarter):
                step(ts(k, src, 1.0 / TWO_PI, 0.25 * quarter, ALU.mult, ALU.add))
                step(ts(k, k, ROUND, None, ALU.add))
                step(ts(k, k, -ROUND, None, ALU.add))
                step(stt(dst, k, -PI_A, src, ALU.mult, ALU.add))
                step(stt(dst, k, -PI_B, dst, ALU.mult, ALU.add))
                step(stt(dst, k, -PI_C, dst, ALU.mult, ALU.add))
                if quarter:
                    step(ts(dst, dst, 0.5 * math.pi, None, ALU.add))
                return ts(dst, dst, PI_MAX, -PI_MAX, ALU.min, ALU.max)

            dt, s1, s2, s3, s4, s5, _ = (s5_s[:, n, :] for n in range(7))
            lr, li = par[:, 1, :], par[:, 2, :]
            dve.wait_ge(S("s5_dt"), 1)
            step(tt(s1, lr, dt, ALU.mult))
            step(tt(s2, li, dt, ALU.mult))
            step(reduced(s3, s2, s4, 0))
            taus = over(step_f[:, 0:NPOW], 2, NQ)
            step(tt(pw_l[:, 0:NPOW], taus, over(s1, 1, NPOW), ALU.mult))
            step(tt(pw_k[:, 0:NPOW], taus, over(s3, 1, NPOW), ALU.mult))
            step(reduced(pw_t[:, 0:NPOW], pw_k[:, 0:NPOW], pw_i[:, 0:NPOW], 1))
            reduced(pw_th[:, 0:NPOW], pw_k[:, 0:NPOW], pw_i[:, 0:NPOW], 0).then_inc(S("s5_pow"), 1)
            dve.wait_ge(S("s5_sin"), 1)
            ar, ai = pw_r, pw_i
            step(tt(ar[:, 0:NPOW], ar[:, 0:NPOW], pw_l[:, 0:NPOW], ALU.mult))
            step(tt(ai[:, 0:NPOW], ai[:, 0:NPOW], pw_l[:, 0:NPOW], ALU.mult))
            step(tt(ang, over(pw_th[:, SL, :], 2, SNC), over(step_f[:], 1, NQ), ALU.mult))
            reduced(ang_r, ang, ang_k, 0).then_inc(S("s5_ang"), 1)
            step(cp(turn[:, 2], over(pw_l[:, SL, :], 2, SNC)))
            nc.vector.memset(turn[:, 2, :, 0:1], 0.0).then_inc(S("s5_turn"), 1)
            dve.wait_ge(S("s5_turn"), 2)
            reduced(ang_r, ang, ang_k, 1).then_inc(S("s5_ang"), 1)
            step(tt(s1, lr, lr, ALU.mult))
            step(tt(s2, li, li, ALU.mult))
            step(tt(s1, s1, s2, ALU.add))
            step(nc.vector.reciprocal(s1, s1))
            step(ts(s2, ar[:, 1, :], -1.0, None, ALU.add))
            step(tt(s3, s2, lr, ALU.mult))
            step(tt(s4, ai[:, 1, :], li, ALU.mult))
            step(tt(s3, s3, s4, ALU.add))
            step(tt(s3, s3, s1, ALU.mult))
            step(tt(s4, ai[:, 1, :], lr, ALU.mult))
            step(tt(s5, s2, li, ALU.mult))
            step(tt(s4, s4, s5, ALU.subtract))
            step(tt(s4, s4, s1, ALU.mult))
            fr, fi = over(s3, 2, SC), over(s4, 2, SC)
            step(tt(bb_r, fr, b_r, ALU.mult))
            step(tt(bb_t, fi, b_i, ALU.mult))
            step(tt(bb_r, bb_r, bb_t, ALU.subtract))
            step(tt(bb_i, fr, b_i, ALU.mult))
            step(tt(bb_t, fi, b_r, ALU.mult))
            step(tt(bb_i, bb_i, bb_t, ALU.add))
            c9r, c9i = over(c_r, 2, NPOW), over(c_i, 2, NPOW)
            a9r, a9i = (over(x[:, 0:NPOW].rearrange("p t q -> p q t"), 3, SC) for x in (ar, ai))
            step(tt(ca_r, c9r, a9r, ALU.mult))
            step(tt(ca_t, c9i, a9i, ALU.mult))
            step(tt(ca_r, ca_r, ca_t, ALU.subtract))
            step(tt(ca_n, c9r, a9i, ALU.mult))
            step(tt(ca_t, c9i, a9r, ALU.mult))
            step(stt(ca_n, ca_n, -1.0, ca_t, ALU.mult, ALU.subtract))
            for j in range(SL):
                cp(pw_t[:, j, :], ar[:, SL - 1 - j, :])
                ins = cp(pw_th[:, j, :], ai[:, SL - 1 - j, :])
            ins.then_inc(S("ca_ready"), 1)
            dve.wait_ge(S("ca_ready"), 1)
            dve.wait_ge(S("s5_turn"), 3)
            b8r, b8i = over(bb_r, 2, SL), over(bb_i, 2, SL)
            a8r, a8i = (over(x[:, 0:SL].rearrange("p t q -> p q t"), 3, SC) for x in (pw_t, pw_th))
            tmp8 = ca_t[:, :, 0:SL, :]
            step(tt(bx_r, b8r, a8r, ALU.mult))
            step(tt(tmp8, b8i, a8i, ALU.mult))
            step(tt(bx_r, bx_r, tmp8, ALU.subtract))
            step(tt(bx_i, b8r, a8i, ALU.mult))
            step(tt(tmp8, b8i, a8r, ALU.mult))
            tt(bx_i, bx_i, tmp8, ALU.add).then_inc(S("bx_ready"), 1)
            mod = col("ada_b_2", 0, 6 * KD)
            by_row_tile = mod.rearrange("p (x j m) -> p j x m", j=4, m=4)
            for j in range(4):
                bank = full(dve, ("mod", j))[:, 0:NADA].rearrange("p (x m) -> p x m", m=4)
                out_of(("mod", j), tt(by_row_tile[:, j], bank, by_row_tile[:, j], ALU.add))
            for j in range(4):
                copied(dve, ("mod", j))
            for s, name in enumerate(("mix_pre_g_2", "ffn_pre_g_2")):
                step(stt(st[:, ST_MOD + KD * s:ST_MOD + KD * (s + 1)], mod[:, (3 * s + 1) * KD:(3 * s + 2) * KD], 1.0,
                         col(name, 0, KD), ALU.add, ALU.mult))
            for s, name in enumerate(("mix_post_g_2", "ffn_post_g_2")):
                step(tt(st[:, ST_PG + KD * s:ST_PG + KD * (s + 1)], mod[:, (3 * s + 2) * KD:(3 * s + 3) * KD],
                        col(name, 0, KD), ALU.mult))

            for par_ in range(2):
                for q4 in range(4):
                    key = ("s5k", par_, q4)
                    bank = full(dve, key)[0:SC, :].rearrange("p (q n) -> p q n", q=4)
                    out_of(key, cp(taps[0:SC, q4 // 2, par_, 4 * (q4 % 2):4 * (q4 % 2) + 4, :], bank))
            for par_ in range(2):
                for q4 in range(4):
                    copied(dve, ("s5k", par_, q4))
            direct = ca_t.rearrange("p q t h -> p (q t h)")[0:SC, 0:SG * SC].rearrange("p (g h) -> p g h", g=SG)
            first = taps.rearrange("p e r q n -> p (e r q) n")[0:SC, :, 0:SC]
            step(tt(direct, over(ident[0:SC, 0:SC], 1, SG), over(s5_d[:], 2, SC), ALU.mult))
            tt(first, first, direct, ALU.add).then_inc(S("taps_ready"), 1)

            for m in range(NL):
                copied(dve, ("xr", m))
                w = lambda t: col("conv_w", 4 * t + m)
                step(ts(xc[:, m, :], xr[:, m, :], w(CONV - 1), col("conv_b", m), ALU.mult, ALU.add))
                for t in range(CONV - 1):
                    back = CONV - 1 - t
                    ins = stt(xc[:, m, back:], xr[:, m, 0:T - back], w(t), xc[:, m, back:], ALU.mult, ALU.add)
                    if t < CONV - 2:
                        step(ins)
                ins.then_inc(S("conv_ready"), 1)
            lm = col("lru_lambda", 0, NL)
            step(ts(lam(5), lm, -1.0, None, ALU.mult))
            tt(lam(0), lm, lam(5), ALU.max).then_inc(S("lam_ready"), 1)
            dve.wait_ge(S("lam_act"), 1)
            ts(lam(2), lam(1), 1.0, None, ALU.add).then_inc(S("lam_ready"), 1)
            dve.wait_ge(S("lam_ready"), 2)
            step(ts(lam(4), lam(2), -1.0, None, ALU.add))
            step(ts(lam(5), lam(4), 0.0, None, ALU.is_equal))
            step(tt(lam(4), lam(4), lam(5), ALU.add))
            step(nc.vector.reciprocal(lam(4), lam(4)))
            step(tt(lam(4), lam(4), lam(1), ALU.mult))
            step(tt(lam(5), lam(5), lam(1), ALU.mult))
            dve.wait_ge(S("lam_act"), 2)
            step(tt(lam(3), lam(3), lam(4), ALU.mult))
            step(tt(lam(3), lam(3), lam(5), ALU.add))
            step(ts(lam(6), lm, -1.0, 0.0, ALU.mult, ALU.max))
            step(tt(lam(6), lam(6), lam(3), ALU.add))
            step(ts(lam(0), lam(6), -LRU_C, None, ALU.mult))
            ts(lam(1), lam(6), LRU_C, None, ALU.mult).then_inc(S("lam_ready"), 1)
            lru_t = att_pt.rearrange("p b j n -> p (b j n)")[:, 0:T]
            for m in range(NL):
                dve.wait_ge(S("lru_decay"), m + 1)
                step(tt(lru_t, lru_a[:, m, :], lru_a[:, m, :], ALU.mult))
                stt(lru_u[:, m, :], lru_t, 1.0, lru_u[:, m, :], ALU.add, ALU.mult).then_inc(S("lru_square"), 1)
                dve.wait_ge(S("lru_square"), m + 1)
            def recurrence(m):
                copied(dve, ("gate", 1, m))
                step(tt(xr[:, m, :], xr[:, m, :], xc[:, m, :], ALU.mult))
                dve.wait_ge(S("lru_root"), m + 1)
                step(tt(lru_u[:, m, :], lru_u[:, m, :], xr[:, m, :], ALU.mult))
                step(scan(xc[:, m, :], lru_a[:, m, :], lru_u[:, m, :], 0.0, ALU.mult, ALU.add))
                copied(dve, ("gr", m))
                step(tt(xc[:, m, :], xc[:, m, :], gr[:, m, :], ALU.mult))
                step(cp(r32(actT[:, 4 + m, :]), xc[:, m, :]))
                tt(r32(actL[:, 4 + m, :]), xc[:, m, :], actT[:, 4 + m, :], ALU.subtract).then_inc(S("rec_ready"), 1)

            mx, nmx = st[:, ST_MX:ST_MX + 8], st[:, ST_MX + 8:ST_MX + 16]
            rden = st[:, ST_RDEN:ST_RDEN + 8]

            def low_parts(name, i):
                tile, key = slice(i * P, (i + 1) * P), (name, i)
                dve.wait_ge(S(f"{name}_high"), i + 1)
                bank = ps[:, plan[key][0], :].rearrange("p (m n) -> p m n", m=4)
                out_of(key, tt(r32(actL[:, 0:4, tile]), bank, actT[:, 0:4, tile], ALU.subtract))

            def maximum(n):
                i, h = divmod(n, HEADS)
                keys_n = (i + 1) * P
                bias = att_bias[:, NT - 1 - i:NT, :].rearrange("p r n -> p (r n)")
                if n >= 4:
                    full(dve, ("pt", *divmod(n - 4, HEADS)))
                key = ("s", i, h)
                bank = full(dve, key)
                out_of(key, nc.vector.tensor_tensor_reduce(
                    out=att_s[:, h % 4, 0:keys_n], in0=bank[:, 0:keys_n], in1=bias, scale=1.0, scalar=NEG,
                    op0=ALU.add, op1=ALU.max, accum_out=mx[:, h:h + 1]))
                copied(dve, key)
                ts(nmx[:, h:h + 1], mx[:, h:h + 1], -1.0, None, ALU.mult).then_inc(S("att_max"), 1)

            def divide(i):
                den = st[:, ST_DEN + 8 * (i % 2):ST_DEN + 8 * (i % 2) + 8]
                dve.wait_ge(S("att_exp"), HEADS * (i + 1))
                step(nc.vector.reciprocal(rden, den))
                if i:
                    full(dve, ("at", i - 1))
                bank = full(dve, ("o", i))
                out_of(("o", i), tt(att_row.rearrange("p (h d) -> p h d", h=HEADS),
                                    bank.rearrange("p (h d) -> p h d", h=HEADS), over(rden, 2, DH), ALU.mult))

            for n in range(NT * HEADS):
                maximum(n)
                if n >= HEADS and n % HEADS == 2:
                    divide(n // HEADS - 1)
                if n >= HEADS and n % HEADS == 6:
                    low_parts("at", n // HEADS - 1)
                if n % HEADS == 4:
                    recurrence(n // HEADS)
            divide(NT - 1)
            low_parts("at", NT - 1)

            def post(s, i, key, gain, done):
                r = st[:, ST_PS + 2 * i + 1:ST_PS + 2 * i + 2]
                dve.wait_ge(S("post_root"), NT * (s - 1) + i + 1)
                step(nc.vector.reciprocal(r, r))
                for n in range(2):
                    half = slice(n * HALF, (n + 1) * HALF)
                    out_of(key(i, n), stt(post_tmp[:, n, :], ps[:, plan[key(i, n)][0], :], r, gain[:, half],
                                          ALU.mult, ALU.mult))
                for n in range(2):
                    copied(dve, key(i, n))
                tt(x_res[:, i, :], x_res[:, i, :], post_tmp.rearrange("p n d -> p (n d)"), ALU.add).then_inc(S(done), 1)
                dve.wait_ge(S(done), i + 1)

            def post_and_norm(s, key, post_gain, done, gain, shift=None):
                for i in range(NT):
                    post(s, i, key, post_gain, done)
                    norm_inverse(s + 1, i)
                    if i:
                        norm_out(s + 1, i - 1, gain, shift)
                norm_out(s + 1, NT - 1, gain, shift)

            post_and_norm(1, lambda i, n: ("wo", 1, i, n), post_g[:, 0, :], "x_mix1", col("mlp_norm_pre", 0, KD))
            for m in range(NF):
                out_of(("f1", m), ts(hidT[:, m, :], full(dve, ("f1", m)), 0.0, None, ALU.max))
            full(dve, ("f1", NF - 1))
            for kk in range(NF):
                dve.wait_ge(S("hid_ready"), kk + 1)
                if kk >= 4:
                    dve.wait_ge(S("split_used"), used_count(piece_no["ff_out", (kk - 4) // 4, (kk - 4) // 2 % 2]))
                step(cp(r32(hid_h[:, kk % 4, :]), hidT[:, kk, :]))
                tt(r32(hid_l[:, kk % 4, :]), hidT[:, kk, :], hid_h[:, kk % 4, :], ALU.subtract)\
                    .then_inc(S("hid_split"), 1)
            post_and_norm(2, lambda i, n: ("f2", i, n), post_g[:, 1, :], "x_mlp", st[:, ST_MOD:ST_MOD + KD], mod[:, 0:KD])
            for s in range(2):
                for k in range(KD):
                    ins = ts(diag[:, k, :], ident[:], st[:, ST_PG + KD * s + k:ST_PG + KD * s + k + 1], None, ALU.mult)
                ins.then_inc(S("diag_ready"), 1)
                for n in range(2):
                    out_of(("pg", s, n), cp(post_g[:, s, n * HALF:(n + 1) * HALF], full(dve, ("pg", s, n))))

            for m in range(2):
                out_of(("za", m), ts(g_t[:, m, :], full(dve, ("za", m)), col("b_alpha_2", m), None, ALU.add))
            for m in range(2):
                copied(dve, ("za", m))
            stt(g_b, g_t, -1.0, g_t, ALU.mult, ALU.max).then_inc(S("gla_abs"), 1)
            dve.wait_ge(S("gla_abs"), 1)
            step(ts(g_t, g_t, -1.0, 0.0, ALU.mult, ALU.max))
            dve.wait_ge(S("gla_log"), 1)
            step(tt(g_t, g_t, g_b, ALU.add))
            step(scan(g_b[:, 0, :], chunk_go[:], g_t[:, 0, :], 0.0, ALU.mult, ALU.add))
            scan(g_b[:, 1, :], chunk_go[:], g_t[:, 1, :], 0.0, ALU.mult, ALU.add).then_inc(S("gla_cum"), 1)
            dve.wait_ge(S("gla_exp"), 1)
            for m in range(4):
                copied(dve, ("gq", m))
            step(tt(gq, gq, g_e, ALU.mult))
            step(tt(gk, gk, g_t, ALU.mult))
            dec = st[:, ST_DEC:ST_DEC + 2 * NCH]
            step(cp(dec.rearrange("p (m c) -> p m c", m=2), g_e[:, :, CH - 1::CH]))
            ends = lambda x: x.rearrange("p m (c t) -> p (m c) t", t=CH)
            tt(ends(g_end), ends(gk), over(dec, 2, CH), ALU.mult).then_inc(S("gla_keys"), 1)
            for q8 in range(2):
                for ri in range(2):
                    key = ("D", ri, q8)
                    out_of(key, cp(s5_x[ri][:, q8 * 8:(q8 + 1) * 8, :],
                                   full(dve, key).rearrange("p (q c) -> p q c", q=8)))
            full(dve, ("og", NT - 1))
            step(nc.vector.memset(g_sT, 0.0))
            for i in range(NT):
                out_of(("ke", i), cp(g_endr[:, i, :], full(dve, ("ke", i))[:, 0:GH * GDK]))
            for h in range(GH):
                out_of(("gs", h), nc.vector.copy_predicated(g_sT[:, h, :], gla_mask.rearrange("p i n -> p (i n)"),
                                                            full(dve, ("gs", h))))
            for ri in range(2):
                for q8 in range(2):
                    copied(dve, ("D", ri, q8))
            dve.wait_ge(S("turn_in"), 16)
            cos, sin, decay = (s5_turn[:, n] for n in range(3))
            x0, x1, v0, v1 = s5_x[0], s5_x[1], s5_v[0], s5_v[1]
            flat = lambda x: x.rearrange("p q c -> p (q c)")
            step(tt(v0, x0, cos, ALU.mult))
            step(tt(s5_tmp, x1, sin, ALU.mult))
            step(tt(v0, v0, s5_tmp, ALU.add))
            step(tt(v1, x1, cos, ALU.mult))
            step(tt(s5_tmp, x0, sin, ALU.mult))
            step(tt(v1, v1, s5_tmp, ALU.subtract))
            step(scan(flat(x0), flat(decay), flat(v0), 0.0, ALU.mult, ALU.add))
            step(scan(flat(x1), flat(decay), flat(v1), 0.0, ALU.mult, ALU.add))
            step(tt(v0, x0, cos, ALU.mult))
            step(tt(s5_tmp, x1, sin, ALU.mult))
            step(tt(v0, v0, s5_tmp, ALU.subtract))
            step(tt(v1, x0, sin, ALU.mult))
            step(tt(s5_tmp, x1, cos, ALU.mult))
            tt(v1, v1, s5_tmp, ALU.add).then_inc(S("s5_states"), 1)
            for c in range(NCH - 1):
                for pair in range(2):
                    key = ("gd", pair, c % 2)
                    src = full(dve, key)[:, (c // 2) * GDV:(c // 2 + 1) * GDV]
                    if c == 0:
                        ins = cp(g_st[:, pair, 0, :], src)
                    else:
                        ins = stt(g_st[:, pair, c, :], g_st[:, pair, c - 1, :],
                                  dec[:, NCH * pair + c:NCH * pair + c + 1], src, ALU.mult, ALU.add)
                    if c >= NCH - 3:
                        out_of(key, ins)
                        copied(dve, key)
                    else:
                        step(ins)
            for i in range(NT):
                copied(dve, ("og", i))
            og_h = og.rearrange("p i (h d) -> p (i h) d", h=GH)
            step(tt(og_h, og_h, over(gla_g[:], 1, NT * GH), ALU.mult))
            for i in range(NT):
                r = st[:, ST_GR + 4 * i:ST_GR + 4 * i + 4]
                dve.wait_ge(S("gla_root"), i + 1)
                step(nc.vector.reciprocal(r, r))
                if i >= 2:
                    full(dve, ("gt", i - 2))
                for par_ in range(2):
                    bank = ps[:, plan[("go", i, par_)][0], :]
                    for hh in range(2):
                        h = 2 * hh + par_
                        ins = stt(g_row[:, i % 2, h * GDV:(h + 1) * GDV], bank[:, hh * GDV:(hh + 1) * GDV],
                                  r[:, 2 * par_ + hh:2 * par_ + hh + 1], og[:, i, h * GDV:(h + 1) * GDV],
                                  ALU.mult, ALU.mult)
                    out_of(("go", i, par_), ins)
            for i in range(NT):
                low_parts("gt", i)
            for m in range(4):
                copied(dve, ("glu", m))
                out_m = sig[:, m % 2, :]
                in_time = out_m.rearrange("p (j c) -> p j c", j=SL)
                step(tt(out_m, yT[:, m, :], out_m, ALU.mult))
                high, low = (x[:, 4 + m, :].rearrange("p (c j) -> p j c", j=SL) for x in (actT, actL))
                step(cp(r32(high), in_time))
                tt(r32(low), in_time, high, ALU.subtract).then_inc(S("s5_out"), 1)
            post_and_norm(3, lambda i, n: ("wo", 2, i, n), post_g[:, 0, :], "x_mix2", st[:, ST_MOD + KD:ST_MOD + 2 * KD],
                          mod[:, 3 * KD:4 * KD])

            out_of("lg", tt(lg, full(dve, "lg")[:, 0:NT * NE].rearrange("p (i e) -> p i e", i=NT),
                            over(router_b[:], 1, NT), ALU.add))
            copied(dve, "lg")
            for i in range(NT):
                step(nc.vector.max(out=top_v[:, i, :], in_=lg[:, i, :]))
                step(nc.vector.max_index(out=top_i[:, i, :], in_max=top_v[:, i, :], in_values=lg[:, i, :]))
            tt(gate[:], top_v[:, :, 0:TOPK], over(top_v[:, :, 0], 2, TOPK), ALU.subtract).then_inc(S("top_diff"), 1)
            dve.wait_ge(S("slots_cleared"), 32)
            step(cp(top_f, top_i))
            e_f = step_f[:, 0:NE]
            for i in range(NT):
                step(tt(pick[:, i], over(e_f, 1, TOPK), over(top_f[:, i, 0:TOPK], 2, NE), ALU.is_equal))
                nc.vector.tensor_reduce(mask[:, i, :], pick[:, i].rearrange("p k e -> p e k"), AX.X, ALU.add)\
                    .then_inc(S("mask_ready"), 1)
            bank = full(dve, "rk")
            step(cp(rank.rearrange("p i e -> p (i e)"), bank[:, 0:NT * NE]))
            out_of("rk", cp(cnt_e, bank[:, NT * NE:(NT + 1) * NE]))
            copied(dve, "rk")
            step(ts(ov, cnt_e, float(P), None, ALU.is_gt))
            step(stt(ov, cnt_e, float(2 * P), ov, ALU.is_gt, ALU.add))
            step(stt(ov, cnt_e, float(3 * P), ov, ALU.is_gt, ALU.add))
            step(scan(ov_in, ones[:, 0:NE], ov, 0.0, ALU.mult, ALU.add))
            step(tt(base_hi, ov_in, ov, ALU.subtract))
            step(ts(base_hi, base_hi, float(NE - 1), float(P), ALU.add, ALU.mult))
            step(stt(base_d, e_f, float(P), base_hi, ALU.mult, ALU.subtract))
            step(ts(pos, rank, float(P), None, ALU.is_lt))
            step(tt(pos, pos, over(base_d, 1, NT), ALU.mult))
            step(tt(pos, pos, over(base_hi, 1, NT), ALU.add))
            step(tt(pos, pos, rank, ALU.add))
            for i in range(NT):
                step(tt(prod[:, i], pick[:, i], over(pos[:, i, :], 1, TOPK), ALU.mult))
            step(nc.vector.tensor_reduce(posf, prod.rearrange("p i k e -> p (i k) e"), AX.X, ALU.add))
            cp(posi[:], posf).then_inc(S("slots_known"), 1)
            step(tt(le_f[0:1], over(ov_in[0:1], 1, MAX_EXTRA + 1), over(step_f[0:1, 0:MAX_EXTRA + 1], 2, NE), ALU.is_le))
            step(nc.vector.tensor_reduce(blk_f[0:1, 0:MAX_EXTRA + 1], le_f[0:1], AX.X, ALU.add))
            step(ts(blk_f[0:1, 0:MAX_EXTRA + 1], blk_f[0:1, 0:MAX_EXTRA + 1], float(NE - 1), None, ALU.min))
            step(cp(blk_e[0:1, 0:NE], e_f[0:1]))
            step(cp(blk_e[0:1, NE:NE + MAX_EXTRA + 1], blk_f[0:1, 0:MAX_EXTRA + 1]))
            dve.wait_ge(S("top_exp"), 1)
            step(nc.vector.tensor_reduce(gsum, gate[:], AX.X, ALU.add))
            step(nc.vector.reciprocal(gsum, gsum))
            step(tt(gate[:], gate[:], over(gsum, 2, TOPK), ALU.mult))
            cp(blk_e[0:1, 63:64], ov_in[0:1, NE - 1:NE]).then_inc(S("blocks_known"), 1)
            dve.wait_ge(S("blocks_known"), 1)

            n_blocks = NE + dve.value_load(blk_e[0:1, 63:64], min_val=0, max_val=MAX_EXTRA)

            def swiglu(b):
                dve.wait_ge(S("bgu_ready"), 2 * b + 2)
                for hf in range(2):
                    half = slice(hf * HALF, (hf + 1) * HALF)
                    dve.wait_ge(S("gu_full"), 4 * b + 2 * hf + 1)
                    tt(sw_t, ps[:, 2 * hf, :], bgu[:, half], ALU.add).then_inc(S("gu_copied"), 1)
                    dve.wait_ge(S("gu_copied"), 4 * b + 2 * hf + 1)
                    ts(sw_g, sw_t, SWI_LIMIT, None, ALU.min).then_inc(S("sw_gate"), 1)
                    dve.wait_ge(S("gu_full"), 4 * b + 2 * hf + 2)
                    tt(sw_u, ps[:, 2 * hf + 1, :], bgu[:, D + hf * HALF:D + (hf + 1) * HALF], ALU.add)\
                        .then_inc(S("gu_copied"), 1)
                    dve.wait_ge(S("gu_copied"), 4 * b + 2 * hf + 2)
                    ts(sw_u, sw_u, SWI_LIMIT, -SWI_LIMIT, ALU.min, ALU.max).then_inc(S("sw_clip"), 1)
                    dve.wait_ge(S("sw_clip"), 2 * b + hf + 1)
                    dve.wait_ge(S("sw_gate"), 2 * b + hf + 1)
                    stt(sw_p, sw_u, 1.0, sw_g, ALU.add, ALU.mult).then_inc(S("sw_up"), 1)
                    dve.wait_ge(S("sw_up"), 2 * b + hf + 1)
                    dve.wait_ge(S("sw_sig"), 2 * b + hf + 1)
                    if not isinstance(b, int):
                        dve.wait_ge(S("hT_full"), b)
                    tt(h_row[:, half], sw_p, sw_s, ALU.mult).then_inc(S("sw_done"), 1)

            def outputs(b):
                dve.wait_ge(S("bdn_ready"), b + 1)
                dve.wait_ge(S("y_stored"), 16 * b + 16)
                for n in range(2):
                    half = slice(n * HALF, (n + 1) * HALF)
                    dve.wait_ge(S("dn_full"), 2 * b + n + 1)
                    tt(y_row[:, half], ps[:, 4 + n, :], bdn[:, half], ALU.add).then_inc(S("y_done"), 1)

            dve.sem_inc(S("y_done"), 1)
            swiglu(0)
            with dve.Fori(1, n_blocks) as b:
                swiglu(b)
                outputs(b - 1)
            outputs(n_blocks - 1)
            for i in range(NT):
                dve.wait_ge(S(f"y_in{i}"), 16 * TOPK)
                step(ts(ff[:, i, :], y_pick[TOPK * i], gate[:, i, 0:1], None, ALU.mult))
                for k in range(1, TOPK):
                    ins = stt(ff[:, i, :], y_pick[TOPK * i + k], gate[:, i, k:k + 1], ff[:, i, :], ALU.mult, ALU.add)
                    if k < TOPK - 1:
                        step(ins)
                ins.then_inc(S("ff_ready"), 1)
            for i in range(NT):
                r = st[:, ST_SS + i:ST_SS + i + 1]
                dve.wait_ge(S("ff_root"), i + 1)
                step(nc.vector.reciprocal(r, r))
                step(stt(ff[:, i, :], ff[:, i, :], r, post_g[:, 1, :], ALU.mult, ALU.mult))
                tt(x_res[:, i, :], x_res[:, i, :], ff[:, i, :], ALU.add).then_inc(S("x_final"), 1)
            dve.wait_ge(S("x_final"), NT)

        @block.tensor
        def _(pe):
            mm = nc.tensor.matmul

            def take(key):
                b, turn_no = plan[key]
                if turn_no:
                    pe.wait_ge(bank_copied[b], turn_no)
                return ps[:, b, :]

            def done(key, ins):
                ins.then_inc(bank_full[plan[key][0]], 1)

            def parts(name, c, h):
                n = piece_no[name, c, h]
                pe.wait_ge(S("split_ready"), n + 1)
                return (r32(part(n, low)).rearrange("p (g n) -> p g n", g=NG) for low in range(2))

            def transposes(s, i):
                pe.wait_ge(S("xn_ready"), NT * (s - 1) + i + 1)
                row = xs[:, i, :] if s == 4 else xn[:, i % 2, :]
                for h in range(2):
                    key = ("norm", s, i, h)
                    bank = take(key)
                    for k in range(4):
                        ins = nc.tensor.transpose(bank[:, k * P:(k + 1) * P], row[:, (4 * h + k) * P:(4 * h + k + 1) * P],
                                                  ident[:])
                    done(key, ins)

            def normed(s):
                pe.wait_ge(S("norm_low"), NT * (s - 1) + NT)

            def three(o, stat, mov, start, stop):
                mm(o, stat[0], mov[0], start=start, stop=False)
                mm(o, stat[0], mov[1], start=False, stop=False)
                return mm(o, stat[1], mov[0], start=False, stop=stop)

            def by_column(name, c, keys, tokens=False):
                banks = {}
                for h in range(2):
                    w = tuple(parts(name, c, h))
                    for g in range(NG):
                        k = NG * h + g
                        for m, key in enumerate(keys):
                            if k == 0:
                                banks[m] = take(key)
                            tile = slice(m * P, (m + 1) * P)
                            if tokens:
                                stat, mov = [r32(x[:, k, tile]) for x in (actT, actL)], [x[:, g, :] for x in w]
                            else:
                                stat, mov = [x[:, g, tile] for x in w], [r32(x[:, k, :]) for x in (actT, actL)]
                            ins = three(banks[m], stat, mov, k == 0, k == KD - 1)
                            if k == KD - 1:
                                done(key, ins)
                    if h == 0:
                        ins.then_inc(S("split_used"), 1)

            def by_row(name, blocks, key, left, s):
                banks = {}

                def product(i, n, k, w, g):
                    if k == 0:
                        banks[i, n] = take(key(i, n))
                    tile = slice(i * P, (i + 1) * P)
                    return three(banks[i, n], [r32(x[:, tile]) for x in left(k)], [x[:, g, :] for x in w], k == 0,
                                 k == 4 * blocks - 1)

                for c in range(blocks - 1):
                    for h in range(2):
                        w = tuple(parts(name, c, h))
                        for g in range(NG):
                            for i in range(NT):
                                ins = product(i, g % 2, 4 * c + 2 * h + g // 2, w, g)
                        ins.then_inc(S("split_used"), 1)
                c = blocks - 1
                w = [tuple(parts(name, c, h)) for h in range(2)]
                for i in range(NT):
                    for n in range(2):
                        for k in range(4):
                            ins = product(i, n, 4 * c + k, w[k // 2], 2 * (k % 2) + n)
                        done(key(i, n), ins)
                    if i:
                        transposes(s + 1, i - 1)
                transposes(s + 1, NT - 1)

            pe.wait_ge(S("constants"), 1)
            for i in range(NT):
                transposes(1, i)
            pe.wait_ge(S("silu_c"), 1)
            for c in range(NADA):
                row = slice(32 * (c % 4), 32 * (c % 4) + 1)
                bank = take(("ada", c // 4)) if c % 4 == 0 else bank
                for h in range(2):
                    n = 2 * c + h
                    pe.wait_ge(S(f"ada_in{n % 4}"), 16 * (n // 4 + 1))
                    w = piece(n % 4).rearrange("p (k n) -> p k n", k=NG)
                    for g in range(NG):
                        k = NG * h + g
                        ins = mm(bank[row, :], silu_c[:, k:k + 1], w[:, g, :], start=(k == 0), stop=(k == KD - 1))
                    if n % 8 == 7:
                        done(("ada", c // 4), ins)
                    else:
                        ins.then_inc(S("ada_used"), 1)
            for c in range(NADA // 4):
                copied(pe, ("ada", c))
            for j in range(4):
                row, bank = slice(32 * j, 32 * j + 1), take(("mod", j))
                for x in range(NADA // 4):
                    for m in range(4):
                        ins = mm(bank[:, 4 * x + m:4 * x + m + 1], mod_row[row, x, m * P:(m + 1) * P], ones[row, 0:1],
                                 start=True, stop=True)
                done(("mod", j), ins)
            pe.wait_ge(S("bx_ready"), 1)
            for n in range(8):
                bank = take(("s5b", n))
                for x in range(4):
                    q, ri = divmod(4 * n + x, 2)
                    src = (bx_r, bx_i)[ri][:, q].rearrange("p j h -> p (j h)")
                    ins = nc.tensor.transpose(bank[:, x * P:(x + 1) * P], src, ident[:])
                done(("s5b", n), ins)
            for par_ in range(2):
                half = slice(SS * par_, SS * (par_ + 1))
                for q4 in range(4):
                    bank = take(("s5k", par_, q4))
                    for x in range(4):
                        q = 4 * q4 + x
                        o = bank[0:SC, x * P:(x + 1) * P]
                        mm(o, bb_r[half, q, :], ca_r[half, q, 0:SL, :].rearrange("p t h -> p (t h)"),
                           start=True, stop=False)
                        ins = mm(o, bb_i[half, q, :], ca_n[half, q, 0:SL, :].rearrange("p t h -> p (t h)"),
                                 start=False, stop=True)
                    done(("s5k", par_, q4), ins)
            normed(1)
            for name, c in (("xr", 3), ("gr", 4), ("q", 0), ("k", 1)):
                by_column("w_in", c, [(name, m) for m in range(4)])
            by_column("w_in", 2, [("v", i) for i in range(NT)], tokens=True)
            for m in range(NL):
                pe.wait_ge(S("conv_ready"), m + 1)
                for g in range(2):
                    done(("gate", g, m), mm(take(("gate", g, m)), w_gate[:, g, m, :], xc[:, m, :], start=True, stop=True))
            for m in range(4):
                copied(pe, ("q", m))
                copied(pe, ("k", m))
                copied(pe, ("v", m))

            def scores(n):
                i, h = divmod(n, HEADS)
                half, keys_n = slice(DH * (h % 2), DH * (h % 2 + 1)), (i + 1) * P
                done(("s", i, h), mm(take(("s", i, h))[:, 0:keys_n], qT[half, h // 2, i * P:(i + 1) * P],
                                     kT[half, h // 2, 0:keys_n], start=True, stop=True))

            def turn_probs(n):
                i, h = divmod(n, HEADS)
                pe.wait_ge(S("att_exp"), n + 1)
                bank = take(("pt", i, h))
                for j in range(i + 1):
                    ins = nc.tensor.transpose(bank[:, j * P:(j + 1) * P], att_s[:, h % 4, j * P:(j + 1) * P], ident[:])
                done(("pt", i, h), ins)

            def values(n):
                i, h = divmod(n, HEADS)
                o = take(("o", i)) if h == 0 else ps[:, 7, :]
                copied(pe, ("pt", i, h))
                for j in range(i + 1):
                    ins = mm(o[:, h * DH:(h + 1) * DH], att_pt[:, h % 2, j, :], v[:, j, h * DH:(h + 1) * DH],
                             start=(j == 0), stop=(j == i))
                if h == HEADS - 1:
                    done(("o", i), ins)

            def turn_rows(i):
                copied(pe, ("o", i))
                bank = take(("at", i))
                for m in range(4):
                    ins = nc.tensor.transpose(bank[:, m * P:(m + 1) * P], att_row[:, m * P:(m + 1) * P], ident[:])
                done(("at", i), ins)

            for n in range(3):
                scores(n)
            for n in range(NT * HEADS):
                if n + 3 < NT * HEADS:
                    scores(n + 3)
                turn_probs(n)
                if n:
                    values(n - 1)
                if n >= HEADS and n % HEADS == 2:
                    turn_rows(n // HEADS - 1)
            values(NT * HEADS - 1)
            turn_rows(NT - 1)
            for i in range(NT):
                copied(pe, ("at", i))
            pe.wait_ge(S("rec_ready"), NL)
            act_k = lambda k: (actT[:, k, :], actL[:, k, :])
            by_row("w_out", 2, lambda i, n: ("wo", 1, i, n), act_k, 1)

            normed(2)
            for c in range(8):
                by_column("ff_in", c, [("f1", 4 * c + m) for m in range(4)])

            def hid_k(k):
                pe.wait_ge(S("hid_split"), k + 1)
                return hid_h[:, k % 4, :], hid_l[:, k % 4, :]

            by_row("ff_out", 8, lambda i, n: ("f2", i, n), hid_k, 2)
            for s in range(2):
                pe.wait_ge(S("diag_ready"), s + 1)
                for n in range(2):
                    bank = take(("pg", s, n))
                    for k in range(4):
                        ins = mm(bank[:, k * P:(k + 1) * P], ones[:], diag[:, 4 * n + k, :], start=True, stop=True)
                    done(("pg", s, n), ins)
            normed(3)
            by_column("w_in_2", 0, [("gq", m) for m in range(4)])
            by_column("w_in_2", 3, [("u", m) for m in range(4)])
            bank = take("a16")
            for n, x in enumerate((actT, actL)):
                for k in range(KD):
                    ins = mm(bank[0:16, :], w_a16[:, k, :], x[:, k, :], start=(n + k == 0), stop=(n == 1 and k == KD - 1))
            done("a16", ins)
            copied(pe, "a16")
            for m in range(2):
                done(("za", m), mm(take(("za", m)), w_alpha[:, m * P:(m + 1) * P], a16[0:16, :], start=True, stop=True))
            by_column("w_in_2", 1, [("gv", i) for i in range(NT)], tokens=True)
            by_column("w_in_2", 2, [("og", i) for i in range(NT)], tokens=True)
            w = ring[:].rearrange("p (q r n) -> p q r n", q=NQ, r=2)
            pe.wait_ge(S("u_in"), 16 * SL)
            for q8 in range(2):
                pe.wait_ge(S(f"inject_in{q8}"), 16)
                for ri in range(2):
                    bank = take(("D", ri, q8))
                    for x in range(8):
                        for par_ in range(2):
                            q = 8 * q8 + x
                            half = slice(SS * par_, SS * (par_ + 1))
                            ins = mm(bank[half, x * SNC:(x + 1) * SNC], w[:, q, ri, half], s5_u[:, 2 * q + par_, :],
                                     start=True, stop=True)
                    done(("D", ri, q8), ins)
            pe.wait_ge(S("gla_keys"), 1)
            for i in range(NT):
                bank = take(("ke", i))
                for m in range(2):
                    ins = nc.tensor.transpose(bank[:, m * P:(m + 1) * P], g_end[:, m, i * P:(i + 1) * P], ident[:])
                done(("ke", i), ins)
            for h in range(GH):
                half = slice(GDK * (h % 2), GDK * (h % 2 + 1))
                bank = take(("gs", h))
                for i in range(NT):
                    tile = slice(i * P, (i + 1) * P)
                    ins = mm(bank[:, tile], gk[half, h // 2, tile], gq[half, h // 2, tile], start=True, stop=True)
                done(("gs", h), ins)
            for i in range(NT):
                copied(pe, ("ke", i))
                copied(pe, ("gv", i))
            for pair in range(2):
                for cp_ in range(2):
                    bank = take(("gd", pair, cp_))
                    rows = slice(CH * cp_, CH * (cp_ + 1))
                    for c in range(cp_, NCH - 1, 2):
                        for hh in range(2):
                            h = 2 * pair + hh
                            ins = mm(bank[GDK * hh:GDK * (hh + 1), (c // 2) * GDV:(c // 2 + 1) * GDV],
                                     g_endr[rows, c // 2, h * GDK:(h + 1) * GDK], gv[rows, c // 2, h * GDV:(h + 1) * GDV],
                                     start=True, stop=True)
                    done(("gd", pair, cp_), ins)
            wt = ring[:, 0:PIECE].rearrange("p (r q n) -> p r q n", r=2, n=P)
            wr = ring[:, PIECE:].rearrange("p (q r n) -> p q r n", r=2, n=P)
            pe.wait_ge(S("s5_states"), 1)
            for q8 in range(2):
                pe.wait_ge(S("s5_in"), 16 * (q8 + 1))
                for par_ in range(2):
                    half = slice(SS * par_, SS * (par_ + 1))
                    bank = take(("Y", par_, q8))
                    for x in range(8):
                        q = 8 * q8 + x
                        mm(bank[:, x * SNC:(x + 1) * SNC], wt[:, par_, x, :], s5_u[:, 2 * q + par_, :],
                           start=True, stop=False)
                        for ri in range(2):
                            ins = mm(bank[:, x * SNC + 1:(x + 1) * SNC], wr[half, x, ri, :],
                                     s5_v[ri][half, q, 0:SNC - 1], start=False, stop=(ri == 1))
                    done(("Y", par_, q8), ins)
            for h in range(GH):
                copied(pe, ("gs", h))
            for pair in range(2):
                for cp_ in range(2):
                    copied(pe, ("gd", pair, cp_))
            for i in range(NT):
                for par_ in range(2):
                    bank = take(("go", i, par_))
                    half = slice(GDK * par_, GDK * (par_ + 1))
                    for hh in range(2):
                        h = 2 * hh + par_
                        o = bank[:, hh * GDV:(hh + 1) * GDV]
                        mm(o, g_sT[:, h, i * P:(i + 1) * P], gv[:, i, h * GDV:(h + 1) * GDV], start=True, stop=True)
                        for x in range(2):
                            c = 2 * i + x
                            if c:
                                ins = mm(o[CH * x:CH * (x + 1), :], gq[half, hh, c * CH:(c + 1) * CH],
                                         g_st[half, hh, c - 1, :], start=False, stop=True, skip_group_check=True)
                    done(("go", i, par_), ins)
            for i in range(NT):
                copied(pe, ("go", i, 0))
                copied(pe, ("go", i, 1))
                bank = take(("gt", i))
                for m in range(4):
                    ins = nc.tensor.transpose(bank[:, m * P:(m + 1) * P], g_row[:, i % 2, m * P:(m + 1) * P], ident[:])
                done(("gt", i), ins)
            pe.wait_ge(S("glu_in"), 16)
            w = piece(1).rearrange("p (k n) -> p k n", k=NG)
            pe.wait_ge(S("y5_gelu"), 4)
            for m in range(4):
                bank = take(("glu", m))
                for k in range(4):
                    ins = mm(bank, w[:, k, m * P:(m + 1) * P], yT[:, k, :], start=(k == 0), stop=(k == 3))
                done(("glu", m), ins)
            for i in range(NT):
                copied(pe, ("gt", i))
            pe.wait_ge(S("s5_out"), 4)
            by_row("w_out_2", 2, lambda i, n: ("wo", 2, i, n), act_k, 3)
            normed(4)
            bank = take("lg")
            for i in range(NT):
                for n, x in enumerate((actT, actL)):
                    for k in range(KD):
                        ins = mm(bank[:, i * NE:(i + 1) * NE], x[:, k, i * P:(i + 1) * P], router_w[:, k, :],
                                 start=(n + k == 0), stop=(n == 1 and k == KD - 1))
            done("lg", ins)
            pe.wait_ge(S("mask_ready"), NT)
            bank = take("rk")
            for i in range(NT + 1):
                for j in range(min(i + 1, NT)):
                    ins = mm(bank[:, i * NE:(i + 1) * NE], before[:] if j == i else ones[:], mask[:, j, :],
                             start=(j == 0), stop=(j == min(i, NT - 1)))
            done("rk", ins)

            copied(pe, "rk")
            pe.wait_ge(S("blocks_known"), 1)
            n_blocks = NE + pe.value_load(blk_e[0:1, 63:64], min_val=0, max_val=MAX_EXTRA)

            def input_in(b):
                pe.wait_ge(S("xg_in"), 16 * b + 16)
                if not (isinstance(b, int) and b < 2):
                    pe.wait_ge(S("hT_ready"), b - 1)
                for k in range(KD):
                    ins = nc.tensor.transpose(ps[:, 6 + k // 4, (k % 4) * P:(k % 4 + 1) * P], xg[:, k * P:(k + 1) * P],
                                              ident[:])
                ins.then_inc(S("xgT_full"), 1)

            def gate_up(b):
                pe.wait_ge(S("xgT_ready"), b + 1)
                for j in range(4):
                    pe.wait_ge(S(f"part_in{j}"), 16 * b + 16)
                    if not isinstance(b, int):
                        pe.wait_ge(S("gu_copied"), 4 * b + j - 3)
                    w = slot(j).rearrange("p (k n) -> p k n", k=KD)
                    for k in range(KD):
                        ins = mm(ps[:, j, :], xgT[:, k, :], w[:, k, :], start=(k == 0), stop=(k == KD - 1))
                    ins.then_inc(S("gu_full"), 1)

            def down(b):
                pe.wait_ge(S("hT_ready"), b + 1)
                pe.wait_ge(S("y_done"), 2 * b + 1)
                for n in range(2):
                    pe.wait_ge(S(f"part_in{4 + n}"), 16 * b + 16)
                    w = slot(4 + n).rearrange("p (k n) -> p k n", k=KD)
                    for k in range(KD):
                        ins = mm(ps[:, 4 + n, :], hT[:, k, :], w[:, k, :], start=(k == 0), stop=(k == KD - 1))
                    ins.then_inc(S("dn_full"), 1)

            def hidden_in(b):
                pe.wait_ge(S("sw_done"), 2 * b + 2)
                pe.wait_ge(S("xgT_ready"), b + 2)
                for k in range(KD):
                    ins = nc.tensor.transpose(ps[:, 6 + k // 4, (k % 4) * P:(k % 4 + 1) * P], h_row[:, k * P:(k + 1) * P],
                                              ident[:])
                ins.then_inc(S("hT_full"), 1)

            input_in(0)
            gate_up(0)
            input_in(1)
            hidden_in(0)
            with pe.Fori(1, n_blocks) as b:
                gate_up(b)
                input_in(b + 1)
                down(b - 1)
                hidden_in(b)
            down(n_blocks - 1)



_LARGE = ["x", "mix_norm_post", "mlp_norm_post", "w_in", "w_out", "w_ff_in", "w_ff_out", "ada_w_2", "w_in_2",
          "w_alpha_2", "gla_norm_g_2", "s5_glu_w_2", "w_out_2", "router_w_2", "router_b_2", "exp_w_gu_2",
          "exp_b_gu_2", "exp_w_down_2", "exp_b_down_2"]


def laid_out(inputs):
    arrays = {name: np.ascontiguousarray(inputs[name]) for name in _LARGE}
    arrays["cols"] = np.ascontiguousarray(
        np.concatenate([np.asarray(inputs[name]).reshape(n, P) for name, n in VECS]).T)

    def states(x):
        x = np.asarray(x).reshape(NQ, 2 * SS, -1)
        return np.ascontiguousarray(x.transpose(1, 0, 2))

    step = np.broadcast_to(np.asarray(inputs["s5_log_dt_2"]).reshape(SG, 1), (SG, SS))
    arrays["s5_par"] = np.ascontiguousarray(np.concatenate(
        [states(x) for x in (step, inputs["s5_lambda_re_2"], inputs["s5_lambda_im_2"])], axis=2).transpose(0, 2, 1))
    for name in ("s5_b_re", "s5_b_im"):
        arrays[name] = states(inputs[name + "_2"])
    for name in ("s5_c_re", "s5_c_im"):
        arrays[name] = states(np.asarray(inputs[name + "_2"])[0].transpose(0, 2, 1))
    arrays["s5_d"] = np.ascontiguousarray(np.asarray(inputs["s5_d_2"]).reshape(2, NQ // 2, 2, SC)
                                          .transpose(3, 0, 2, 1).reshape(SC, SG))
    for name in ("w_rgate", "w_igate"):
        w = np.asarray(inputs[name])[0]
        n = w.shape[1]
        two = np.zeros((P, NL, P), w.dtype)
        for g in range(2):
            two[g * n:(g + 1) * n, :, g * n:(g + 1) * n] = w[g::2].transpose(1, 0, 2)
        arrays[name] = two
    return arrays


def kernel(**inputs):
    import concourse.bacc as bacc
    from concourse.bass_utils import run_bass_kernel_spmd

    nc = bacc.Bacc("TRN2", target_bir_lowering=False, num_devices=1)
    arrays = {f"in_{name}": x for name, x in laid_out(inputs).items()}
    handles = {name[3:]: nc.dram_tensor(name, x.shape, mybir.dt.from_np(x.dtype), kind="ExternalInput").ap()
               for name, x in arrays.items()}
    out = nc.dram_tensor("out", (1, T, D), F32, kind="ExternalOutput").ap()
    program(nc, handles, out)
    result = run_bass_kernel_spmd(nc, [arrays], core_ids=[0])
    return result.results[0]["out"]
```

```python
import math
from contextlib import ExitStack

import numpy as np

import concourse.bass as bass
from concourse import mybir

F32 = mybir.dt.float32
F32R = mybir.dt.float32r
I32 = mybir.dt.int32
U32 = mybir.dt.uint32
ALU = mybir.AluOpType
ACT = mybir.ActivationFunctionType
AX = mybir.AxisListType

P = 128
T = 512
NT = T // P
D = 1024
KD = D // P
EPS = 1e-6
HALF = 512
FF = 4 * D
NF = FF // P
HEADS, DH = 8, 64
NEG = -1.0e30
LRU_C = 8.0
CONV = 4
NL = 4
GH, GDK, GDV, CH = 4, 64, 128, 64
NCH = T // CH
TAU = 16.0
SG, SC, SS = 32, 16, 64
NQ = SG // 2
SL = 8
SNC = T // SL
NPOW = SL + 1
TWO_PI = 2.0 * math.pi
PI_A = 6.28125
PI_B = 0.0019350051879882812
PI_C = TWO_PI - PI_A - PI_B
ROUND = 12582912.0
PI_MAX = 3.1415925
NE, TOPK = 32, 4
SWI_ALPHA, SWI_LIMIT = 1.702, 7.0
MAX_EXTRA = (T * TOPK - 1) // P
MAX_BLOCKS = NE + MAX_EXTRA
SLOTS = (MAX_BLOCKS + 1) * P
BLK = KD * HALF
PIECE = BLK // 2
RAW, SPLIT = 6, 4
NG = PIECE // HALF
SCR = 21760
NADA = 6 * D // HALF

VECS = [("mix_norm_pre", 8), ("mlp_norm_pre", 8), ("mix_pre_g_2", 8), ("ffn_pre_g_2", 8),
        ("mix_post_g_2", 8), ("ffn_post_g_2", 8), ("conv_w", 16), ("conv_b", 4), ("b_rgate", 4),
        ("b_igate", 4), ("lru_lambda", 4), ("b_alpha_2", 2), ("s5_glu_b_2", 4), ("c_2", 8),
        ("ada_b_2", 48)]
NVEC = sum(n for _, n in VECS)
COL = {}
for _i, (_name, _n) in enumerate(VECS):
    COL[_name] = (sum(n for _, n in VECS[:_i]), _n)

N_SMALL = 16
N_S5 = 4 + 1 + 2 * SL

ST_SS, ST_R, ST_PS, ST_DEN, ST_MX = 0, 4, 8, 16, 32
ST_LAM, ST_MOD, ST_PG, ST_GR, ST_DEC = 64, 96, 112, 128, 160
ST_RDEN = 176
ST_N = 192


def bank_plan():
    turns, plan, count = [0] * 8, {}, [0]

    def give(key, bank=None):
        if bank is None:
            bank, count[0] = count[0] % 8, count[0] + 1
        plan[key] = (bank, turns[bank])
        turns[bank] += 1

    def norm(s):
        for i in range(NT):
            for h in range(2):
                give(("norm", s, i, h), 2 * i + h)

    def rows(*key):
        for i in range(NT):
            for n in range(2):
                give((*key, i, n), 2 * i + n)

    for x in range(NADA // 4):
        give(("ada", x), x)
    norm(1)
    for x in range(NADA // 4):
        give(("mod", x), 5 + x)
    keys = [("s5b", n) for n in range(8)]
    keys += [("s5k", par, q4) for par in range(2) for q4 in range(4)]
    keys += [(w, m) for w in ("xr", "gr", "q", "k", "v") for m in range(4)]
    keys += [("gate", g, m) for m in range(NL) for g in range(2)]
    for key in keys:
        give(key)
    for i in range(NT):
        give(("o", i), 7)
        for h in range(HEADS):
            give(("s", i, h), h % 4)
            give(("pt", i, h), 4 + h % 2)
        give(("at", i), 6)
    rows("wo", 1)
    norm(2)
    for m in range(NF):
        give(("f1", m), m % 8)
    rows("f2")
    norm(3)
    count[0] = 0
    keys = [("gq", m) for m in range(4)] + [("u", m) for m in range(4)]
    keys += [("pg", s, n) for s in range(2) for n in range(2)] + ["a16"]
    keys += [("za", m) for m in range(2)] + [("gv", i) for i in range(NT)] + [("og", i) for i in range(NT)]
    keys += [("D", ri, q8) for q8 in range(2) for ri in range(2)]
    keys += [("ke", i) for i in range(NT)] + [("gs", h) for h in range(GH)]
    keys += [("gd", pair, cp) for pair in range(2) for cp in range(2)]
    keys += [("Y", par, q8) for q8 in range(2) for par in range(2)]
    keys += [("go", i, par) for i in range(NT) for par in range(2)] + [("gt", i) for i in range(NT)]
    keys += [("glu", m) for m in range(4)]
    for key in keys:
        give(key)
    rows("wo", 2)
    norm(4)
    for i in range(NT):
        give(("lg", i), 2 * i)
    give("rk", 1)
    return plan


def weight_plan():
    def columns(name, c, last):
        return [(name, c, 0, None), (name, c, 1, last)]

    def rows(name, order, last):
        return [(name, c, h, last if (c, h) == (order[-1], 1) else None) for c in order for h in range(2)]

    plan = []
    for c in (3, 4, 0, 1, 2):
        plan += columns("w_in", c, (("q", "k", "v", "xr", "gr")[c], 3))
    plan += rows("w_out", (0, 1), ("wo", 1, NT - 1, 1))
    for c in range(8):
        plan += columns("ff_in", c, ("f1", 4 * c + 3))
    plan += rows("ff_out", range(8), ("f2", NT - 1, 1))
    for c in (0, 3, 1, 2):
        plan += columns("w_in_2", c, (("gq", "gv", "og", "u")[c], 3))
    return plan + rows("w_out_2", (0, 1), ("wo", 2, NT - 1, 1))


def program(nc, a, out):
    plan = bank_plan()
    pieces = weight_plan()
    piece_no = {piece[:3]: n for n, piece in enumerate(pieces)}
    after_s5 = piece_no["w_out_2", 0, 0]

    with ExitStack() as ctx:
        def sb(name, shape, dt=F32):
            return ctx.enter_context(nc.sbuf_tensor(name, shape, dt))

        with ExitStack() as rounded:
            def fr(name, shape):
                return rounded.enter_context(nc.sbuf_tensor(name, shape, F32))

            split = fr("split", [P, 4 * PIECE])
            actT = fr("actT", [P, KD, T])
            actL = fr("actL", [P, KD, T])
            xT_h, xT_l, hT_h, hT_l = (fr(name, [P, KD, P]) for name in ("xT_h", "xT_l", "hT_h", "hT_l"))

        def scratch(name, shape, dt=F32):
            return nc.dram_tensor(name, shape, dt, kind="Internal").ap()

        sems = {}

        def S(name):
            if name not in sems:
                sems[name] = ctx.enter_context(nc.semaphore(name))
            return sems[name]

        inject_dram = scratch("s5_inject", (P, BLK))
        s5_dram = [scratch(f"s5_response{q8}", (P, BLK)) for q8 in range(2)]
        turn_dram = scratch("s5_turn", (P, 3 * NQ * SNC))
        u_dram = scratch("u_dram", (T, T))
        y_dram = scratch("y_dram", (T, T))
        xs_dram = scratch("xs_dram", (T, D))
        slot_token = scratch("slot_token", (SLOTS, 1), I32)
        y_slots = scratch("y_slots", (SLOTS, D))

        plain = sb("plain", [P, 4 * PIECE + 2 * KD * T])
        plain_actT = plain[:, 4 * PIECE:4 * PIECE + KD * T].rearrange("p (k t) -> p k t", k=KD)
        scr = sb("scr", [P, SCR])
        ring = sb("ring", [P, 2 * PIECE])
        x_res = sb("x_res", [P, NT, D])
        ident = sb("ident", [P, P])
        ones = sb("ones", [P, P])
        masks = sb("masks", [P, 2, T])
        att_bias = masks[:, 0].rearrange("p (i n) -> p i n", i=NT)
        gla_mask = masks[:, 1].rearrange("p (i n) -> p i n", i=NT).bitcast(I32)
        zero = sb("zero", [P, 256])
        step_f = sb("step_f", [P, SNC])
        chunk_go = sb("chunk_go", [P, T])
        before = sb("before", [P, P])
        cols = sb("cols", [P, NVEC])
        silu_c = sb("silu_c", [P, KD])
        post_g = sb("post_g", [P, 2, D])
        st = sb("st", [P, ST_N])
        eps = sb("eps", [P, 1])
        w_a16 = sb("w_a16", [P, KD, 16])
        w_alpha = sb("w_alpha", [16, GH * GDK])
        w_gate = sb("w_gate", [P, 2, NL, P])
        gla_g = sb("gla_g", [P, GDV])
        router_w = sb("router_w", [P, KD, NE])
        router_b = sb("router_b", [P, NE])
        tok_id = sb("tok_id", [P, NT], I32)

        def view(at, *shape, of=scr):
            ap = of[:, at:at + math.prod(shape)]
            if len(shape) == 1:
                return ap
            names = "abcd"[:len(shape)]
            return ap.rearrange(f"p ({' '.join(names)}) -> p {' '.join(names)}",
                                **dict(zip(names, shape)))

        def col(name, k=0, n=1):
            return cols[:, COL[name][0] + k:COL[name][0] + k + n]

        def over(ap, axis, n):
            ap = ap.unsqueeze(axis)
            shape = list(ap.shape)
            shape[axis] = n
            return ap.broadcast_to(shape)

        def raw(k):
            return ring[:, k * PIECE:(k + 1) * PIECE] if k < 2 else \
                scr[:, 4 * D + (k - 2) * PIECE:4 * D + (k - 1) * PIECE]

        def halves(k):
            both = split[:, k % 2 * BLK:(k % 2 + 1) * BLK] if k < 2 else (actT, actL)[k - 2].rearrange("p k t -> p (k t)")
            return both[:, 0:PIECE], both[:, PIECE:BLK]

        def piece(s):
            return ring[:, s * PIECE:(s + 1) * PIECE] if s < 2 else scr[:, 17664 + (s - 2) * PIECE:17664 + (s - 1) * PIECE]

        def part(n, low):
            at = (2 * (n % 2) + low) * PIECE
            return split[:, at:at + PIECE]

        def r32(ap):
            return ap.bitcast(F32R)

        xn, junk, post_tmp = view(0, 2, D), view(2048, D), view(3072, 2, HALF)
        mask_f, dist = view(11264, NT, P), view(11776, NT, P).bitcast(I32)
        dist_i, cnt, cnt_t = view(12288, NT, P).bitcast(I32), view(12800, NT, P), view(13568, NT, P)
        par = view(3072, 3, NQ)
        b_r, b_i, c_r, c_i = (view(3120 + 256 * n, NQ, SC) for n in range(4))
        bb_r, bb_i, bb_t = (view(4144 + 256 * n, NQ, SC) for n in range(3))
        pw_l, pw_th, pw_k, pw_t, pw_r, pw_i = (view(4912 + 272 * n, NPOW, NQ) for n in range(6))
        s5_s = view(6544 - 0, 7, NQ)
        ca_r, ca_n, ca_t = view(6656, NQ, NPOW, SC), view(8960, NQ, NPOW, SC), view(11264, NQ, NPOW, SC)
        bx_r, bx_i = view(13568, NQ, SL, SC), view(15616, NQ, SL, SC)
        inject = view(17664, NQ, 2, P)
        taps = view(13568, 2, 2, NQ // 2, P)
        turn = view(2 * BLK, 3, NQ, SNC, of=plain)
        mod_row = view(3 * PIECE, NADA // 4, HALF, of=plain)
        ang, ang_k, ang_r = (view(13568 + 1024 * n, NQ, SNC) for n in range(3))
        step_i = view(14080, SNC).bitcast(I32)
        s5_d = sb("s5_d", [SC, SG])
        att_s, att_pt, att_row = view(0, 4, T), view(2048, 2, NT, P), view(3072, T)
        qT, kT, v = view(4096, 4, T), view(6144, 4, T), view(8192, NT, T)
        xr, gr, xc = view(10240, NL, T), view(12288, NL, T), view(14336, NL, T)
        lru_a, lru_u = view(16384, NL, T), view(18432, NL, T)
        hidT = view(4096, NF, T)
        hid_h, hid_l = actT[:, 0:4, :], actT[:, 4:8, :]
        diag = (view(20480, KD, P), view(3072, KD, P))
        gq, gk, g_t, g_b, g_e = (view(4096 + 1024 * n, 2, T) for n in range(5))
        g_end, g_endr, g_row = g_b, view(8192, NT, GH * GDK), view(6144, 2, T)
        gv, og = view(9216, NT, T), view(11264, NT, T)
        g_st = view(13312, 2, NCH - 1, GDV)
        a16 = view(15360, T)
        g_sT = plain_actT[:, 0:4, :]
        uT = view(17920, 4, T)
        s5_u = view(15872, SG, SNC)
        s5_x = [view(17920 + 1024 * ri, NQ, SNC) for ri in range(2)]
        s5_v = [plain_actT[:, 4 + 2 * ri:6 + 2 * ri, :].rearrange("p a (b c) -> p (a b) c", c=SNC) for ri in range(2)]
        s5_turn = view(0, 3, NQ, SNC)
        s5_tmp = view(19968, NQ, SNC)
        s5_y = view(17920, SG, SNC)
        yT = view(15872, 4, T)
        sig = view(19968, 2, T)
        xs = view(8192, NT, D)
        y4 = view(12288, D)
        junk4 = view(20480, D)
        lg, mask = view(13312, NT, NE), view(13440, NT, NE)
        pick, prod = view(13568, NT, TOPK, NE), view(14080, NT, TOPK, NE)
        rank, pos = view(14592, NT, NE), view(14720, NT, NE)
        cnt_e, ov, ov_in, base_hi, base_d = (view(14848 + 32 * n, NE) for n in range(5))
        le_f = view(15040, MAX_EXTRA + 1, NE)
        top_v, top_f = view(15552, NT, 8), view(15616, NT, 8)
        top_i = view(15584, NT, 8).bitcast(U32)
        gsum, posf, blk_f = view(15648, NT), view(15656, NT * TOPK), view(15672, NE)
        gate = sb("gate", [P, NT, TOPK])
        posi = sb("posi", [P, NT * TOPK], I32)
        blk_e = sb("blk_e", [1, 64], I32)
        bgu, bdn, y_row = view(12288, 2 * D), view(14336, D), view(15360, D)
        sw_t, sw_g, sw_s, sw_u = (view(16384 + HALF * n, HALF) for n in range(4))
        sw_p = sw_t
        xT = view(18432, KD, P)
        h_row = view(19456, D)
        bg_row, bu_row = view(20480, D), w_gate[:].rearrange("p a b c -> p (a b c)")
        bdn_row = masks[:].rearrange("p a b -> p (a b)")
        slot_idx = sb("slot_idx", [P, 1], I32)
        xg = post_g[:, 0, :]
        y_pick = [view(n * D, D) for n in range(NT * TOPK)]
        ff = view(NT * TOPK * D, NT, D)

        ps = ctx.enter_context(nc.psum_tensor("ps", [P, 8, HALF], F32))
        bank_full = [S(f"bank_full{b}") for b in range(8)]
        bank_copied = [S(f"bank_copied{b}") for b in range(8)]

        def full(eng, key):
            b, turn_no = plan[key]
            eng.wait_ge(bank_full[b], turn_no + 1)
            return ps[:, b, :]

        def copied(eng, key):
            b, turn_no = plan[key]
            eng.wait_ge(bank_copied[b], turn_no + 1)

        def out_of(key, ins):
            ins.then_inc(bank_copied[plan[key][0]], 1)

        def lam(n):
            return st[:, ST_LAM + NL * n:ST_LAM + NL * (n + 1)]

        def stepper(eng, name):
            n = [0]

            def step(ins):
                n[0] += 1
                ins.then_inc(S(name), 1)
                eng.wait_ge(S(name), n[0])
            return step

        helped = [piece_no["ff_in", 1, 0], piece_no["w_in_2", 3, 0]]

        def used_count(n):
            return sum(last is None for *_, last in pieces[:n + 1])

        def place(b, x, back=0):
            return (x if isinstance(b, int) and b == 0 else x - 4) - back

        MOST = (NG - 1) * HALF

        block = ctx.enter_context(nc.Block())

        @block.sync
        def _(sp):
            for i in range(NT):
                sp.dma_start(x_res[:, i, :], a["x"][0, i * P:(i + 1) * P, :]).then_inc(S(f"x_in{i}"), 16)
            sp.wait_ge(S("small_in"), 16 * N_SMALL)

            def ada_free(n):
                if n % 8 == 7:
                    full(sp, ("ada", n // 8))
                else:
                    sp.wait_ge(S("ada_used"), n - n // 8 + 1)

            for n in range(2 * NADA):
                if n >= 4:
                    ada_free(n - 4)
                c, h = divmod(n, 2)
                src = a["ada_w_2"][0, h * NG * P:(h + 1) * NG * P, c * HALF:(c + 1) * HALF]
                sp.dma_start(piece(n % 4).rearrange("p (k n) -> p k n", k=NG), src.rearrange("(k p) n -> p k n", p=P))\
                    .then_inc(S(f"ada_in{n % 4}"), 16)

            def load_piece(n):
                name, c, h, _ = pieces[n]
                if name in ("w_out", "ff_out", "w_out_2"):
                    w, row = a["w_ff_out" if name == "ff_out" else name], (2 * c + h) * 2 * P
                    src = w[0, row:row + 2 * P, :]
                else:
                    w, at = a["w_ff_in" if name == "ff_in" else name], c * HALF
                    if (name, c) == ("w_in_2", 3):
                        at += 16
                    src = w[0, h * NG * P:(h + 1) * NG * P, at:at + HALF]
                src = src.rearrange("(k p) n -> p k n", p=P)
                sp.dma_start(piece(n % 2).rearrange("p (k n) -> p k n", k=src.shape[1]), src)\
                    .then_inc(S(f"piece_in{n % 2}"), 16)

            for n in range(after_s5):
                if n < 2:
                    ada_free(2 * NADA - 4 + n)
                else:
                    sp.wait_ge(S("split_ready"), n - 1)
                load_piece(n)
            sp.wait_ge(S("s5_const"), 16 * N_S5)
            for q8 in range(2):
                sp.wait_ge(S("split_ready"), after_s5 - 1 + q8)
                sp.dma_start(piece(q8), inject_dram[:, q8 * PIECE:(q8 + 1) * PIECE]).then_inc(S(f"inject_in{q8}"), 16)
            for q8 in range(2):
                full(sp, ("Y", 1, 0) if q8 else ("D", 1, 1))
                sp.dma_start(ring[:], s5_dram[q8]).then_inc(S("s5_in"), 16)
            full(sp, ("Y", 1, 1))
            sp.dma_start(piece(1).rearrange("p (k n) -> p k n", k=NG),
                         a["s5_glu_w_2"][0].rearrange("(k p) n -> p k n", p=P)).then_inc(S("glu_in"), 16)
            assert after_s5 % 2 == 0
            load_piece(after_s5)
            sp.wait_ge(S("y5_stored"), 16 * SL)
            sp.dma_start(yT, y_dram.rearrange("(m p) n -> p m n", p=P)).then_inc(S("y5_in"), 16)
            full(sp, ("glu", 3))
            load_piece(after_s5 + 1)
            for n in range(after_s5 + 2, len(pieces)):
                sp.wait_ge(S("split_ready"), n - 1)
                load_piece(n)

            def load_part(b, x, e, d=None):
                o = place(b, x)
                if not isinstance(b, int) or 12 * b + o >= RAW:
                    sp.wait_ge(S("low_dve"), 12 * b + o - RAW + 1)
                    sp.wait_ge(S("low_pool"), 12 * b + o - RAW + 1)
                j, h = divmod(x if d is None else d, 2)
                w, at = (a["exp_w_gu_2"], (j % 2) * D + (j // 2) * HALF) if d is None else (a["exp_w_down_2"], j * HALF)
                src = w[0, bass.ds(e, 1), h * NG * P:(h + 1) * NG * P, at:at + HALF]
                sp.dma_start(raw(o % RAW).rearrange("p (k n) -> p k n", k=NG), src.rearrange("o (k p) n -> p (o k) n", p=P))\
                    .then_inc(S(f"raw_in{o % RAW}"), 16)

            sp.wait_ge(S("split_ready"), len(pieces))
            for x in range(2):
                load_part(0, x, 0)
            full(sp, ("lg", NT - 1))
            sp.wait_ge(S("xs_stored"), 16 * NT)
            for x in range(2, 8):
                load_part(0, x, 0)
            for x in range(12):
                load_part(1, x, 1 if x < 8 else 0, None if x < 8 else x - 8)
            sp.wait_ge(S("blocks_known"), 1)
            n_blocks = NE + sp.value_load(blk_e[0:1, 63:64], min_val=0, max_val=MAX_EXTRA)
            with sp.Fori(2, n_blocks) as b:
                e = sp.value_load(blk_e[0:1, bass.ds(b, 1)], min_val=0, max_val=NE - 1)
                e_last = sp.value_load(blk_e[0:1, bass.ds(b - 1, 1)], min_val=0, max_val=NE - 1)
                for x in range(12):
                    load_part(b, x, e if x < 8 else e_last, None if x < 8 else x - 8)
            e_last = sp.value_load(blk_e[0:1, bass.ds(n_blocks - 1, 1)], min_val=0, max_val=NE - 1)
            for x in range(4):
                load_part(n_blocks, x, e_last, x)
            for i in range(NT):
                sp.wait_ge(S("x_final"), i + 1)
                sp.dma_start(out[0, i * P:(i + 1) * P, :], x_res[:, i, :]).then_inc(S("out_stored"), 16)
            sp.wait_ge(S("out_stored"), 16 * NT)

        @block.gpsimd
        def _(pool):
            step = stepper(pool, "pool_step")
            step(nc.gpsimd.memset(ident[:], 0.0))
            step(nc.gpsimd.affine_select(out=ident[:], in_=ident[:], compare_op=ALU.not_equal, fill=1.0,
                                         base=0, pattern=[[-1, P]], channel_multiplier=1))
            step(nc.gpsimd.memset(ones[:], 1.0))
            step(nc.gpsimd.memset(before[:], 1.0))
            step(nc.gpsimd.affine_select(out=before[:], in_=before[:], compare_op=ALU.is_gt, fill=0.0,
                                         base=0, pattern=[[1, P]], channel_multiplier=-1))
            step(nc.gpsimd.memset(eps[:], EPS))
            step(nc.gpsimd.memset(mask_f, 1.0))
            step(nc.gpsimd.affine_select(out=mask_f, in_=mask_f, compare_op=ALU.is_ge, fill=0.0,
                                         base=0, pattern=[[0, NT], [1, P]], channel_multiplier=-1))
            step(nc.gpsimd.memset(mask_f[0:CH, :, CH:P], 0.0))
            step(nc.gpsimd.iota(dist, pattern=[[-P, NT], [-1, P]], base=(NT - 1) * P, channel_multiplier=1))
            step(nc.gpsimd.iota(step_i, pattern=[[1, SNC]], base=0, channel_multiplier=0))
            step(nc.gpsimd.iota(tok_id[:], pattern=[[P, NT]], base=0, channel_multiplier=1))
            step(nc.gpsimd.memset(zero[:], 0.0))
            step(nc.gpsimd.memset(mod_row, 0.0))
            step(nc.gpsimd.memset(chunk_go[:], 1.0))
            nc.gpsimd.memset(chunk_go[:, ::CH], 0.0).then_inc(S("constants"), 1)

            def split_piece(n):
                pool.wait_ge(S(f"piece_in{n % 2}"), 16 * (n // 2 + 1))
                if n == 1:
                    for x in range(NADA // 4):
                        full(pool, ("mod", x))
                if n >= 2:
                    last = pieces[n - 2][3]
                    if last:
                        full(pool, last)
                    else:
                        pool.wait_ge(S("split_used"), used_count(n - 2))
                three = lambda ap: ap.rearrange("p (a b) -> p a b", b=P)
                if n not in helped:
                    nc.gpsimd.tensor_tensor(three(r32(part(n, 0))), three(piece(n % 2)), over(ones[:], 1, PIECE // P), ALU.mult)\
                        .then_inc(S("split_high"), 1)
                pool.wait_ge(S("split_high"), n + 1)
                nc.gpsimd.tensor_tensor(r32(part(n, 1)), piece(n % 2), part(n, 0), ALU.subtract)\
                    .then_inc(S("split_ready"), 1)

            pool.wait_ge(S("constants"), 1)
            for n in range(len(pieces)):
                split_piece(n)
                if n == piece_no["w_in", 2, 1]:
                    pool.dma_start(slot_token.rearrange("(b s) o -> b (s o)", s=P),
                                   zero[0:MAX_BLOCKS + 1, 0:P].bitcast(I32)).then_inc(S("slots_cleared"), 16)
                    pool.dma_start(y_slots[NE * P:, :].rearrange("(s b) (h d) -> s (b h) d", s=P, h=4),
                                   over(zero[:], 1, 4 * (SLOTS // P - NE))).then_inc(S("slots_cleared"), 16)
            def low_part(b, x):
                o = place(b, x)
                pool.wait_ge(S("high"), 12 * b + o + 1)
                high, low = halves(o % SPLIT)
                nc.gpsimd.tensor_tensor(r32(low[:, MOST:]), raw(o % RAW)[:, MOST:], high[:, MOST:], ALU.subtract)\
                    .then_inc(S("low_pool"), 1)

            for x in range(4):
                low_part(0, x)
            pool.wait_ge(S("slots_cleared"), 32)
            pool.wait_ge(S("slots_known"), 1)
            for n in range(NT * TOPK):
                pool.indirect_dma_start(slot_token[:, :], bass.IndirectOffsetOnAxis(posi[:, n:n + 1], 0),
                                        tok_id[:, n // TOPK:n // TOPK + 1], None).then_inc(S("slots_filled"), 16)
            pool.wait_ge(S("slots_filled"), 16 * NT * TOPK)
            pool.wait_ge(S("xs_stored"), 16 * NT)
            pool.wait_ge(S("blocks_known"), 1)

            def token_list(b):
                pool.dma_start(slot_idx[:], slot_token[bass.ds(b * P, P), :]).then_inc(S("idx_in"), 16)

            def gather(b):
                pool.wait_ge(S("idx_in"), 16 * b + 16)
                if not (isinstance(b, int) and b == 0):
                    pool.wait_ge(S("xgT_full"), b)
                pool.sem_inc(S("gather_clear"), 1)
                pool.indirect_dma_start(xg, None, xs_dram[:, :], bass.IndirectOffsetOnAxis(slot_idx[:, 0:1], 0))\
                    .then_inc(S("xg_in"), 16)

            def gate_bias_row(e, b):
                pool.dma_start(bg_row[0:1, :], a["exp_b_gu_2"][0, bass.ds(e, 1), 0:D]).then_inc(S("bgu_in"), 16)
                pool.dma_start(bu_row[0:1, :], a["exp_b_gu_2"][0, bass.ds(e, 1), D:2 * D]).then_inc(S("bgu_in"), 16)

            def gate_bias(b):
                pool.wait_ge(S("bgu_in"), 32 * b + 32)
                if not (isinstance(b, int) and b == 0):
                    pool.wait_ge(S("gu_copied"), 4 * b)
                pool.sem_inc(S("gate_bias_clear"), 1)
                nc.gpsimd.partition_broadcast(bgu[:, 0:D], bg_row[0:1, :], P).then_inc(S("bgu_ready"), 1)
                nc.gpsimd.partition_broadcast(bgu[:, D:], bu_row[0:1, :], P).then_inc(S("bgu_ready"), 1)
                pool.wait_ge(S("bgu_ready"), 2 * b + 2)

            def down_bias_row(e, b):
                pool.dma_start(bdn_row[0:1, :], a["exp_b_down_2"][0, bass.ds(e, 1), :]).then_inc(S("bdn_in"), 16)

            def down_bias(b):
                pool.wait_ge(S("bdn_in"), 16 * b + 16)
                pool.wait_ge(S("y_done"), 2 * b + 1)
                pool.sem_inc(S("down_bias_clear"), 1)
                nc.gpsimd.partition_broadcast(bdn, bdn_row[0:1, :], P).then_inc(S("bdn_ready"), 1)
                pool.wait_ge(S("bdn_ready"), b + 1)

            n_blocks = NE + pool.value_load(blk_e[0:1, 63:64], min_val=0, max_val=MAX_EXTRA)

            def expert(b):
                return pool.value_load(blk_e[0:1, bass.ds(b, 1)], min_val=0, max_val=NE - 1)

            def loop_turn(b):
                pool.wait_ge(S("xg_in"), 16 * b + 16)
                if isinstance(b, int) and b == 0:
                    pieces_n, chores = 8, {}
                else:
                    pieces_n, chores = 12, {3: lambda: down_bias_row(expert(b - 1), b - 1), 8: lambda: down_bias(b - 1)}
                chores |= {0: lambda: token_list(b + 1), 1: lambda: gate_bias_row(expert(b + 1), b + 1),
                           4: lambda: gather(b + 1), pieces_n - 1: lambda: gate_bias(b + 1)}
                for x in range(pieces_n):
                    if x >= 4 or not (isinstance(b, int) and b == 0):
                        low_part(b, x)
                    if x in chores:
                        chores[x]()

            token_list(0)
            gather(0)
            gate_bias_row(0, 0)
            gate_bias(0)
            loop_turn(0)
            loop_turn(1)
            with pool.Fori(2, n_blocks) as b:
                loop_turn(b)
            for x in range(4):
                low_part(n_blocks, x)
            down_bias_row(expert(n_blocks - 1), n_blocks - 1)
            down_bias(n_blocks - 1)
            pool.wait_ge(S("y_stored"), 16 * n_blocks + 16)
            pool.sem_inc(S("pick_clear"), 1)
            for n in range(NT * TOPK):
                pool.indirect_dma_start(y_pick[n], None, y_slots[:, :],
                                        bass.IndirectOffsetOnAxis(posi[:, n:n + 1], 0)).then_inc(S(f"y_in{n // TOPK}"), 16)
            for i in range(NT):
                pool.wait_ge(S(f"y_in{i}"), 16 * TOPK)

        @block.scalar
        def _(act):
            step = stepper(act, "act_step")
            af = nc.scalar.activation
            small = [(cols[:], a["cols"]), (par, a["s5_par"]), (b_r, a["s5_b_re"]), (b_i, a["s5_b_im"]),
                     (c_r, a["s5_c_re"]), (c_i, a["s5_c_im"]), (s5_d[:], a["s5_d"]), (w_gate[:, 0], a["w_rgate"]),
                     (w_gate[:, 1], a["w_igate"]), (w_alpha[:], a["w_alpha_2"][0]),
                     (gla_g[:], a["gla_norm_g_2"][0].partition_broadcast(P)),
                     (router_w[:], a["router_w_2"][0].rearrange("(k p) n -> p k n", p=P)),
                     (router_b[:], a["router_b_2"][0].partition_broadcast(P)),
                     (post_g[:, 0, :], a["mix_norm_post"][0].partition_broadcast(P)),
                     (post_g[:, 1, :], a["mlp_norm_post"][0].partition_broadcast(P)),
                     (w_a16[:], a["w_in_2"][0, :, 1536:1552].rearrange("(k p) n -> p k n", p=P))]
            assert len(small) == N_SMALL
            for dst, src in small:
                act.dma_start(dst, src).then_inc(S("small_in"), 16)

            def squares(s, i, dst, *ready):
                act.wait_ge(*ready)
                if i:
                    act.wait_ge(S("norm_sum"), NT * (s - 1) + i)
                r = st[:, ST_SS + i:ST_SS + i + 1]
                af(dst, x_res[:, i, :], ACT.Square, accum_out=r).then_inc(S("norm_sum"), 1)
                act.wait_ge(S("norm_sum"), NT * (s - 1) + i + 1)
                af(r, r, ACT.Sqrt, scale=1.0 / D, bias=eps[:, 0:1]).then_inc(S("norm_root"), 1)

            def norm_rows(s, i):
                act.wait_ge(S("norm_inv"), NT * (s - 1) + i + 1)
                dst = xs[:, i, :] if s == 4 else xn[:, i % 2, :]
                if s < 4 and i >= 2:
                    act.wait_ge(S("norm_low"), NT * (s - 1) + i - 1)
                af(dst, x_res[:, i, :], ACT.Copy, scale=st[:, ST_SS + i:ST_SS + i + 1]).then_inc(S("xn_ready"), 1)

            def norm_high(s, i):
                y = (y4 if s == 4 else xn[:, i % 2, :]).rearrange("p (k n) -> p k n", n=P)
                act.wait_ge(S("norm_out"), NT * (s - 1) + i + 1)
                af(r32(actT[:, :, i * P:(i + 1) * P]), y, ACT.Copy).then_inc(S("norm_high"), 1)

            act.wait_ge(S("constants"), 1)
            for i in range(NT):
                squares(1, i, junk, S(f"x_in{i}"), 16)
            act.wait_ge(S("small_in"), 16 * N_SMALL)
            af(silu_c[:], col("c_2", 0, KD), ACT.Silu).then_inc(S("silu_c"), 1)
            act.wait_ge(S("att_count"), 1)
            af(att_bias, cnt_t, ACT.Ln).then_inc(S("att_log"), 1)
            af(s5_s[:, 0, :], par[:, 0, :], ACT.Exp).then_inc(S("s5_dt"), 1)
            act.wait_ge(S("s5_pow"), 1)
            step(af(pw_l, pw_l, ACT.Exp))
            step(af(pw_i, pw_th, ACT.Sin))
            af(pw_r, pw_t, ACT.Sin).then_inc(S("s5_sin"), 1)
            act.wait_ge(S("s5_ang"), 1)
            af(turn[:, 1], ang_r, ACT.Sin).then_inc(S("s5_turn"), 1)
            act.wait_ge(S("s5_ang"), 2)
            af(turn[:, 0], ang_r, ACT.Sin).then_inc(S("s5_turn"), 1)
            act.wait_ge(S("s5_turn"), 3)
            act.dma_start(turn_dram, turn.rearrange("p a b c -> p (a b c)")).then_inc(S("turn_stored"), 16)
            for q8 in range(2):
                for n in range(PIECE // 256):
                    act.dma_start(s5_dram[q8][:, n * 256:(n + 1) * 256], zero[:]).then_inc(S("toeplitz_zero"), 16)
            act.wait_ge(S("ca_ready"), 1)
            for q8 in range(2):
                ro = s5_dram[q8][:, PIECE:].rearrange("p (q r n) -> p q r n", q=8, r=2)
                for ri, ca in enumerate((ca_r, ca_n)):
                    act.dma_start(ro[:, :, ri, :], ca[:, 8 * q8:8 * q8 + 8, 1:NPOW, :].rearrange("p q t h -> p q (t h)"))\
                        .then_inc(S("s5_const"), 16)
            for c in range(NADA):
                row = slice(32 * (c % 4), 32 * (c % 4) + 1)
                ins = af(mod_row[row, c // 4, :], full(act, ("ada", c // 4))[row, :], ACT.Copy)
                if c % 4 == 3:
                    out_of(("ada", c // 4), ins)
            act.wait_ge(S("turn_stored"), 16)
            for i in range(NT):
                norm_rows(1, i)
                if i:
                    norm_high(1, i - 1)
            norm_high(1, NT - 1)
            for n in range(8):
                dst = inject.rearrange("p q r n -> p (q r) n")[:, 4 * n:4 * n + 4, :]
                src = full(act, ("s5b", n)).rearrange("p (a n) -> p a n", a=4)
                out_of(("s5b", n), af(dst, src, ACT.Copy))
            for n in range(8):
                copied(act, ("s5b", n))
            act.dma_start(inject_dram, inject.rearrange("p q r n -> p (q r n)")).then_inc(S("s5_const"), 16)
            act.wait_ge(S("taps_ready"), 1)
            act.wait_ge(S("toeplitz_zero"), 16 * 2 * (PIECE // 256))
            for q8 in range(2):
                tz = s5_dram[q8][:, 0:PIECE].rearrange("p (g n) -> p g n", g=NQ)
                tp = taps[0:SC, q8].rearrange("p r q n -> p (r q) n")
                for j in range(SL):
                    act.dma_start(tz[j * SC:(j + 1) * SC, :, j * SC:P], tp[:, :, 0:P - j * SC]).then_inc(S("s5_const"), 16)
            act.wait_ge(S("s5_const"), 16 * N_S5)

            for m in range(4):
                out_of(("xr", m), af(xr[:, m, :], full(act, ("xr", m)), ACT.Copy))
            for m in range(4):
                out_of(("gr", m), af(gr[:, m, :], full(act, ("gr", m)), ACT.Gelu_apprx_tanh))
            for m in range(4):
                out_of(("q", m), af(qT[:, m, :], full(act, ("q", m)), ACT.Copy, scale=DH ** -0.5))
            for m in range(4):
                out_of(("k", m), af(kT[:, m, :], full(act, ("k", m)), ACT.Copy))
            for m in range(4):
                out_of(("v", m), af(v[:, m, :], full(act, ("v", m)), ACT.Copy))
            act.wait_ge(S("lam_ready"), 1)
            af(lam(1), lam(0), ACT.Exp, scale=-1.0).then_inc(S("lam_act"), 1)
            act.wait_ge(S("lam_ready"), 2)
            af(lam(3), lam(2), ACT.Ln).then_inc(S("lam_act"), 1)
            for m in range(NL):
                out_of(("gate", 0, m), af(lru_a[:, m, :], full(act, ("gate", 0, m)), ACT.Sigmoid,
                                          bias=col("b_rgate", m)))
                out_of(("gate", 1, m), af(xr[:, m, :], full(act, ("gate", 1, m)), ACT.Sigmoid,
                                          bias=col("b_igate", m)))
            act.wait_ge(S("lam_ready"), 3)
            for m in range(NL):
                copied(act, ("gate", 0, m))
                step(af(lru_u[:, m, :], lru_a[:, m, :], ACT.Tanh, scale=lam(1)[:, m:m + 1]))
                af(lru_a[:, m, :], lru_a[:, m, :], ACT.Exp, scale=lam(0)[:, m:m + 1]).then_inc(S("lru_decay"), 1)
            def probs(n):
                i, h = divmod(n, HEADS)
                act.wait_ge(S("att_max"), n + 1)
                s_row, d = att_s[:, h % 4, 0:(i + 1) * P], ST_DEN + 8 * (i % 2) + h
                af(s_row, s_row, ACT.Exp, bias=st[:, ST_MX + 8 + h:ST_MX + 9 + h], accum_out=st[:, d:d + 1])\
                    .then_inc(S("att_exp"), 1)

            def rows_high(i):
                bank = full(act, ("at", i)).rearrange("p (m n) -> p m n", m=4)
                af(r32(actT[:, 0:4, i * P:(i + 1) * P]), bank, ACT.Copy).then_inc(S("at_high"), 1)

            probs(0)
            for n in range(NT * HEADS):
                if n + 1 < NT * HEADS:
                    probs(n + 1)
                i, h = divmod(n, HEADS)
                out_of(("pt", i, h), af(att_pt[:, h % 2, 0:i + 1, :],
                                        full(act, ("pt", i, h))[:, 0:(i + 1) * P].rearrange("p (j n) -> p j n", n=P),
                                        ACT.Copy))
                if n >= HEADS and n % HEADS == 2:
                    rows_high(n // HEADS - 1)
                if n == HEADS:
                    for m in range(NL):
                        act.wait_ge(S("lru_square"), m + 1)
                        af(lru_u[:, m, :], lru_u[:, m, :], ACT.Sqrt).then_inc(S("lru_root"), 1)
            rows_high(NT - 1)

            def post_squares(s, i, key):
                c = [st[:, ST_PS + 2 * i + n:ST_PS + 2 * i + n + 1] for n in range(2)]
                for n in range(2):
                    bank = full(act, key(i, n))
                    step(af(junk[:, 0:HALF], bank, ACT.Square, scale=D ** -0.5, accum_out=c[n]))
                step(af(c[0], c[0], ACT.Identity, bias=eps[:, 0:1]))
                af(c[1], c[1], ACT.Sqrt, bias=c[0]).then_inc(S("post_root"), 1)

            def post_and_norm(s, key, dst, done):
                post_squares(s, 0, key)
                for i in range(NT):
                    if i + 1 < NT:
                        post_squares(s, i + 1, key)
                    squares(s + 1, i, dst, S(done), i + 1)
                    if i >= 2:
                        norm_high(s + 1, i - 2)
                    norm_rows(s + 1, i)
                for i in (NT - 2, NT - 1):
                    norm_high(s + 1, i)

            def help_split(n):
                act.wait_ge(S(f"piece_in{n % 2}"), 16 * (n // 2 + 1))
                act.wait_ge(S("split_used"), used_count(n - 2))
                act.wait_ge(S("split_ready"), n)
                af(r32(part(n, 0)), piece(n % 2), ACT.Copy).then_inc(S("split_high"), 1)

            post_and_norm(1, lambda i, n: ("wo", 1, i, n), junk, "x_mix1")
            help_split(helped[0])
            for m in range(NF):
                copied(act, ("f1", m))
                af(hidT[:, m, :], hidT[:, m, :], ACT.Square).then_inc(S("hid_ready"), 1)
            post_and_norm(2, lambda i, n: ("f2", i, n), junk, "x_mlp")
            help_split(helped[1])

            for m in range(2):
                out_of(("gq", m), af(gq[:, m, :], full(act, ("gq", m)), ACT.Copy, scale=GDK ** -0.5))
            for m in range(2):
                out_of(("gq", 2 + m), af(gk[:, m, :], full(act, ("gq", 2 + m)), ACT.Copy))
            for m in range(4):
                out_of(("u", m), af(uT[:, m, :].rearrange("p (j c) -> p j c", j=SL),
                                    full(act, ("u", m)).rearrange("p (c j) -> p j c", j=SL), ACT.Copy))
            for m in range(4):
                copied(act, ("u", m))
                act.dma_start(u_dram[m * P:(m + 1) * P, :], uT[:, m, :]).then_inc(S("u_stored"), 16)
            act.dma_start(s5_turn.rearrange("p a b c -> p (a b c)"), turn_dram).then_inc(S("turn_in"), 16)
            out_of("a16", af(a16[0:16, :], full(act, "a16")[0:16, :], ACT.Copy))
            act.wait_ge(S("u_stored"), 16 * 4)
            ud = u_dram.rearrange("(g h) (j c) -> j h g c", h=SC, j=SL)
            for j in range(SL):
                act.dma_start(s5_u[j * SC:(j + 1) * SC, :, :], ud[j]).then_inc(S("u_in"), 16)
            act.wait_ge(S("gla_abs"), 1)
            step(af(g_b, g_b, ACT.Exp, scale=-1.0))
            af(g_b, g_b, ACT.Ln, bias=1.0).then_inc(S("gla_log"), 1)
            act.wait_ge(S("gla_cum"), 1)
            step(af(g_e, g_b, ACT.Exp, scale=-1.0 / TAU))
            af(g_t, g_b, ACT.Exp, scale=1.0 / TAU).then_inc(S("gla_exp"), 1)
            for i in range(NT):
                out_of(("gv", i), af(gv[:, i, :], full(act, ("gv", i)), ACT.Copy))
            for i in range(NT):
                out_of(("og", i), af(og[:, i, :], full(act, ("og", i)), ACT.Silu))
            for q8 in range(2):
                for par_ in range(2):
                    bank = full(act, ("Y", par_, q8))
                    dst = s5_y.rearrange("p (q r) c -> p q r c", r=2)[:, q8 * 8:(q8 + 1) * 8, par_, :]
                    out_of(("Y", par_, q8), af(dst, bank.rearrange("p (q c) -> p q c", q=8), ACT.Copy))
            for par_ in range(2):
                for q8 in range(2):
                    copied(act, ("Y", par_, q8))
            yd = y_dram.rearrange("(g h) (j c) -> j h g c", h=SC, j=SL)
            for j in range(SL):
                act.dma_start(yd[j], s5_y[j * SC:(j + 1) * SC, :, :]).then_inc(S("y5_stored"), 16)
            for i in range(NT):
                for par_ in range(2):
                    bank = full(act, ("go", i, par_))
                    for hh in range(2):
                        c = ST_GR + 4 * i + 2 * par_ + hh
                        step(af(a16[:, 0:GDV], bank[:, hh * GDV:(hh + 1) * GDV], ACT.Square,
                                accum_out=st[:, c:c + 1]))
                r = st[:, ST_GR + 4 * i:ST_GR + 4 * i + 4]
                af(r, r, ACT.Sqrt, scale=1.0 / GDV, bias=eps[:, 0:1]).then_inc(S("gla_root"), 1)
            for i in range(NT):
                bank = full(act, ("gt", i)).rearrange("p (m n) -> p m n", m=4)
                af(r32(actT[:, 0:4, i * P:(i + 1) * P]), bank, ACT.Copy).then_inc(S("gt_high"), 1)
            act.wait_ge(S("y5_in"), 16)
            for m in range(4):
                af(yT[:, m, :], yT[:, m, :], ACT.Gelu_apprx_tanh).then_inc(S("y5_gelu"), 1)
            for m in range(4):
                bank = full(act, ("glu", m))
                if m >= 2:
                    act.wait_ge(S("s5_out"), m - 1)
                out_of(("glu", m), af(sig[:, m % 2, :], bank, ACT.Sigmoid, bias=col("s5_glu_b_2", m)))
            post_and_norm(3, lambda i, n: ("wo", 2, i, n), junk4, "x_mix2")
            for i in range(NT):
                act.wait_ge(S("xn_ready"), 3 * NT + i + 1)
                act.dma_start(xs_dram[i * P:(i + 1) * P, :], xs[:, i, :]).then_inc(S("xs_stored"), 16)
            act.wait_ge(S("top_diff"), 1)
            af(gate[:], gate[:], ACT.Exp).then_inc(S("top_exp"), 1)
            full(act, ("lg", NT - 1))

            def high_part(b, x):
                o = place(b, x)
                act.wait_ge(S(f"raw_in{o % RAW}"), 16 * (2 * b + o // RAW + 1))
                first, second = isinstance(b, int) and b == 0, isinstance(b, int) and b == 1
                if not first or x >= SPLIT:
                    if (o - SPLIT) % 2 == 0:
                        act.wait_ge(S("part_used"), 6 * b + (o - SPLIT) // 2 + 1)
                    elif x >= SPLIT:
                        act.wait_ge(S("gu_full"), 4 * b + (x - SPLIT) // 2 + 1)
                    elif second:
                        act.wait_ge(S("gu_full"), (x + SPLIT) // 2 + 1)
                    else:
                        act.wait_ge(S("dn_full"), 2 * b + x // 2 - 3)
                af(r32(halves(o % SPLIT)[0]), raw(o % RAW), ACT.Copy).then_inc(S("high"), 1)

            for x in range(4):
                high_part(0, x)
            act.wait_ge(S("blocks_known"), 1)
            n_blocks = NE + act.value_load(blk_e[0:1, 63:64], min_val=0, max_val=MAX_EXTRA)

            def input_out(b):
                act.wait_ge(S("xgT_full"), b + 1)
                for k in range(KD):
                    ins = af(xT[:, k, :], ps[:, 6 + k // 4, (k % 4) * P:(k % 4 + 1) * P], ACT.Identity,
                             scale=st[:, ST_MOD + 8 + k:ST_MOD + 9 + k], bias=col("ada_b_2", 3 * KD + k))
                ins.then_inc(S("xgT_ready"), 1)

            def gates(b, hf):
                act.wait_ge(S("sw_gate"), 2 * b + hf + 1)
                if not (isinstance(b, int) and b == 0) or hf:
                    act.wait_ge(S("sw_done"), 2 * b + hf)
                af(sw_s, sw_g, ACT.Sigmoid, scale=SWI_ALPHA).then_inc(S("sw_sig"), 1)

            def hidden_out(b):
                act.wait_ge(S("hT_full"), b + 1)
                for half in range(2):
                    ins = af(r32(hT_h[:, 4 * half:4 * half + 4, :]), ps[:, 6 + half, :].rearrange("p (k s) -> p k s", k=4),
                             ACT.Copy)
                ins.then_inc(S("hT_high"), 1)

            def store(b):
                act.wait_ge(S("y_done"), 2 * b + 3)
                act.dma_start(y_slots[bass.ds(b * P, P), :], y_row).then_inc(S("y_stored"), 16)

            def loop_turn(b):
                if isinstance(b, int) and b == 0:
                    input_out(0)
                else:
                    for x in range(4):
                        high_part(b, x)
                    hidden_out(b - 1)
                    if not isinstance(b, int):
                        store(b - 2)
                for x in range(4, 8):
                    high_part(b, x)
                gates(b, 0)
                if not (isinstance(b, int) and b == 0):
                    for x in range(8, 12):
                        high_part(b, x)
                gates(b, 1)
                input_out(b + 1)

            act.sem_inc(S("y_stored"), 16)
            loop_turn(0)
            loop_turn(1)
            with act.Fori(2, n_blocks) as b:
                loop_turn(b)
            for x in range(4):
                high_part(n_blocks, x)
            hidden_out(n_blocks - 1)
            store(n_blocks - 2)
            store(n_blocks - 1)
            for i in range(NT):
                act.wait_ge(S("ff_ready"), i + 1)
                r = st[:, ST_SS + i:ST_SS + i + 1]
                step(af(junk4, ff[:, i, :], ACT.Square, accum_out=r))
                af(r, r, ACT.Sqrt, scale=1.0 / D, bias=eps[:, 0:1]).then_inc(S("ff_root"), 1)
            act.wait_ge(S("ff_root"), NT)

        @block.vector
        def _(dve):
            step = stepper(dve, "dve_step")
            tt, ts, stt = nc.vector.tensor_tensor, nc.vector.tensor_scalar, nc.vector.scalar_tensor_tensor
            cp, scan = nc.vector.tensor_copy, nc.vector.tensor_tensor_scan

            dve.wait_ge(S("constants"), 1)
            step(cp(gla_mask, mask_f))
            step(cp(step_f[:], step_i))

            def norm_inverse(s, i):
                r = st[:, ST_SS + i:ST_SS + i + 1]
                dve.wait_ge(S("norm_root"), NT * (s - 1) + i + 1)
                nc.vector.reciprocal(r, r).then_inc(S("norm_inv"), 1)

            def norm_out(s, i, gain, shift=None):
                y = (y4 if s == 4 else xn[:, i % 2, :]).rearrange("p (k n) -> p k n", n=P)
                if s == 4 and i:
                    dve.wait_ge(S("norm_low"), NT * (s - 1) + i)
                tile = slice(i * P, (i + 1) * P)
                for h in range(2):
                    full(dve, ("norm", s, i, h))
                for h in range(2):
                    key = ("norm", s, i, h)
                    bank = ps[:, plan[key][0], :].rearrange("p (k n) -> p k n", n=P)
                    out_of(key, tt(y[:, 4 * h:4 * h + 4], bank, over(gain[:, 4 * h:4 * h + 4], 2, P), ALU.mult))
                for h in range(2):
                    copied(dve, ("norm", s, i, h))
                if shift is not None:
                    tt(y, y, over(shift, 2, P), ALU.add).then_inc(S("norm_out"), 1)
                else:
                    dve.sem_inc(S("norm_out"), 1)
                dve.wait_ge(S("norm_high"), NT * (s - 1) + i + 1)
                tt(r32(actL[:, :, tile]), y, actT[:, :, tile], ALU.subtract).then_inc(S("norm_low"), 1)

            dve.wait_ge(S("small_in"), 16 * N_SMALL)
            for bits, dst in ((15, cnt), (3, cnt_t)):
                step(ts(dist_i, dist, bits, None, ALU.bitwise_and))
                step(ts(dst, dist_i, 0.0, None, ALU.is_equal))
            step(tt(cnt, cnt, cnt_t, ALU.add))
            step(ts(cnt_t, dist, float(P), None, ALU.is_le))
            step(tt(cnt, cnt, cnt_t, ALU.add))
            step(ts(cnt_t, dist, 0.0, None, ALU.is_ge))
            step(tt(cnt, cnt, cnt_t, ALU.mult))
            ts(cnt_t, cnt, 1.0, None, ALU.max).then_inc(S("att_count"), 1)
            step(ts(cnt, cnt, 0.0, NEG, ALU.is_equal, ALU.mult))
            dve.wait_ge(S("att_log"), 1)
            step(tt(att_bias, att_bias, cnt, ALU.add))

            def reduced(dst, src, k, quarter):
                step(ts(k, src, 1.0 / TWO_PI, 0.25 * quarter, ALU.mult, ALU.add))
                step(ts(k, k, ROUND, None, ALU.add))
                step(ts(k, k, -ROUND, None, ALU.add))
                step(stt(dst, k, -PI_A, src, ALU.mult, ALU.add))
                step(stt(dst, k, -PI_B, dst, ALU.mult, ALU.add))
                step(stt(dst, k, -PI_C, dst, ALU.mult, ALU.add))
                if quarter:
                    step(ts(dst, dst, 0.5 * math.pi, None, ALU.add))
                return ts(dst, dst, PI_MAX, -PI_MAX, ALU.min, ALU.max)

            dt, s1, s2, s3, s4, s5, _ = (s5_s[:, n, :] for n in range(7))
            lr, li = par[:, 1, :], par[:, 2, :]
            dve.wait_ge(S("s5_dt"), 1)
            step(tt(s1, lr, dt, ALU.mult))
            step(tt(s2, li, dt, ALU.mult))
            step(reduced(s3, s2, s4, 0))
            taus = over(step_f[:, 0:NPOW], 2, NQ)
            step(tt(pw_l[:, 0:NPOW], taus, over(s1, 1, NPOW), ALU.mult))
            step(tt(pw_k[:, 0:NPOW], taus, over(s3, 1, NPOW), ALU.mult))
            step(reduced(pw_t[:, 0:NPOW], pw_k[:, 0:NPOW], pw_i[:, 0:NPOW], 1))
            reduced(pw_th[:, 0:NPOW], pw_k[:, 0:NPOW], pw_i[:, 0:NPOW], 0).then_inc(S("s5_pow"), 1)
            dve.wait_ge(S("s5_sin"), 1)
            ar, ai = pw_r, pw_i
            step(tt(ar[:, 0:NPOW], ar[:, 0:NPOW], pw_l[:, 0:NPOW], ALU.mult))
            step(tt(ai[:, 0:NPOW], ai[:, 0:NPOW], pw_l[:, 0:NPOW], ALU.mult))
            step(tt(ang, over(pw_th[:, SL, :], 2, SNC), over(step_f[:], 1, NQ), ALU.mult))
            reduced(ang_r, ang, ang_k, 0).then_inc(S("s5_ang"), 1)
            step(cp(turn[:, 2], over(pw_l[:, SL, :], 2, SNC)))
            nc.vector.memset(turn[:, 2, :, 0:1], 0.0).then_inc(S("s5_turn"), 1)
            dve.wait_ge(S("s5_turn"), 2)
            reduced(ang_r, ang, ang_k, 1).then_inc(S("s5_ang"), 1)
            step(tt(s1, lr, lr, ALU.mult))
            step(tt(s2, li, li, ALU.mult))
            step(tt(s1, s1, s2, ALU.add))
            step(nc.vector.reciprocal(s1, s1))
            step(ts(s2, ar[:, 1, :], -1.0, None, ALU.add))
            step(tt(s3, s2, lr, ALU.mult))
            step(tt(s4, ai[:, 1, :], li, ALU.mult))
            step(tt(s3, s3, s4, ALU.add))
            step(tt(s3, s3, s1, ALU.mult))
            step(tt(s4, ai[:, 1, :], lr, ALU.mult))
            step(tt(s5, s2, li, ALU.mult))
            step(tt(s4, s4, s5, ALU.subtract))
            step(tt(s4, s4, s1, ALU.mult))
            fr, fi = over(s3, 2, SC), over(s4, 2, SC)
            step(tt(bb_r, fr, b_r, ALU.mult))
            step(tt(bb_t, fi, b_i, ALU.mult))
            step(tt(bb_r, bb_r, bb_t, ALU.subtract))
            step(tt(bb_i, fr, b_i, ALU.mult))
            step(tt(bb_t, fi, b_r, ALU.mult))
            step(tt(bb_i, bb_i, bb_t, ALU.add))
            c9r, c9i = over(c_r, 2, NPOW), over(c_i, 2, NPOW)
            a9r, a9i = (over(x[:, 0:NPOW].rearrange("p t q -> p q t"), 3, SC) for x in (ar, ai))
            step(tt(ca_r, c9r, a9r, ALU.mult))
            step(tt(ca_t, c9i, a9i, ALU.mult))
            step(tt(ca_r, ca_r, ca_t, ALU.subtract))
            step(tt(ca_n, c9r, a9i, ALU.mult))
            step(tt(ca_t, c9i, a9r, ALU.mult))
            step(stt(ca_n, ca_n, -1.0, ca_t, ALU.mult, ALU.subtract))
            for j in range(SL):
                cp(pw_t[:, j, :], ar[:, SL - 1 - j, :])
                ins = cp(pw_th[:, j, :], ai[:, SL - 1 - j, :])
            ins.then_inc(S("ca_ready"), 1)
            dve.wait_ge(S("ca_ready"), 1)
            dve.wait_ge(S("s5_turn"), 3)
            b8r, b8i = over(bb_r, 2, SL), over(bb_i, 2, SL)
            a8r, a8i = (over(x[:, 0:SL].rearrange("p t q -> p q t"), 3, SC) for x in (pw_t, pw_th))
            tmp8 = ca_t[:, :, 0:SL, :]
            step(tt(bx_r, b8r, a8r, ALU.mult))
            step(tt(tmp8, b8i, a8i, ALU.mult))
            step(tt(bx_r, bx_r, tmp8, ALU.subtract))
            step(tt(bx_i, b8r, a8i, ALU.mult))
            step(tt(tmp8, b8i, a8r, ALU.mult))
            tt(bx_i, bx_i, tmp8, ALU.add).then_inc(S("bx_ready"), 1)
            gain = col("mix_norm_pre", 0, KD)
            norm_inverse(1, 0)
            for i in range(1, NT):
                norm_inverse(1, i)
                norm_out(1, i - 1, gain)
            norm_out(1, NT - 1, gain)

            mod = col("ada_b_2", 0, 6 * KD)
            by_row_x = mod.rearrange("p (x j m) -> p x m j", j=4, m=4)
            for x in range(NADA // 4):
                bank = full(dve, ("mod", x)).rearrange("p (m j z) -> p m j z", m=4, j=4)[:, :, :, 0]
                out_of(("mod", x), tt(by_row_x[:, x], bank, by_row_x[:, x], ALU.add))
            for x in range(NADA // 4):
                copied(dve, ("mod", x))
            for s, name in enumerate(("mix_pre_g_2", "ffn_pre_g_2")):
                step(stt(st[:, ST_MOD + KD * s:ST_MOD + KD * (s + 1)], mod[:, (3 * s + 1) * KD:(3 * s + 2) * KD], 1.0,
                         col(name, 0, KD), ALU.add, ALU.mult))
            for s, name in enumerate(("mix_post_g_2", "ffn_post_g_2")):
                step(tt(st[:, ST_PG + KD * s:ST_PG + KD * (s + 1)], mod[:, (3 * s + 2) * KD:(3 * s + 3) * KD],
                        col(name, 0, KD), ALU.mult))

            for par_ in range(2):
                for q4 in range(4):
                    key = ("s5k", par_, q4)
                    bank = full(dve, key)[0:SC, :].rearrange("p (q n) -> p q n", q=4)
                    out_of(key, cp(taps[0:SC, q4 // 2, par_, 4 * (q4 % 2):4 * (q4 % 2) + 4, :], bank))
            for par_ in range(2):
                for q4 in range(4):
                    copied(dve, ("s5k", par_, q4))
            direct = ca_t.rearrange("p q t h -> p (q t h)")[0:SC, 0:SG * SC].rearrange("p (g h) -> p g h", g=SG)
            first = taps.rearrange("p e r q n -> p (e r q) n")[0:SC, :, 0:SC]
            step(tt(direct, over(ident[0:SC, 0:SC], 1, SG), over(s5_d[:], 2, SC), ALU.mult))
            tt(first, first, direct, ALU.add).then_inc(S("taps_ready"), 1)

            for m in range(NL):
                copied(dve, ("xr", m))
                w = lambda t: col("conv_w", 4 * t + m)
                step(ts(xc[:, m, :], xr[:, m, :], w(CONV - 1), col("conv_b", m), ALU.mult, ALU.add))
                for t in range(CONV - 1):
                    back = CONV - 1 - t
                    ins = stt(xc[:, m, back:], xr[:, m, 0:T - back], w(t), xc[:, m, back:], ALU.mult, ALU.add)
                    if t < CONV - 2:
                        step(ins)
                ins.then_inc(S("conv_ready"), 1)
            lm = col("lru_lambda", 0, NL)
            step(ts(lam(5), lm, -1.0, None, ALU.mult))
            tt(lam(0), lm, lam(5), ALU.max).then_inc(S("lam_ready"), 1)
            dve.wait_ge(S("lam_act"), 1)
            ts(lam(2), lam(1), 1.0, None, ALU.add).then_inc(S("lam_ready"), 1)
            dve.wait_ge(S("lam_ready"), 2)
            step(ts(lam(4), lam(2), -1.0, None, ALU.add))
            step(ts(lam(5), lam(4), 0.0, None, ALU.is_equal))
            step(tt(lam(4), lam(4), lam(5), ALU.add))
            step(nc.vector.reciprocal(lam(4), lam(4)))
            step(tt(lam(4), lam(4), lam(1), ALU.mult))
            step(tt(lam(5), lam(5), lam(1), ALU.mult))
            dve.wait_ge(S("lam_act"), 2)
            step(tt(lam(3), lam(3), lam(4), ALU.mult))
            step(tt(lam(3), lam(3), lam(5), ALU.add))
            step(ts(lam(6), lm, -1.0, 0.0, ALU.mult, ALU.max))
            step(tt(lam(6), lam(6), lam(3), ALU.add))
            step(ts(lam(0), lam(6), -LRU_C, None, ALU.mult))
            ts(lam(1), lam(6), LRU_C, None, ALU.mult).then_inc(S("lam_ready"), 1)
            def recurrence(m):
                copied(dve, ("gate", 1, m))
                step(tt(xr[:, m, :], xr[:, m, :], xc[:, m, :], ALU.mult))
                dve.wait_ge(S("lru_root"), m + 1)
                step(tt(lru_u[:, m, :], lru_u[:, m, :], xr[:, m, :], ALU.mult))
                step(scan(xc[:, m, :], lru_a[:, m, :], lru_u[:, m, :], 0.0, ALU.mult, ALU.add))
                copied(dve, ("gr", m))
                step(tt(xc[:, m, :], xc[:, m, :], gr[:, m, :], ALU.mult))
                step(cp(r32(actT[:, 4 + m, :]), xc[:, m, :]))
                tt(r32(actL[:, 4 + m, :]), xc[:, m, :], actT[:, 4 + m, :], ALU.subtract).then_inc(S("rec_ready"), 1)

            mx, nmx = st[:, ST_MX:ST_MX + 8], st[:, ST_MX + 8:ST_MX + 16]
            rden = st[:, ST_RDEN:ST_RDEN + 8]

            def low_parts(name, i):
                tile, key = slice(i * P, (i + 1) * P), (name, i)
                dve.wait_ge(S(f"{name}_high"), i + 1)
                bank = ps[:, plan[key][0], :].rearrange("p (m n) -> p m n", m=4)
                out_of(key, tt(r32(actL[:, 0:4, tile]), bank, actT[:, 0:4, tile], ALU.subtract))

            def maximum(n):
                i, h = divmod(n, HEADS)
                keys_n = (i + 1) * P
                bias = att_bias[:, NT - 1 - i:NT, :].rearrange("p r n -> p (r n)")
                if n >= 4:
                    full(dve, ("pt", *divmod(n - 4, HEADS)))
                key = ("s", i, h)
                bank = full(dve, key)
                out_of(key, nc.vector.tensor_tensor_reduce(
                    out=att_s[:, h % 4, 0:keys_n], in0=bank[:, 0:keys_n], in1=bias, scale=1.0, scalar=NEG,
                    op0=ALU.add, op1=ALU.max, accum_out=mx[:, h:h + 1]))
                copied(dve, key)
                ts(nmx[:, h:h + 1], mx[:, h:h + 1], -1.0, None, ALU.mult).then_inc(S("att_max"), 1)

            def divide(i):
                den = st[:, ST_DEN + 8 * (i % 2):ST_DEN + 8 * (i % 2) + 8]
                dve.wait_ge(S("att_exp"), HEADS * (i + 1))
                step(nc.vector.reciprocal(rden, den))
                if i:
                    full(dve, ("at", i - 1))
                bank = full(dve, ("o", i))
                out_of(("o", i), tt(att_row.rearrange("p (h d) -> p h d", h=HEADS),
                                    bank.rearrange("p (h d) -> p h d", h=HEADS), over(rden, 2, DH), ALU.mult))

            def square(m):
                lru_t = view(3584, T)
                if m:
                    dve.wait_ge(S("lru_square"), m)
                dve.wait_ge(S("lru_decay"), m + 1)
                step(tt(lru_t, lru_a[:, m, :], lru_a[:, m, :], ALU.mult))
                stt(lru_u[:, m, :], lru_t, 1.0, lru_u[:, m, :], ALU.add, ALU.mult).then_inc(S("lru_square"), 1)

            for n in range(NT * HEADS):
                maximum(n)
                if n >= HEADS and n % HEADS == 2:
                    divide(n // HEADS - 1)
                if n >= HEADS and n % HEADS == 6:
                    low_parts("at", n // HEADS - 1)
                if n < NL:
                    square(n)
                elif n >= 12 and n % 4 == 0 and n < 28:
                    recurrence((n - 12) // 4)
            divide(NT - 1)
            low_parts("at", NT - 1)

            def post(s, i, key, gain, done):
                r = st[:, ST_PS + 2 * i + 1:ST_PS + 2 * i + 2]
                dve.wait_ge(S("post_root"), NT * (s - 1) + i + 1)
                step(nc.vector.reciprocal(r, r))
                for n in range(2):
                    half = slice(n * HALF, (n + 1) * HALF)
                    out_of(key(i, n), stt(post_tmp[:, n, :], ps[:, plan[key(i, n)][0], :], r, gain[:, half],
                                          ALU.mult, ALU.mult))
                for n in range(2):
                    copied(dve, key(i, n))
                tt(x_res[:, i, :], x_res[:, i, :], post_tmp.rearrange("p n d -> p (n d)"), ALU.add).then_inc(S(done), 1)
                dve.wait_ge(S(done), i + 1)

            def post_and_norm(s, key, post_gain, done, gain, shift=None):
                post(s, 0, key, post_gain, done)
                for i in range(NT):
                    norm_inverse(s + 1, i)
                    if i + 1 < NT:
                        post(s, i + 1, key, post_gain, done)
                    if i:
                        norm_out(s + 1, i - 1, gain, shift)
                norm_out(s + 1, NT - 1, gain, shift)

            post_and_norm(1, lambda i, n: ("wo", 1, i, n), post_g[:, 0, :], "x_mix1", col("mlp_norm_pre", 0, KD))
            for m in range(NF):
                out_of(("f1", m), ts(hidT[:, m, :], full(dve, ("f1", m)), 0.0, None, ALU.max))
            full(dve, ("f1", NF - 1))
            for kk in range(NF):
                dve.wait_ge(S("hid_ready"), kk + 1)
                if kk >= 4:
                    dve.wait_ge(S("split_used"), used_count(piece_no["ff_out", (kk - 4) // 4, (kk - 4) // 2 % 2]))
                step(cp(r32(hid_h[:, kk % 4, :]), hidT[:, kk, :]))
                tt(r32(hid_l[:, kk % 4, :]), hidT[:, kk, :], hid_h[:, kk % 4, :], ALU.subtract)\
                    .then_inc(S("hid_split"), 1)
            post_and_norm(2, lambda i, n: ("f2", i, n), post_g[:, 1, :], "x_mlp", st[:, ST_MOD:ST_MOD + KD], mod[:, 0:KD])
            for s in range(2):
                for k in range(KD):
                    ins = ts(diag[s][:, k, :], ident[:], st[:, ST_PG + KD * s + k:ST_PG + KD * s + k + 1], None, ALU.mult)
                ins.then_inc(S("diag_ready"), 1)
            for s in range(2):
                for n in range(2):
                    out_of(("pg", s, n), cp(post_g[:, s, n * HALF:(n + 1) * HALF], full(dve, ("pg", s, n))))

            for m in range(2):
                out_of(("za", m), ts(g_t[:, m, :], full(dve, ("za", m)), col("b_alpha_2", m), None, ALU.add))
            for m in range(2):
                copied(dve, ("za", m))
            stt(g_b, g_t, -1.0, g_t, ALU.mult, ALU.max).then_inc(S("gla_abs"), 1)
            dve.wait_ge(S("gla_abs"), 1)
            step(ts(g_t, g_t, -1.0, 0.0, ALU.mult, ALU.max))
            dve.wait_ge(S("gla_log"), 1)
            step(tt(g_t, g_t, g_b, ALU.add))
            step(scan(g_b[:, 0, :], chunk_go[:], g_t[:, 0, :], 0.0, ALU.mult, ALU.add))
            scan(g_b[:, 1, :], chunk_go[:], g_t[:, 1, :], 0.0, ALU.mult, ALU.add).then_inc(S("gla_cum"), 1)
            dve.wait_ge(S("gla_exp"), 1)
            for m in range(4):
                copied(dve, ("gq", m))
            step(tt(gq, gq, g_e, ALU.mult))
            step(tt(gk, gk, g_t, ALU.mult))
            dec = st[:, ST_DEC:ST_DEC + 2 * NCH]
            step(cp(dec.rearrange("p (m c) -> p m c", m=2), g_e[:, :, CH - 1::CH]))
            ends = lambda x: x.rearrange("p m (c t) -> p (m c) t", t=CH)
            tt(ends(g_end), ends(gk), over(dec, 2, CH), ALU.mult).then_inc(S("gla_keys"), 1)
            for q8 in range(2):
                for ri in range(2):
                    key = ("D", ri, q8)
                    out_of(key, cp(s5_x[ri][:, q8 * 8:(q8 + 1) * 8, :],
                                   full(dve, key).rearrange("p (q c) -> p q c", q=8)))
            full(dve, ("og", NT - 1))
            step(nc.vector.memset(g_sT, 0.0))
            for i in range(NT):
                out_of(("ke", i), cp(g_endr[:, i, :], full(dve, ("ke", i))[:, 0:GH * GDK]))
            for h in range(GH):
                out_of(("gs", h), nc.vector.copy_predicated(g_sT[:, h, :], gla_mask.rearrange("p i n -> p (i n)"),
                                                            full(dve, ("gs", h))))
            for ri in range(2):
                for q8 in range(2):
                    copied(dve, ("D", ri, q8))
            dve.wait_ge(S("turn_in"), 16)
            cos, sin, decay = (s5_turn[:, n] for n in range(3))
            x0, x1, v0, v1 = s5_x[0], s5_x[1], s5_v[0], s5_v[1]
            flat = lambda x: x.rearrange("p q c -> p (q c)")
            step(tt(v0, x0, cos, ALU.mult))
            step(tt(s5_tmp, x1, sin, ALU.mult))
            step(tt(v0, v0, s5_tmp, ALU.add))
            step(tt(v1, x1, cos, ALU.mult))
            step(tt(s5_tmp, x0, sin, ALU.mult))
            step(tt(v1, v1, s5_tmp, ALU.subtract))
            step(scan(flat(x0), flat(decay), flat(v0), 0.0, ALU.mult, ALU.add))
            step(scan(flat(x1), flat(decay), flat(v1), 0.0, ALU.mult, ALU.add))
            step(tt(v0, x0, cos, ALU.mult))
            step(tt(s5_tmp, x1, sin, ALU.mult))
            step(tt(v0, v0, s5_tmp, ALU.subtract))
            step(tt(v1, x0, sin, ALU.mult))
            step(tt(s5_tmp, x1, cos, ALU.mult))
            tt(v1, v1, s5_tmp, ALU.add).then_inc(S("s5_states"), 1)
            for c in range(NCH - 1):
                for pair in range(2):
                    key = ("gd", pair, c % 2)
                    src = full(dve, key)[:, (c // 2) * GDV:(c // 2 + 1) * GDV]
                    if c == 0:
                        ins = cp(g_st[:, pair, 0, :], src)
                    else:
                        ins = stt(g_st[:, pair, c, :], g_st[:, pair, c - 1, :],
                                  dec[:, NCH * pair + c:NCH * pair + c + 1], src, ALU.mult, ALU.add)
                    if c >= NCH - 3:
                        out_of(key, ins)
                        copied(dve, key)
                    else:
                        step(ins)
            for i in range(NT):
                copied(dve, ("og", i))
            og_h = og.rearrange("p i (h d) -> p (i h) d", h=GH)
            step(tt(og_h, og_h, over(gla_g[:], 1, NT * GH), ALU.mult))
            for i in range(NT):
                r = st[:, ST_GR + 4 * i:ST_GR + 4 * i + 4]
                dve.wait_ge(S("gla_root"), i + 1)
                step(nc.vector.reciprocal(r, r))
                if i >= 2:
                    full(dve, ("gt", i - 2))
                for par_ in range(2):
                    bank = ps[:, plan[("go", i, par_)][0], :]
                    for hh in range(2):
                        h = 2 * hh + par_
                        ins = stt(g_row[:, i % 2, h * GDV:(h + 1) * GDV], bank[:, hh * GDV:(hh + 1) * GDV],
                                  r[:, 2 * par_ + hh:2 * par_ + hh + 1], og[:, i, h * GDV:(h + 1) * GDV],
                                  ALU.mult, ALU.mult)
                    out_of(("go", i, par_), ins)
            for i in range(NT):
                low_parts("gt", i)
            for m in range(4):
                copied(dve, ("glu", m))
                out_m = sig[:, m % 2, :]
                in_time = out_m.rearrange("p (j c) -> p j c", j=SL)
                step(tt(out_m, yT[:, m, :], out_m, ALU.mult))
                high, low = (x[:, 4 + m, :].rearrange("p (c j) -> p j c", j=SL) for x in (actT, actL))
                step(cp(r32(high), in_time))
                tt(r32(low), in_time, high, ALU.subtract).then_inc(S("s5_out"), 1)
            post_and_norm(3, lambda i, n: ("wo", 2, i, n), post_g[:, 0, :], "x_mix2", st[:, ST_MOD + KD:ST_MOD + 2 * KD],
                          mod[:, 3 * KD:4 * KD])

            for i in range(NT):
                out_of(("lg", i), tt(lg[:, i, :], full(dve, ("lg", i))[:, 0:NE], router_b[:], ALU.add))
                copied(dve, ("lg", i))
                step(nc.vector.max(out=top_v[:, i, :], in_=lg[:, i, :]))
                step(nc.vector.max_index(out=top_i[:, i, :], in_max=top_v[:, i, :], in_values=lg[:, i, :]))
            tt(gate[:], top_v[:, :, 0:TOPK], over(top_v[:, :, 0], 2, TOPK), ALU.subtract).then_inc(S("top_diff"), 1)
            dve.wait_ge(S("slots_cleared"), 32)
            step(cp(top_f, top_i))
            e_f = step_f[:, 0:NE]
            for i in range(NT):
                step(tt(pick[:, i], over(e_f, 1, TOPK), over(top_f[:, i, 0:TOPK], 2, NE), ALU.is_equal))
                nc.vector.tensor_reduce(mask[:, i, :], pick[:, i].rearrange("p k e -> p e k"), AX.X, ALU.add)\
                    .then_inc(S("mask_ready"), 1)
            bank = full(dve, "rk")
            step(cp(rank.rearrange("p i e -> p (i e)"), bank[:, 0:NT * NE]))
            out_of("rk", cp(cnt_e, bank[:, NT * NE:(NT + 1) * NE]))
            copied(dve, "rk")
            step(ts(ov, cnt_e, float(P), None, ALU.is_gt))
            step(stt(ov, cnt_e, float(2 * P), ov, ALU.is_gt, ALU.add))
            step(stt(ov, cnt_e, float(3 * P), ov, ALU.is_gt, ALU.add))
            step(scan(ov_in, ones[:, 0:NE], ov, 0.0, ALU.mult, ALU.add))
            step(tt(base_hi, ov_in, ov, ALU.subtract))
            step(ts(base_hi, base_hi, float(NE - 1), float(P), ALU.add, ALU.mult))
            step(stt(base_d, e_f, float(P), base_hi, ALU.mult, ALU.subtract))
            step(ts(pos, rank, float(P), None, ALU.is_lt))
            step(tt(pos, pos, over(base_d, 1, NT), ALU.mult))
            step(tt(pos, pos, over(base_hi, 1, NT), ALU.add))
            step(tt(pos, pos, rank, ALU.add))
            for i in range(NT):
                step(tt(prod[:, i], pick[:, i], over(pos[:, i, :], 1, TOPK), ALU.mult))
            step(nc.vector.tensor_reduce(posf, prod.rearrange("p i k e -> p (i k) e"), AX.X, ALU.add))
            cp(posi[:], posf).then_inc(S("slots_known"), 1)
            step(tt(le_f[0:1], over(ov_in[0:1], 1, MAX_EXTRA + 1), over(step_f[0:1, 0:MAX_EXTRA + 1], 2, NE), ALU.is_le))
            step(nc.vector.tensor_reduce(blk_f[0:1, 0:MAX_EXTRA + 1], le_f[0:1], AX.X, ALU.add))
            step(ts(blk_f[0:1, 0:MAX_EXTRA + 1], blk_f[0:1, 0:MAX_EXTRA + 1], float(NE - 1), None, ALU.min))
            step(cp(blk_e[0:1, 0:NE], e_f[0:1]))
            step(cp(blk_e[0:1, NE:NE + MAX_EXTRA + 1], blk_f[0:1, 0:MAX_EXTRA + 1]))
            dve.wait_ge(S("top_exp"), 1)
            step(nc.vector.tensor_reduce(gsum, gate[:], AX.X, ALU.add))
            step(nc.vector.reciprocal(gsum, gsum))
            step(tt(gate[:], gate[:], over(gsum, 2, TOPK), ALU.mult))
            cp(blk_e[0:1, 63:64], ov_in[0:1, NE - 1:NE]).then_inc(S("blocks_known"), 1)
            dve.wait_ge(S("blocks_known"), 1)

            n_blocks = NE + dve.value_load(blk_e[0:1, 63:64], min_val=0, max_val=MAX_EXTRA)

            def low_parts_of(b, xs_):
                for x in xs_:
                    o = place(b, x)
                    dve.wait_ge(S("high"), 12 * b + o + 1)
                    high, low = halves(o % SPLIT)
                    tt(r32(low[:, 0:MOST]), raw(o % RAW)[:, 0:MOST], high[:, 0:MOST], ALU.subtract)\
                        .then_inc(S("low_dve"), 1)

            def input_parts(b):
                dve.wait_ge(S("xgT_ready"), b + 1)
                cp(r32(xT_h[:]), xT).then_inc(S("xT_high"), 1)
                dve.wait_ge(S("xT_high"), b + 1)
                tt(r32(xT_l[:]), xT, xT_h[:], ALU.subtract).then_inc(S("xT_low"), 1)

            def hidden_low(b):
                dve.wait_ge(S("hT_high"), b + 1)
                for half in range(2):
                    ins = tt(r32(hT_l[:, 4 * half:4 * half + 4, :]), ps[:, 6 + half, :].rearrange("p (k s) -> p k s", k=4),
                             hT_h[:, 4 * half:4 * half + 4, :], ALU.subtract)
                ins.then_inc(S("hT_low"), 1)

            def swiglu(b, hf):
                first = isinstance(b, int) and b == 0
                half = slice(hf * HALF, (hf + 1) * HALF)
                dve.wait_ge(S("bgu_ready"), 2 * b + 2)
                dve.wait_ge(S("gu_full"), 4 * b + 2 * hf + 1)
                if not first or hf:
                    dve.wait_ge(S("sw_done"), 2 * b + hf)
                tt(sw_t, ps[:, 2 * hf, :], bgu[:, half], ALU.add).then_inc(S("gu_copied"), 1)
                dve.wait_ge(S("gu_copied"), 4 * b + 2 * hf + 1)
                ts(sw_g, sw_t, SWI_LIMIT, None, ALU.min).then_inc(S("sw_gate"), 1)
                dve.wait_ge(S("gu_full"), 4 * b + 2 * hf + 2)
                tt(sw_u, ps[:, 2 * hf + 1, :], bgu[:, D + hf * HALF:D + (hf + 1) * HALF], ALU.add)\
                    .then_inc(S("gu_copied"), 1)
                dve.wait_ge(S("gu_copied"), 4 * b + 2 * hf + 2)
                ts(sw_u, sw_u, SWI_LIMIT, -SWI_LIMIT, ALU.min, ALU.max).then_inc(S("sw_clip"), 1)
                dve.wait_ge(S("sw_clip"), 2 * b + hf + 1)
                dve.wait_ge(S("sw_gate"), 2 * b + hf + 1)
                stt(sw_p, sw_u, 1.0, sw_g, ALU.add, ALU.mult).then_inc(S("sw_up"), 1)
                dve.wait_ge(S("sw_up"), 2 * b + hf + 1)
                dve.wait_ge(S("sw_sig"), 2 * b + hf + 1)
                if not first:
                    dve.wait_ge(S("hT_full"), b)
                tt(h_row[:, half], sw_p, sw_s, ALU.mult).then_inc(S("sw_done"), 1)

            def outputs(b):
                dve.wait_ge(S("bdn_ready"), b + 1)
                dve.wait_ge(S("y_stored"), 16 * b + 16)
                for n in range(2):
                    half = slice(n * HALF, (n + 1) * HALF)
                    dve.wait_ge(S("dn_full"), 2 * b + n + 1)
                    tt(y_row[:, half], ps[:, 4 + n, :], bdn[:, half], ALU.add).then_inc(S("y_done"), 1)

            def loop_turn(b):
                low_parts_of(b, range(4))
                if isinstance(b, int) and b == 0:
                    input_parts(0)
                else:
                    hidden_low(b - 1)
                    if not isinstance(b, int):
                        outputs(b - 2)
                low_parts_of(b, range(4, 8))
                swiglu(b, 0)
                if not (isinstance(b, int) and b == 0):
                    low_parts_of(b, range(8, 12))
                swiglu(b, 1)
                input_parts(b + 1)

            dve.sem_inc(S("y_done"), 1)
            loop_turn(0)
            loop_turn(1)
            with dve.Fori(2, n_blocks) as b:
                loop_turn(b)
            low_parts_of(n_blocks, range(4))
            hidden_low(n_blocks - 1)
            outputs(n_blocks - 2)
            outputs(n_blocks - 1)
            for i in range(NT + 1):
                if i < NT:
                    dve.wait_ge(S(f"y_in{i}"), 16 * TOPK)
                    step(ts(ff[:, i, :], y_pick[TOPK * i], gate[:, i, 0:1], None, ALU.mult))
                    for k in range(1, TOPK):
                        ins = stt(ff[:, i, :], y_pick[TOPK * i + k], gate[:, i, k:k + 1], ff[:, i, :], ALU.mult, ALU.add)
                        if k < TOPK - 1:
                            step(ins)
                    ins.then_inc(S("ff_ready"), 1)
                if i:
                    r, row = st[:, ST_SS + i - 1:ST_SS + i], ff[:, i - 1, :]
                    dve.wait_ge(S("ff_root"), i)
                    step(nc.vector.reciprocal(r, r))
                    step(stt(row, row, r, post_g[:, 1, :], ALU.mult, ALU.mult))
                    tt(x_res[:, i - 1, :], x_res[:, i - 1, :], row, ALU.add).then_inc(S("x_final"), 1)
            dve.wait_ge(S("x_final"), NT)

        @block.tensor
        def _(pe):
            mm = nc.tensor.matmul

            def take(key):
                b, turn_no = plan[key]
                if turn_no:
                    pe.wait_ge(bank_copied[b], turn_no)
                return ps[:, b, :]

            def done(key, ins):
                ins.then_inc(bank_full[plan[key][0]], 1)

            def parts(name, c, h):
                n = piece_no[name, c, h]
                pe.wait_ge(S("split_ready"), n + 1)
                return (r32(part(n, low)).rearrange("p (g n) -> p g n", g=NG) for low in range(2))

            def transposes(s, i):
                pe.wait_ge(S("xn_ready"), NT * (s - 1) + i + 1)
                row = xs[:, i, :] if s == 4 else xn[:, i % 2, :]
                for h in range(2):
                    key = ("norm", s, i, h)
                    bank = take(key)
                    for k in range(4):
                        ins = nc.tensor.transpose(bank[:, k * P:(k + 1) * P], row[:, (4 * h + k) * P:(4 * h + k + 1) * P],
                                                  ident[:])
                    done(key, ins)

            def normed(s):
                pe.wait_ge(S("norm_low"), NT * (s - 1) + NT)

            def three(o, stat, mov, start, stop):
                mm(o, stat[0], mov[0], start=start, stop=False)
                mm(o, stat[0], mov[1], start=False, stop=False)
                return mm(o, stat[1], mov[0], start=False, stop=stop)

            def by_column(name, c, keys, tokens=False):
                banks = {}
                for h in range(2):
                    w = tuple(parts(name, c, h))
                    for g in range(NG):
                        k = NG * h + g
                        for m, key in enumerate(keys):
                            if k == 0:
                                banks[m] = take(key)
                            tile = slice(m * P, (m + 1) * P)
                            if tokens:
                                stat, mov = [r32(x[:, k, tile]) for x in (actT, actL)], [x[:, g, :] for x in w]
                            else:
                                stat, mov = [x[:, g, tile] for x in w], [r32(x[:, k, :]) for x in (actT, actL)]
                            ins = three(banks[m], stat, mov, k == 0, k == KD - 1)
                            if k == KD - 1:
                                done(key, ins)
                    if h == 0:
                        ins.then_inc(S("split_used"), 1)

            def first_column(name, c, keys, s):
                w = [tuple(parts(name, c, h)) for h in range(2)]
                for th in range(2):
                    pe.wait_ge(S("norm_low"), NT * (s - 1) + 2 * th + 2)
                    time = slice(th * T // 2, (th + 1) * T // 2)
                    for k in range(KD):
                        for m, key in enumerate(keys):
                            bank = take(key) if th + k == 0 else ps[:, plan[key][0], :]
                            ins = three(bank[:, time], [x[:, k % NG, m * P:(m + 1) * P] for x in w[k // NG]],
                                        [r32(x[:, k, time]) for x in (actT, actL)], k == 0, k == KD - 1)
                            if th and k == KD - 1:
                                done(key, ins)
                        if th and k == NG - 1:
                            ins.then_inc(S("split_used"), 1)
                        if not th and k == 1:
                            transposes(s, NT - 1)

            def by_row(name, order, key, left, s, first_ready, ready):
                banks = {}

                def product(i, n, k, w, g):
                    if k == 4 * order[0]:
                        banks[i, n] = take(key(i, n))
                    tile = slice(i * P, (i + 1) * P)
                    return three(banks[i, n], [r32(x[:, tile]) for x in left(k)], [x[:, g, :] for x in w],
                                 k == 4 * order[0], k == 4 * order[-1] + 3)

                for c in order:
                    for h in range(2):
                        w = tuple(parts(name, c, h))
                        final = (c, h) == (order[-1], 1)
                        for i in range(NT):
                            if c == order[0] and h == 0:
                                first_ready(i)
                            if c == order[-1] and h == 0:
                                ready(i)
                            for n in range(2):
                                for kk in range(2):
                                    ins = product(i, n, 4 * c + 2 * h + kk, w, 2 * kk + n)
                                if final:
                                    done(key(i, n), ins)
                            if final and i >= 2:
                                transposes(s + 1, i - 2)
                        if not final:
                            ins.then_inc(S("split_used"), 1)
                transposes(s + 1, NT - 2)

            pe.wait_ge(S("constants"), 1)
            pe.wait_ge(S("silu_c"), 1)
            for c in range(NADA):
                row = slice(32 * (c % 4), 32 * (c % 4) + 1)
                bank = take(("ada", c // 4)) if c % 4 == 0 else bank
                for h in range(2):
                    n = 2 * c + h
                    pe.wait_ge(S(f"ada_in{n % 4}"), 16 * (n // 4 + 1))
                    w = piece(n % 4).rearrange("p (k n) -> p k n", k=NG)
                    for g in range(NG):
                        k = NG * h + g
                        ins = mm(bank[row, :], silu_c[:, k:k + 1], w[:, g, :], start=(k == 0), stop=(k == KD - 1))
                    if n % 8 == 7:
                        done(("ada", c // 4), ins)
                    else:
                        ins.then_inc(S("ada_used"), 1)
            for i in range(NT):
                transposes(1, i)
            for x in range(NADA // 4):
                copied(pe, ("ada", x))
            for x in range(NADA // 4):
                bank = take(("mod", x))
                for m in range(4):
                    ins = nc.tensor.transpose(bank[:, m * P:(m + 1) * P], mod_row[:, x, m * P:(m + 1) * P], ident[:])
                done(("mod", x), ins)
            pe.wait_ge(S("bx_ready"), 1)
            for n in range(8):
                bank = take(("s5b", n))
                for x in range(4):
                    q, ri = divmod(4 * n + x, 2)
                    src = (bx_r, bx_i)[ri][:, q].rearrange("p j h -> p (j h)")
                    ins = nc.tensor.transpose(bank[:, x * P:(x + 1) * P], src, ident[:])
                done(("s5b", n), ins)
            for par_ in range(2):
                half = slice(SS * par_, SS * (par_ + 1))
                for q4 in range(4):
                    bank = take(("s5k", par_, q4))
                    for x in range(4):
                        q = 4 * q4 + x
                        o = bank[0:SC, x * P:(x + 1) * P]
                        mm(o, bb_r[half, q, :], ca_r[half, q, 0:SL, :].rearrange("p t h -> p (t h)"),
                           start=True, stop=False)
                        ins = mm(o, bb_i[half, q, :], ca_n[half, q, 0:SL, :].rearrange("p t h -> p (t h)"),
                                 start=False, stop=True)
                    done(("s5k", par_, q4), ins)
            normed(1)
            for name, c in (("xr", 3), ("gr", 4), ("q", 0), ("k", 1)):
                by_column("w_in", c, [(name, m) for m in range(4)])
            by_column("w_in", 2, [("v", i) for i in range(NT)], tokens=True)
            for m in range(NL):
                pe.wait_ge(S("conv_ready"), m + 1)
                for g in range(2):
                    done(("gate", g, m), mm(take(("gate", g, m)), w_gate[:, g, m, :], xc[:, m, :], start=True, stop=True))
            for m in range(4):
                copied(pe, ("q", m))
                copied(pe, ("k", m))
                copied(pe, ("v", m))

            def scores(n):
                i, h = divmod(n, HEADS)
                half, keys_n = slice(DH * (h % 2), DH * (h % 2 + 1)), (i + 1) * P
                done(("s", i, h), mm(take(("s", i, h))[:, 0:keys_n], qT[half, h // 2, i * P:(i + 1) * P],
                                     kT[half, h // 2, 0:keys_n], start=True, stop=True))

            def turn_probs(n):
                i, h = divmod(n, HEADS)
                pe.wait_ge(S("att_exp"), n + 1)
                bank = take(("pt", i, h))
                for j in range(i + 1):
                    ins = nc.tensor.transpose(bank[:, j * P:(j + 1) * P], att_s[:, h % 4, j * P:(j + 1) * P], ident[:])
                done(("pt", i, h), ins)

            def values(n):
                i, h = divmod(n, HEADS)
                o = take(("o", i)) if h == 0 else ps[:, 7, :]
                copied(pe, ("pt", i, h))
                for j in range(i + 1):
                    ins = mm(o[:, h * DH:(h + 1) * DH], att_pt[:, h % 2, j, :], v[:, j, h * DH:(h + 1) * DH],
                             start=(j == 0), stop=(j == i))
                if h == HEADS - 1:
                    done(("o", i), ins)

            def turn_rows(i):
                copied(pe, ("o", i))
                bank = take(("at", i))
                for m in range(4):
                    ins = nc.tensor.transpose(bank[:, m * P:(m + 1) * P], att_row[:, m * P:(m + 1) * P], ident[:])
                done(("at", i), ins)

            for n in range(3):
                scores(n)
            for n in range(NT * HEADS):
                if n + 3 < NT * HEADS:
                    scores(n + 3)
                turn_probs(n)
                if n:
                    values(n - 1)
                if n >= HEADS and n % HEADS == 2:
                    turn_rows(n // HEADS - 1)
            values(NT * HEADS - 1)
            def attended(i):
                if i == NT - 2:
                    turn_rows(NT - 1)
                copied(pe, ("at", i))

            act_k = lambda k: (actT[:, k, :], actL[:, k, :])
            by_row("w_out", (0, 1), lambda i, n: ("wo", 1, i, n), act_k, 1, attended,
                   lambda i: pe.wait_ge(S("rec_ready"), NL))

            first_column("ff_in", 0, [("f1", m) for m in range(4)], 2)
            for c in range(1, 8):
                by_column("ff_in", c, [("f1", 4 * c + m) for m in range(4)])

            def hid_k(k):
                pe.wait_ge(S("hid_split"), k + 1)
                return hid_h[:, k % 4, :], hid_l[:, k % 4, :]

            by_row("ff_out", range(8), lambda i, n: ("f2", i, n), hid_k, 2, lambda i: None,
                   lambda i: None)
            first_column("w_in_2", 0, [("gq", m) for m in range(4)], 3)
            by_column("w_in_2", 3, [("u", m) for m in range(4)])
            for s in range(2):
                pe.wait_ge(S("diag_ready"), s + 1)
                for n in range(2):
                    bank = take(("pg", s, n))
                    for k in range(4):
                        ins = mm(bank[:, k * P:(k + 1) * P], ones[:], diag[s][:, 4 * n + k, :], start=True, stop=True)
                    done(("pg", s, n), ins)
            bank = take("a16")
            for n, x in enumerate((actT, actL)):
                for k in range(KD):
                    ins = mm(bank[0:16, :], w_a16[:, k, :], x[:, k, :], start=(n + k == 0), stop=(n == 1 and k == KD - 1))
            done("a16", ins)
            copied(pe, "a16")
            for m in range(2):
                done(("za", m), mm(take(("za", m)), w_alpha[:, m * P:(m + 1) * P], a16[0:16, :], start=True, stop=True))
            by_column("w_in_2", 1, [("gv", i) for i in range(NT)], tokens=True)
            by_column("w_in_2", 2, [("og", i) for i in range(NT)], tokens=True)
            w = ring[:].rearrange("p (q r n) -> p q r n", q=NQ, r=2)
            pe.wait_ge(S("u_in"), 16 * SL)
            for q8 in range(2):
                pe.wait_ge(S(f"inject_in{q8}"), 16)
                for ri in range(2):
                    bank = take(("D", ri, q8))
                    for x in range(8):
                        for par_ in range(2):
                            q = 8 * q8 + x
                            half = slice(SS * par_, SS * (par_ + 1))
                            ins = mm(bank[half, x * SNC:(x + 1) * SNC], w[:, q, ri, half], s5_u[:, 2 * q + par_, :],
                                     start=True, stop=True)
                    done(("D", ri, q8), ins)
            pe.wait_ge(S("gla_keys"), 1)
            for i in range(NT):
                bank = take(("ke", i))
                for m in range(2):
                    ins = nc.tensor.transpose(bank[:, m * P:(m + 1) * P], g_end[:, m, i * P:(i + 1) * P], ident[:])
                done(("ke", i), ins)
            for h in range(GH):
                half = slice(GDK * (h % 2), GDK * (h % 2 + 1))
                bank = take(("gs", h))
                for i in range(NT):
                    tile = slice(i * P, (i + 1) * P)
                    ins = mm(bank[:, tile], gk[half, h // 2, tile], gq[half, h // 2, tile], start=True, stop=True)
                done(("gs", h), ins)
            for i in range(NT):
                copied(pe, ("ke", i))
                copied(pe, ("gv", i))
            for pair in range(2):
                for cp_ in range(2):
                    bank = take(("gd", pair, cp_))
                    rows = slice(CH * cp_, CH * (cp_ + 1))
                    for c in range(cp_, NCH - 1, 2):
                        for hh in range(2):
                            h = 2 * pair + hh
                            ins = mm(bank[GDK * hh:GDK * (hh + 1), (c // 2) * GDV:(c // 2 + 1) * GDV],
                                     g_endr[rows, c // 2, h * GDK:(h + 1) * GDK], gv[rows, c // 2, h * GDV:(h + 1) * GDV],
                                     start=True, stop=True)
                    done(("gd", pair, cp_), ins)
            wt = ring[:, 0:PIECE].rearrange("p (r q n) -> p r q n", r=2, n=P)
            wr = ring[:, PIECE:].rearrange("p (q r n) -> p q r n", r=2, n=P)
            pe.wait_ge(S("s5_states"), 1)
            for q8 in range(2):
                pe.wait_ge(S("s5_in"), 16 * (q8 + 1))
                for par_ in range(2):
                    half = slice(SS * par_, SS * (par_ + 1))
                    bank = take(("Y", par_, q8))
                    for x in range(8):
                        q = 8 * q8 + x
                        mm(bank[:, x * SNC:(x + 1) * SNC], wt[:, par_, x, :], s5_u[:, 2 * q + par_, :],
                           start=True, stop=False)
                        for ri in range(2):
                            ins = mm(bank[:, x * SNC + 1:(x + 1) * SNC], wr[half, x, ri, :],
                                     s5_v[ri][half, q, 0:SNC - 1], start=False, stop=(ri == 1))
                    done(("Y", par_, q8), ins)
            for h in range(GH):
                copied(pe, ("gs", h))
            for pair in range(2):
                for cp_ in range(2):
                    copied(pe, ("gd", pair, cp_))
            for i in range(NT):
                for par_ in range(2):
                    bank = take(("go", i, par_))
                    half = slice(GDK * par_, GDK * (par_ + 1))
                    for hh in range(2):
                        h = 2 * hh + par_
                        o = bank[:, hh * GDV:(hh + 1) * GDV]
                        mm(o, g_sT[:, h, i * P:(i + 1) * P], gv[:, i, h * GDV:(h + 1) * GDV], start=True, stop=True)
                        for x in range(2):
                            c = 2 * i + x
                            if c:
                                ins = mm(o[CH * x:CH * (x + 1), :], gq[half, hh, c * CH:(c + 1) * CH],
                                         g_st[half, hh, c - 1, :], start=False, stop=True, skip_group_check=True)
                    done(("go", i, par_), ins)
            for i in range(NT):
                copied(pe, ("go", i, 0))
                copied(pe, ("go", i, 1))
                bank = take(("gt", i))
                for m in range(4):
                    ins = nc.tensor.transpose(bank[:, m * P:(m + 1) * P], g_row[:, i % 2, m * P:(m + 1) * P], ident[:])
                done(("gt", i), ins)
            pe.wait_ge(S("glu_in"), 16)
            w = piece(1).rearrange("p (k n) -> p k n", k=NG)
            pe.wait_ge(S("y5_gelu"), 4)
            for m in range(4):
                bank = take(("glu", m))
                for k in range(4):
                    ins = mm(bank, w[:, k, m * P:(m + 1) * P], yT[:, k, :], start=(k == 0), stop=(k == 3))
                done(("glu", m), ins)
            by_row("w_out_2", (0, 1), lambda i, n: ("wo", 2, i, n), act_k, 3, lambda i: copied(pe, ("gt", i)),
                   lambda i: pe.wait_ge(S("s5_out"), 4))
            for i in range(NT):
                if i == 1:
                    transposes(4, NT - 1)
                pe.wait_ge(S("norm_low"), 3 * NT + i + 1)
                bank = take(("lg", i))
                for n, x in enumerate((actT, actL)):
                    for k in range(KD):
                        ins = mm(bank[:, 0:NE], x[:, k, i * P:(i + 1) * P], router_w[:, k, :],
                                 start=(n + k == 0), stop=(n == 1 and k == KD - 1))
                done(("lg", i), ins)
            pe.wait_ge(S("mask_ready"), NT)
            bank = take("rk")
            for i in range(NT + 1):
                for j in range(min(i + 1, NT)):
                    ins = mm(bank[:, i * NE:(i + 1) * NE], before[:] if j == i else ones[:], mask[:, j, :],
                             start=(j == 0), stop=(j == min(i, NT - 1)))
            done("rk", ins)

            copied(pe, "rk")
            pe.wait_ge(S("blocks_known"), 1)
            n_blocks = NE + pe.value_load(blk_e[0:1, 63:64], min_val=0, max_val=MAX_EXTRA)

            def input_in(b):
                pe.wait_ge(S("xg_in"), 16 * b + 16)
                if not (isinstance(b, int) and b < 2):
                    pe.wait_ge(S("hT_low"), b - 1)
                for k in range(KD):
                    ins = nc.tensor.transpose(ps[:, 6 + k // 4, (k % 4) * P:(k % 4 + 1) * P], xg[:, k * P:(k + 1) * P],
                                              ident[:])
                ins.then_inc(S("xgT_full"), 1)

            def piece_product(b, x, o, stat, h):
                pe.wait_ge(S("low_dve"), 12 * b + place(b, x) + 1)
                w = [r32(y).rearrange("p (g n) -> p g n", g=NG) for y in halves(place(b, x) % SPLIT)]
                for g in range(NG):
                    k = NG * h + g
                    if g == NG - 1:
                        pe.wait_ge(S("low_pool"), 12 * b + place(b, x) + 1)
                    ins = three(o, [r32(y[:, k, :]) for y in stat], [y[:, g, :] for y in w], k == 0, k == KD - 1)
                return ins

            def gate_up(b):
                pe.wait_ge(S("xT_low"), b + 1)
                for j in range(4):
                    if not (isinstance(b, int) and b == 0):
                        pe.wait_ge(S("gu_copied"), 4 * b + j - 3)
                    piece_product(b, 2 * j, ps[:, j, :], (xT_h, xT_l), 0).then_inc(S("part_used"), 1)
                    piece_product(b, 2 * j + 1, ps[:, j, :], (xT_h, xT_l), 1).then_inc(S("gu_full"), 1)

            def down(b, turn_no, first_piece):
                pe.wait_ge(S("hT_low"), b + 1)
                pe.wait_ge(S("y_done"), 2 * b + 1)
                for n in range(2):
                    x = first_piece + 2 * n
                    piece_product(turn_no, x, ps[:, 4 + n, :], (hT_h, hT_l), 0).then_inc(S("part_used"), 1)
                    piece_product(turn_no, x + 1, ps[:, 4 + n, :], (hT_h, hT_l), 1).then_inc(S("dn_full"), 1)

            def hidden_in(b):
                pe.wait_ge(S("sw_done"), 2 * b + 2)
                pe.wait_ge(S("xgT_ready"), b + 2)
                for k in range(KD):
                    ins = nc.tensor.transpose(ps[:, 6 + k // 4, (k % 4) * P:(k % 4 + 1) * P], h_row[:, k * P:(k + 1) * P],
                                              ident[:])
                ins.then_inc(S("hT_full"), 1)

            def loop_turn(b):
                gate_up(b)
                input_in(b + 1)
                if not (isinstance(b, int) and b == 0):
                    down(b - 1, b, 8)
                hidden_in(b)

            input_in(0)
            loop_turn(0)
            loop_turn(1)
            with pe.Fori(2, n_blocks) as b:
                loop_turn(b)
            down(n_blocks - 1, n_blocks, 0)


_LARGE = ["x", "mix_norm_post", "mlp_norm_post", "w_in", "w_out", "w_ff_in", "w_ff_out", "ada_w_2", "w_in_2",
          "w_alpha_2", "gla_norm_g_2", "s5_glu_w_2", "w_out_2", "router_w_2", "router_b_2", "exp_w_gu_2",
          "exp_b_gu_2", "exp_w_down_2", "exp_b_down_2"]


def laid_out(inputs):
    arrays = {name: np.ascontiguousarray(inputs[name]) for name in _LARGE}
    arrays["cols"] = np.ascontiguousarray(
        np.concatenate([np.asarray(inputs[name]).reshape(n, P) for name, n in VECS]).T)

    def states(x):
        x = np.asarray(x).reshape(NQ, 2 * SS, -1)
        return np.ascontiguousarray(x.transpose(1, 0, 2))

    step = np.broadcast_to(np.asarray(inputs["s5_log_dt_2"]).reshape(SG, 1), (SG, SS))
    arrays["s5_par"] = np.ascontiguousarray(np.concatenate(
        [states(x) for x in (step, inputs["s5_lambda_re_2"], inputs["s5_lambda_im_2"])], axis=2).transpose(0, 2, 1))
    for name in ("s5_b_re", "s5_b_im"):
        arrays[name] = states(inputs[name + "_2"])
    for name in ("s5_c_re", "s5_c_im"):
        arrays[name] = states(np.asarray(inputs[name + "_2"])[0].transpose(0, 2, 1))
    arrays["s5_d"] = np.ascontiguousarray(np.asarray(inputs["s5_d_2"]).reshape(2, NQ // 2, 2, SC)
                                          .transpose(3, 0, 2, 1).reshape(SC, SG))
    for name in ("w_rgate", "w_igate"):
        w = np.asarray(inputs[name])[0]
        n = w.shape[1]
        two = np.zeros((P, NL, P), w.dtype)
        for g in range(2):
            two[g * n:(g + 1) * n, :, g * n:(g + 1) * n] = w[g::2].transpose(1, 0, 2)
        arrays[name] = two
    return arrays


def kernel(**inputs):
    import concourse.bacc as bacc
    from concourse.bass_utils import run_bass_kernel_spmd

    nc = bacc.Bacc("TRN2", target_bir_lowering=False, num_devices=1)
    arrays = {f"in_{name}": x for name, x in laid_out(inputs).items()}
    handles = {name[3:]: nc.dram_tensor(name, x.shape, mybir.dt.from_np(x.dtype), kind="ExternalInput").ap()
               for name, x in arrays.items()}
    out = nc.dram_tensor("out", (1, T, D), F32, kind="ExternalOutput").ap()
    program(nc, handles, out)
    result = run_bass_kernel_spmd(nc, [arrays], core_ids=[0])
    return result.results[0]["out"]
```
